# Optimizing a Trainium2 kernel written in Bass

```python
import jax, jax.numpy as jnp
from jax import lax
import numpy as np

D_MODEL = 1024
BATCH = 1
SEQ = 128
DEPTH = 4
DEC_BATCH = 1
DEC_SEQ = 256
PAST_LEN = 128

GRID_W = 64
N_MIXERS = 3
N_ATTN_LAYERS = (DEPTH + 2) // 3
N_POOL_LAYERS = (DEPTH + 1) // 3
N_RET_LAYERS = DEPTH // 3

HEAD_DIM = 128
N_HEADS = D_MODEL // HEAD_DIM
N_KV_HEADS = 2
Q_BLOCK = 128
ROPE_THETA = 10000.0

POOL_WINDOWS = (2, 4, 8, 16)
POOL_GROUP = D_MODEL // 4

RET_HEADS = 8
RET_DK = D_MODEL // RET_HEADS
RET_DV = 2 * RET_DK
RET_CHUNK = 128

N_GROUPS = 4
EXPERTS_PER_GROUP = 4
N_EXPERTS = N_GROUPS * EXPERTS_PER_GROUP
D_EXPERT = 256
TOP_K_IN_GROUP = 2

EPS = 1e-6

kernel_name = 'hybrid_diffusion_trunk_step'

def _rmsnorm(x, g):
    xf = x.astype(jnp.float32)
    y = xf * lax.rsqrt(jnp.mean(xf * xf, axis=-1, keepdims=True) + EPS)
    return (y * g.astype(jnp.float32)).astype(x.dtype)

def _adaln(cond, w, b):
    m = jax.nn.silu(cond) @ w + b
    return jnp.split(m, 6, axis=-1)

def _modulate(h, shift, scale):
    return h * (1 + scale) + shift

def _rotate(x, ang):
    f = ang.shape[-1]
    cos = jnp.cos(ang)[None, :, None, :].astype(x.dtype)
    sin = jnp.sin(ang)[None, :, None, :].astype(x.dtype)
    x1, x2 = x[..., :f], x[..., f:]
    return jnp.concatenate([x1 * cos - x2 * sin, x1 * sin + x2 * cos], axis=-1)

def _axial_rope(x):
    L = x.shape[1]
    rows = L // GRID_W
    t_row = jnp.broadcast_to(jnp.arange(rows)[:, None], (rows, GRID_W)).reshape(-1)
    t_col = jnp.broadcast_to(jnp.arange(GRID_W)[None, :], (rows, GRID_W)).reshape(-1)
    nf = HEAD_DIM // 4
    inv = ROPE_THETA ** (-jnp.arange(nf, dtype=jnp.float32) / nf)
    ang_r = t_row.astype(jnp.float32)[:, None] * inv[None, :]
    ang_c = t_col.astype(jnp.float32)[:, None] * inv[None, :]
    half = HEAD_DIM // 2
    return jnp.concatenate([_rotate(x[..., :half], ang_r), _rotate(x[..., half:], ang_c)], axis=-1)

def _attend(q, k, v):
    B, Lq, H, Dh = q.shape
    kv = k.shape[2]
    g = H // kv
    nb = Lq // Q_BLOCK
    qb = q.reshape(B, nb, Q_BLOCK, kv, g, Dh).transpose(1, 0, 2, 3, 4, 5)
    scale = Dh ** -0.5

    def one_block(qblk):
        s = jnp.einsum('bqkgd,bskd->bkgqs', qblk, k).astype(jnp.float32) * scale
        p = jax.nn.softmax(s, axis=-1).astype(v.dtype)
        return jnp.einsum('bkgqs,bskd->bqkgd', p, v)

    o = lax.map(one_block, qb)
    return o.transpose(1, 0, 2, 3, 4, 5).reshape(B, Lq, H * Dh)

def _attn_project(h, w_qkv, q_norm, k_norm):
    B, L, _ = h.shape
    p = h @ w_qkv
    nq = N_HEADS * HEAD_DIM
    nk = N_KV_HEADS * HEAD_DIM
    q = _rmsnorm(p[..., :nq].reshape(B, L, N_HEADS, HEAD_DIM), q_norm)
    k = _rmsnorm(p[..., nq:nq + nk].reshape(B, L, N_KV_HEADS, HEAD_DIM), k_norm)
    v = p[..., nq + nk:].reshape(B, L, N_KV_HEADS, HEAD_DIM)
    return q, k, v

def _attn_context(h, w_qkv, q_norm, k_norm, w_o):
    q, k, v = _attn_project(h, w_qkv, q_norm, k_norm)
    return _attend(q, k, v) @ w_o, k, v

def _attn_latent(h, k_ctx, v_ctx, w_qkv, q_norm, k_norm, w_o):
    q, k, v = _attn_project(h, w_qkv, q_norm, k_norm)
    keys = jnp.concatenate([k_ctx.astype(k.dtype), _axial_rope(k)], axis=1)
    vals = jnp.concatenate([v_ctx.astype(v.dtype), v], axis=1)
    return _attend(_axial_rope(q), keys, vals) @ w_o

def _pool_mixer(h, w, scale):
    B, L, D = h.shape
    hf = h.astype(jnp.float32)
    cs = jnp.concatenate([jnp.zeros((B, 1, D), jnp.float32), jnp.cumsum(hf, axis=1)], axis=1)
    t = jnp.arange(L)
    outs = []
    for gi, win in enumerate(POOL_WINDOWS):
        lo, hi = gi * POOL_GROUP, (gi + 1) * POOL_GROUP
        start = jnp.clip(t - win // 2, 0, L)
        end = jnp.clip(t + win - win // 2, 0, L)
        csg = cs[..., lo:hi]
        mean = (jnp.take(csg, end, axis=1) - jnp.take(csg, start, axis=1)) / (end - start).astype(jnp.float32)[None, :, None]
        outs.append((mean - hf[..., lo:hi]).astype(h.dtype) @ w[gi])
    return jnp.concatenate(outs, axis=-1) * scale

def _retention_chunkwise(q, k, v, log_g, S0):
    B, L, H, DK = q.shape
    DV = v.shape[-1]
    C = RET_CHUNK
    n = L // C
    idx = jnp.arange(C, dtype=jnp.float32)
    diff = idx[:, None] - idx[None, :]
    intra = jnp.where(diff[None] >= 0, jnp.exp(jnp.maximum(diff, 0.0)[None] * log_g[:, None, None]), 0.0)
    q_dec = jnp.exp((idx + 1.0)[:, None] * log_g[None, :])
    k_dec = jnp.exp((C - 1.0 - idx)[:, None] * log_g[None, :])
    c_dec = jnp.exp(C * log_g)

    def chunks(a):
        return a.astype(jnp.float32).reshape(B, n, C, H, a.shape[-1]).transpose(1, 0, 2, 3, 4)

    def step(S, xs):
        qc, kc, vc = xs
        s = jnp.einsum('bihd,bjhd->bhij', qc, kc) * intra
        o = jnp.einsum('bhij,bjhv->bihv', s, vc) + jnp.einsum('bihd,bhdv->bihv', qc, S) * q_dec[None, :, :, None]
        S = S * c_dec[None, :, None, None] + jnp.einsum('bjhd,bjhv->bhdv', kc * k_dec[None, :, :, None], vc)
        return S, o

    S, o = lax.scan(step, S0.astype(jnp.float32), (chunks(q), chunks(k), chunks(v)))
    return o.transpose(1, 0, 2, 3, 4).reshape(B, L, H, DV), S

def _retention_mixer(h, S0, w_in, decay_logit, norm_g, w_out):
    B, L, _ = h.shape
    p = h @ w_in
    nq = RET_HEADS * RET_DK
    nv = RET_HEADS * RET_DV
    q = p[..., :nq].reshape(B, L, RET_HEADS, RET_DK)
    k = p[..., nq:2 * nq].reshape(B, L, RET_HEADS, RET_DK) * (RET_DK ** -0.5)
    v = p[..., 2 * nq:2 * nq + nv].reshape(B, L, RET_HEADS, RET_DV)
    gate = p[..., 2 * nq + nv:]
    log_g = jax.nn.log_sigmoid(decay_logit.astype(jnp.float32))
    o_f, S_f = _retention_chunkwise(q, k, v, log_g[0], S0[:, 0])
    o_b, S_b = _retention_chunkwise(q[:, ::-1], k[:, ::-1], v[:, ::-1], log_g[1], S0[:, 1])
    o = o_f + o_b[:, ::-1]
    mu = jnp.mean(o, axis=-1, keepdims=True)
    var = jnp.mean(jnp.square(o - mu), axis=-1, keepdims=True)
    o = ((o - mu) * lax.rsqrt(var + EPS)).reshape(B, L, nv) * norm_g.astype(jnp.float32)
    y = (o.astype(h.dtype) * jax.nn.silu(gate)) @ w_out
    return y, jnp.stack([S_f, S_b], axis=1)

def _moe(h, w_rg, b_rg, w_re, b_re, w_gate, w_up, w_down):
    B, L, D = h.shape
    t = h.reshape(B * L, D)
    pg = jax.nn.softmax((t @ w_rg + b_rg).astype(jnp.float32), axis=-1)
    p_top, g_idx = lax.top_k(pg, 1)
    le = (t @ w_re + b_re).astype(jnp.float32).reshape(-1, N_GROUPS, EXPERTS_PER_GROUP)
    le_sel = jnp.einsum('tg,tge->te', jax.nn.one_hot(g_idx[:, 0], N_GROUPS, dtype=jnp.float32), le)
    pe = jax.nn.softmax(le_sel, axis=-1)
    pe_top, e_idx = lax.top_k(pe, TOP_K_IN_GROUP)
    w = p_top * pe_top / jnp.sum(pe_top, axis=-1, keepdims=True)
    expert_id = g_idx * EXPERTS_PER_GROUP + e_idx
    gates = jnp.sum(jax.nn.one_hot(expert_id, N_EXPERTS, dtype=jnp.float32) * w[..., None], axis=1)
    hg = jnp.einsum('td,edf->tef', t, w_gate)
    hu = jnp.einsum('td,edf->tef', t, w_up)
    act = jax.nn.silu(hg) * hu * gates[:, :, None].astype(t.dtype)
    y = jnp.einsum('tef,efd->td', act, w_down)
    return y.reshape(B, L, D)

def setup_inputs(seed: int = 0) -> dict:
    key = jax.random.key(seed)
    ks = list(jax.random.split(key, 32))
    D = D_MODEL

    def nrm(i, shape, s):
        return jax.random.normal(ks[i], shape, jnp.float32) * s

    expo = 5.0 + jnp.arange(RET_HEADS, dtype=jnp.float32)
    base_logit = jnp.log(2.0 ** expo - 1.0)
    return {
        'x_prompt': nrm(0, (BATCH, SEQ, D), 1.0),
        'x_sample': nrm(1, (DEC_BATCH, DEC_SEQ, D), 1.0),
        'cache_k': nrm(2, (DEC_BATCH, N_ATTN_LAYERS, PAST_LEN, N_KV_HEADS, HEAD_DIM), 1.0),
        'cache_v': nrm(3, (DEC_BATCH, N_ATTN_LAYERS, PAST_LEN, N_KV_HEADS, HEAD_DIM), 1.0),
        'state_ret': nrm(4, (DEC_BATCH, N_RET_LAYERS, 2, RET_HEADS, RET_DK, RET_DV), 0.5),
        'c': nrm(5, (DEC_BATCH, D), 1.0),
        'c_ctx': nrm(6, (D,), 1.0),
        'norm1': 1.0 + nrm(7, (DEPTH, D), 0.05),
        'norm2': 1.0 + nrm(8, (DEPTH, D), 0.05),
        'w_ada': nrm(9, (DEPTH, D, 6 * D), 0.5 * D ** -0.5),
        'b_ada': nrm(10, (DEPTH, 6 * D), 0.05),
        'attn_w_qkv': nrm(11, (N_ATTN_LAYERS, D, (N_HEADS + 2 * N_KV_HEADS) * HEAD_DIM), D ** -0.5),
        'attn_q_norm': 1.0 + nrm(12, (N_ATTN_LAYERS, HEAD_DIM), 0.05),
        'attn_k_norm': 1.0 + nrm(13, (N_ATTN_LAYERS, HEAD_DIM), 0.05),
        'attn_w_o': nrm(14, (N_ATTN_LAYERS, N_HEADS * HEAD_DIM, D), (N_HEADS * HEAD_DIM) ** -0.5),
        'pool_w': nrm(15, (N_POOL_LAYERS, 4, POOL_GROUP, POOL_GROUP), POOL_GROUP ** -0.5),
        'pool_scale': 1.0 + nrm(16, (N_POOL_LAYERS, D), 0.05),
        'ret_w_in': nrm(17, (N_RET_LAYERS, D, 2 * RET_HEADS * RET_DK + 2 * RET_HEADS * RET_DV), D ** -0.5),
        'ret_decay_logit': base_logit[None, None, :] + nrm(18, (N_RET_LAYERS, 2, RET_HEADS), 0.1),
        'ret_norm': 1.0 + nrm(19, (N_RET_LAYERS, RET_HEADS * RET_DV), 0.05),
        'ret_w_out': nrm(20, (N_RET_LAYERS, RET_HEADS * RET_DV, D), (RET_HEADS * RET_DV) ** -0.5),
        'moe_w_router_g': nrm(21, (DEPTH, D, N_GROUPS), D ** -0.5),
        'moe_b_router_g': nrm(22, (DEPTH, N_GROUPS), 0.01),
        'moe_w_router_e': nrm(23, (DEPTH, D, N_EXPERTS), D ** -0.5),
        'moe_b_router_e': nrm(24, (DEPTH, N_EXPERTS), 0.01),
        'moe_w_gate': nrm(25, (DEPTH, N_EXPERTS, D, D_EXPERT), D ** -0.5),
        'moe_w_up': nrm(26, (DEPTH, N_EXPERTS, D, D_EXPERT), D ** -0.5),
        'moe_w_down': nrm(27, (DEPTH, N_EXPERTS, D_EXPERT, D), D_EXPERT ** -0.5),
        'norm_f': 1.0 + nrm(28, (D,), 0.05),
    }

def reference(x_prompt, x_sample, cache_k, cache_v, state_ret, c, c_ctx,
              norm1, norm2, w_ada, b_ada,
              attn_w_qkv, attn_q_norm, attn_k_norm, attn_w_o,
              pool_w, pool_scale,
              ret_w_in, ret_decay_logit, ret_norm, ret_w_out,
              moe_w_router_g, moe_b_router_g, moe_w_router_e, moe_b_router_e,
              moe_w_gate, moe_w_up, moe_w_down, norm_f):
    xp, xs = x_prompt, x_sample
    new_k, new_v, new_s = [], [], []
    for i in range(DEPTH):
        kind, j = i % N_MIXERS, i // N_MIXERS
        mp = _adaln(c_ctx[None, None, :], w_ada[i], b_ada[i])
        ms = _adaln(c[:, None, :], w_ada[i], b_ada[i])
        hp = _modulate(_rmsnorm(xp, norm1[i]), mp[0], mp[1])
        hs = _modulate(_rmsnorm(xs, norm1[i]), ms[0], ms[1])
        if kind == 0:
            yp, kc, vc = _attn_context(hp, attn_w_qkv[j], attn_q_norm[j], attn_k_norm[j], attn_w_o[j])
            ys = _attn_latent(hs, cache_k[:, j], cache_v[:, j], attn_w_qkv[j], attn_q_norm[j], attn_k_norm[j], attn_w_o[j])
            new_k.append(kc)
            new_v.append(vc)
        elif kind == 1:
            yp = _pool_mixer(hp, pool_w[j], pool_scale[j])
            ys = _pool_mixer(hs, pool_w[j], pool_scale[j])
        else:
            s0 = jnp.zeros((xp.shape[0], 2, RET_HEADS, RET_DK, RET_DV), jnp.float32)
            yp, sc = _retention_mixer(hp, s0, ret_w_in[j], ret_decay_logit[j], ret_norm[j], ret_w_out[j])
            ys, _ = _retention_mixer(hs, state_ret[:, j], ret_w_in[j], ret_decay_logit[j], ret_norm[j], ret_w_out[j])
            new_s.append(sc.astype(xp.dtype))
        xp = xp + mp[2] * yp
        xs = xs + ms[2] * ys
        hp = _modulate(_rmsnorm(xp, norm2[i]), mp[3], mp[4])
        hs = _modulate(_rmsnorm(xs, norm2[i]), ms[3], ms[4])
        moe_args = (moe_w_router_g[i], moe_b_router_g[i], moe_w_router_e[i], moe_b_router_e[i],
                    moe_w_gate[i], moe_w_up[i], moe_w_down[i])
        xp = xp + mp[5] * _moe(hp, *moe_args)
        xs = xs + ms[5] * _moe(hs, *moe_args)
    y_prompt = _rmsnorm(xp, norm_f)
    y_sample = _rmsnorm(xs, norm_f)
    new_cache_k = jnp.stack(new_k, axis=1)
    new_cache_v = jnp.stack(new_v, axis=1)
    new_state_ret = jnp.stack(new_s, axis=1)
    return (y_prompt, y_sample, new_cache_k, new_cache_v, new_state_ret)


_drawn_inputs = setup_inputs


def setup_inputs(seed=0):
    import zlib

    import numpy as np

    out = dict(_drawn_inputs(seed))
    spreads = {}
    factors = {'attn_q_norm': 6.008,
     'pool_scale': 2.808,
     'ret_norm': 4.197,
     'moe_b_router_g': 3.74,
     'moe_b_router_e': 5.651}
    for name, (base, spread) in spreads.items():
        noise = np.random.default_rng([zlib.crc32(name.encode()), seed]).standard_normal(out[name].shape)
        drawn = base * np.exp(spread * noise) if base else spread * noise
        out[name] = __import__('jax').numpy.asarray(drawn.astype(out[name].dtype))
    for name, factor in factors.items():
        out[name] = (out[name] * factor).astype(out[name].dtype)
    return out
```

```python
from contextlib import ExitStack

import numpy as np

D = 1024
KD = D // 128
SEQ, DEC, PAST = 128, 256, 128
TILES = (SEQ + DEC) // 128
T = TILES * 128
COND = (0, 1, 1)
DEPTH = 4
HEADS, KV, HD = 8, 2, 128
NQKV = (HEADS + 2 * KV) * HD
NQK = HEADS + KV
RH, RK, RV = 8, 128, 256
GROUPS, PER = 4, 4
EXPERTS = GROUPS * PER
FE = 256
CAP = 128
PASSES = -(-T // CAP)
EPS = 1e-6
ADA_N = 384
ADA_P = 6 * D // ADA_N
PAD = 8
PW = PAD + SEQ + PAD + PAD + DEC + PAD
POFF = (PAD, 3 * PAD + SEQ, 3 * PAD + SEQ + 128)
WINDOWS = (2, 4, 8, 16)


def shape_constants():
    p = np.arange(128, dtype=np.float32)
    ident = np.eye(128, dtype=np.float32)
    tri = (p[:, None] < p[None, :]).astype(np.float32)
    iota = np.broadcast_to(p, (128, 128))
    sel = (p[:, None] % 32 == np.arange(2)[None, :]).astype(np.float32)
    tie = np.broadcast_to(np.float32(4) - np.arange(4, dtype=np.float32), (128, 4))
    caps = np.broadcast_to(CAP * np.arange(1, PASSES + 1, dtype=np.float32), (128, PASSES))
    halfpow = np.full((128, 32), -0.5, np.float32)
    base = np.concatenate([ident, tri, iota, sel, tie, caps, halfpow], axis=1).astype(np.float32)
    j, i = p[:, None], p[None, :]
    scale = np.float32(RK ** -0.5)
    ret = np.concatenate([np.maximum(i - j, 0), (i >= j) * scale, np.maximum(j - i, 0), (j >= i) * scale,
                          np.broadcast_to(i + 1, (128, 128)), np.broadcast_to(128 - i, (128, 128)),
                          127 - j, j], axis=1).astype(np.float32)
    nf = HD // 4
    inv = np.float32(10000.0) ** (-np.arange(nf, dtype=np.float32) / np.float32(nf))
    t = np.arange(DEC)
    ang = np.stack([(t // 64).astype(np.float32)[:, None] * inv, (t % 64).astype(np.float32)[:, None] * inv], 1)
    cos, sin = np.cos(ang).astype(np.float32), np.sin(ang).astype(np.float32)
    rope = np.stack([np.stack([cos, cos], 2), np.stack([-sin, sin], 2)], 1).reshape(2, 128, 2 * 128)
    rope = np.ascontiguousarray(rope.transpose(1, 0, 2))
    cnt = np.ones((4, PW), np.float32)
    for g, win in enumerate(WINDOWS):
        for off, n in ((POFF[0], SEQ), (POFF[1], DEC)):
            s = np.arange(n)
            cnt[g, off:off + n] = np.clip(s + win - win // 2, 0, n) - np.clip(s - win // 2, 0, n)
    return {"k_base": base, "k_ret": ret, "k_rope": rope, "k_cnt": (np.float32(1) / cnt)}


def build_trunk(nc, A, O, depth=DEPTH):
    import concourse.bass as bass
    from concourse import mybir

    F, R, I32 = mybir.dt.float32, mybir.dt.float32r, mybir.dt.int32
    ALU, ACT, AX = mybir.AluOpType, mybir.ActivationFunctionType, mybir.AxisListType
    ds = bass.ds
    PE, V, S, G = nc.tensor, nc.vector, nc.scalar, nc.gpsimd

    size = lambda shape: 4 * int(np.prod(shape))
    top = [-(-nc.sbuf_base // 64) * 64]

    def place(name, shape, dt=F, at=None):
        off = top[0] if at is None else at
        if at is None:
            top[0] = off + -(-size(shape) // 32) * 32
        return nc.alloc_sbuf_tensor_at(name, [128] + list(shape), dt, offset=off), off + -(-size(shape) // 32) * 32

    def keep(name, shape, dt=F):
        return place(name, shape, dt)[0]

    x = keep("x", [TILES, D])
    gu_ring = [keep(f"gate_up_weights{i}", [KD, 2 * FE]) for i in range(2)]
    dn_ring = [keep(f"down_weights{i}", [2, D]) for i in range(2)]
    panel = [keep(f"panel{i}", [KD, 512]) for i in range(2)]
    gate_bc = keep("gate_bc", [2, D])
    tmp = keep("residual_term", [2, 512])
    mraw = keep("ada_raw", [48, 2])
    mods = keep("mods", [48, 2])
    kb = keep("const_base", [3 * 128 + 2 + 4 + PASSES + 32])
    vecs = keep("vector_rows", [3, 128])
    vT = keep("vectors", [96 + 192])
    cond32 = keep("cond_columns", [KD, 32])
    wr = keep("router_weights", [DEPTH, KD, 20])
    rb = keep("router_bias", [DEPTH, 20])
    mpan = keep("ada_panel_rows", [ADA_N])
    ssq = keep("sum_squares", [4])
    msq = keep("mean_squares", [4])
    rstd = keep("rstd", [4])
    rankm = keep("rank_in_expert", [TILES, EXPERTS])
    gates_r = keep("gates_pair", [TILES, EXPERTS, 2], R)
    extra = keep("extra_passes", [4], I32)
    ones = keep("ones", [128])
    rt = keep("route_scratch", [480])
    base = top[0]

    def region(*items, start=base):
        out, at = [], start
        for name, shape, *dt in items:
            t, at = place(name, shape, *(dt or [F]), at=at)
            out.append(t)
        assert at <= nc.sbuf_usable_end, (at, nc.sbuf_usable_end)
        return out, at

    (xn, hT), mix0 = region(("xn", [TILES, D]), ("hT", [KD, T]))
    (qkv, sqv, ropet, kT, ckv, prob, probT, rope, gqk, stat), _ = region(
        ("qkv", [TILES, NQKV]), ("qk_sq", [NQK * HD]), ("rope_t", [NQK * HD]), ("kT", [KV, 512]),
        ("cache_rows", [2, KV * HD]), ("prob", [2, 896]), ("probT", [2, 896]), ("rope_tab", [2, 256]),
        ("qk_gain", [NQK * HD]), ("attn_stat", [96]), start=mix0)
    (oT, qT), _ = region(("oT", [HEADS, T]), ("qT", [HEADS, T]))
    (hp, win_a, win_b, uT, icnt), _ = region(("h_padded", [KD, PW]), ("win_a", [2, PW]), ("win_b", [2, PW]),
                                            ("pool_u", [KD, PW]), ("inv_count", [4, PW]), start=mix0)
    (yTo, rqkv, rg, rkd, rqT, rkT, rqf, rqb, rST, rs0, rs1, rso, rof, rMT, rdf, rdb, rnorm, kret,
     rsm), _ = region(
        ("yT_odd", [RH, T]), ("ret_qkv_sb", [TILES, 512]), ("ret_gate", [TILES, RV]), ("ret_k_decayed", [4, RK]), ("ret_qT", [T]), ("ret_kT", [T]),
        ("ret_q_fwd", [2, 128]), ("ret_q_bwd", [2, 128]), ("ret_scoresT", [TILES, 128]),
        ("ret_state_in", [2, RV]), ("ret_state_mid", [2, RV]), ("ret_state_out", [2, RV]),
        ("ret_o", [TILES, RV]), ("ret_mask", [RH, 128]), ("ret_dec_f", [RH, 128]), ("ret_dec_b", [RH, 128]),
        ("ret_gain", [RH, RV]), ("k_ret_sb", [6 * 128 + 2]), ("ret_small", [192]), start=mix0)
    rq, rk, rv = rqkv[:, :, 0:RK], rqkv[:, :, RK:2 * RK], rqkv[:, :, 2 * RK:512]
    (yTe,), _ = region(("yT_even", [RH, T]))
    (yhi, ylo, PT), moe0 = region(("y_hi", [PER, D], R), ("y_lo", [PER, D], R), ("PT", [PER, T], R))
    (htok,), _ = region(("h_tok", [TILES, D]), start=mix0)
    assert moe0 - base >= 3 * size([TILES, D])
    (hhi, hlo, Pm, hg, silu, act, actT, gsum, gslot), _ = region(
        ("h_hi", [TILES, D], R), ("h_lo", [TILES, D], R), ("P", [2, TILES, CAP], R), ("hT_gathered", [2, KD, CAP]),
        ("silu", [FE]), ("act", [FE]), ("actT", [2, CAP]), ("gate_slot", [1]), ("gate_pair", [2, 2]), start=moe0)
    (ofin,), _ = region(("y_final", [TILES, D]), start=mix0)

    ident, tri, iota = kb[:, 0:128], kb[:, 128:256], kb[:, 256:384]
    sel = kb[:, 384:386]
    tie = kb[:, 386:390]
    caps = kb[:, 390:390 + PASSES]
    hpow = kb[:, 390 + PASSES:422 + PASSES]
    biasT = vT[:, 96:288]

    ps = [nc.alloc_psum_tensor(f"bank{i}", [128, 512], F) for i in range(8)]
    sems = {}

    def sem(name):
        if name not in sems:
            sems[name] = nc.alloc_semaphore(name)
        return sems[name]

    panels = [("ada", 0, i) for i in range(ADA_P)]
    first_panel = {("ada", 0): 0}
    prj_base = {}
    prj = 0
    for l in range(depth):
        kind = l % 3
        first_panel["mix", l] = len(panels)
        prj_base[l] = prj
        if kind == 0:
            panels += [("attn", l, i) for i in range(5)]
            prj += 5 * TILES
        elif kind == 1:
            panels += [("pool", l, 0)]
            prj += 2 * TILES
        else:
            panels += [("ret", l, i) for i in range(2 * RH)] + [("rout", l, i) for i in range(4)]
            prj += 2 * TILES
        if l + 1 < depth:
            first_panel["ada", l + 1] = len(panels)
            panels += [("ada", l + 1, i) for i in range(ADA_P)]

    def released(s):
        kind, l, i = panels[s]
        if kind == "ada":
            return sem("ada_product"), l * ADA_P + i + 1
        if kind == "attn":
            return sem("proj_done"), prj_base[l] + TILES * (i + 1)
        if kind == "pool":
            return sem("proj_done"), prj_base[l] + 2 * TILES
        if kind == "ret":
            return (sem("ret_qkv"), i // 2 + 1) if i % 2 == 0 else (sem("ret_gate"), i // 2 + 1)
        return sem("proj_done"), prj_base[l] + (TILES if i < 2 else 2 * TILES)

    def slot_of(s):
        return s % 2

    def panel_landed(eng, s, i=0, per=0):
        eng.wait_ge(sem(f"panel_landed{s % 2}"), 48 * (s // 2 + 1) + i * (48 * per // 2))

    ada_w = A["w_ada"].rearrange("l (k p) n -> l p k n", p=128)
    qkv_w = A["attn_w_qkv"].rearrange("l (k p) n -> l p k n", p=128)
    wo_w = A["attn_w_o"].rearrange("l (k p) n -> l p k n", p=128)
    rin_w = A["ret_w_in"].rearrange("l (k p) n -> l p k n", p=128)
    rout_w = A["ret_w_out"].rearrange("l (k p) n -> l p k n", p=128)
    wg_w = A["moe_w_gate"].rearrange("l e (k p) f -> l e p k f", p=128)
    wu_w = A["moe_w_up"].rearrange("l e (k p) f -> l e p k f", p=128)
    wd_w = A["moe_w_down"].rearrange("l e (c p) n -> l e p c n", p=128)

    CREDIT = {"ada_evac": 1, "ada_col": 1, "ada_mod": 1}
    if depth > 2:
        CREDIT.update(ret_in_sb=1, ret_gate_sb=1, ret_yT_sb=1, ret_O_ps=1, state_stored=16)
    for z in ("m", "o"):
        CREDIT.update({z + "_hg_act": 1, z + "_hg_dve": 1, z + "_act": 2, z + "_PT_sb": 1, z + "_actT_sb": 1,
                       z + "_actT": 1, z + "_scatter": 1, z + "_term": 1, z + "_PT": 2, z + "_gateup": 2,
                       z + "_down": 4, z + "_y_hi": 1, z + "_y_lo": 1, z + "_added": 2})
    for n in ("hg_act", "hg_dve", "act", "PT_sb", "actT_sb", "actT", "scatter", "term", "PT", "gateup", "down",
              "y_hi", "y_lo", "added", "P", "gather", "silu"):
        for z in "mo":
            sem(f"{z}_{n}")
    for n in CREDIT:
        sem(n)

    def atleast(eng, name, n):
        eng.wait_ge(sem(name), n + CREDIT.get(name, 0))

    class Order:

        def __init__(self, eng, name):
            self.eng, self.sem, self.n, self.base = eng, sem(name), 0, 0

        def __call__(self, ins):
            self.n += 1
            ins.then_inc(self.sem, 1)
            self.eng.wait_ge(self.sem, self.base + self.n)

        def enter(self, i, per):
            self.kept, self.per = self.n, per
            self.base, self.n = i * per + self.n, 0

        def leave(self, times):
            assert self.n == self.per, (self.n, self.per)
            self.n, self.base = self.kept + times * self.per, 0

    block = nc.Block()
    ctx = ExitStack()
    ctx.enter_context(block)

    def load_panel(sp, s, src_of, i=0, per=0):
        dst = panel[s % 2]
        parts = src_of(dst)
        for n, (d, a) in enumerate(parts):
            sp.dma_start(d, a).then_inc(sem(f"panel_landed{s % 2}"), 48 - 16 * (len(parts) - 1) if n == 0 else 16)

    def panel_source(kind, l, i):
        a = l // 3
        if kind == "ada":
            return lambda d: [(d[:, :, 0:ADA_N], ada_w[l, :, :, ds(i * ADA_N, ADA_N)])]
        if kind == "attn" and not isinstance(i, int) or kind == "attn" and i < 3:
            return lambda d: [(d[:, :, :], qkv_w[a, :, :, i * 512:(i + 1) * 512])]
        if kind == "attn":
            return lambda d: [(d[:, :, :], wo_w[a, :, :, (i - 3) * 512:(i - 2) * 512])]
        if kind == "pool":
            pw = A["pool_w"][a].rearrange("g (c p) n -> p (g c) n", p=128)
            return lambda d: [(d[:, :, 0:256], pw)]
        if kind == "rout":
            return lambda d: [(d[:, :, :], rout_w[0, :, (i % 2) * 8:(i % 2) * 8 + 8, (i // 2) * 512:(i // 2) * 512 + 512])]
        raise ValueError(kind)

    def ret_qkv_source(h):
        return lambda d: [(d[:, :, 0:RK], rin_w[0, :, :, ds(h * RK, RK)]),
                          (d[:, :, RK:2 * RK], rin_w[0, :, :, ds(h * RK + RH * RK, RK)]),
                          (d[:, :, 2 * RK:512], rin_w[0, :, :, ds(h * RV + 2 * RH * RK, RV)])]

    def ret_gate_source(h):
        return lambda d: [(d[:, :, 0:RV], rin_w[0, :, :, ds(h * RV + 2 * RH * RK + RH * RV, RV)])]

    def at_e(w, l, e):
        return w[l, e] if isinstance(e, int) else w[l, ds(e, 1)].rearrange("o p k f -> (o p) k f")

    def load_expert(sp, z, l, e, slot):
        sp.dma_start(gu_ring[slot][:, :, 0:FE], at_e(wg_w, l, e)).then_inc(sem(f"{z}_gu_landed{slot}"), 16)
        sp.dma_start(gu_ring[slot][:, :, FE:2 * FE], at_e(wu_w, l, e)).then_inc(sem(f"{z}_gu_landed{slot}"), 16)

    def load_down(sp, z, l, e, slot):
        sp.dma_start(dn_ring[slot][:], at_e(wd_w, l, e)).then_inc(sem(f"{z}_dn_landed{slot}"), 16)

    @block.sync
    def _(sp):
        sp.dma_start(vecs[0:96, 0, :], A["vectors"]).then_inc(sem("vec_landed"), 16)
        sp.dma_start(vecs[0:96, 1:3, :], A["b_ada"].rearrange("l (c n) -> (l c) n", n=128)
                     .rearrange("(a r) n -> r a n", a=2)).then_inc(sem("vec_landed"), 16)
        sp.dma_start(kb[:], A["k_base"]).then_inc(sem("const_landed"), 16)
        passes = []
        for s in range(2):
            load_panel(sp, s, panel_source("ada", 0, s))
        sp.dma_start(x[:, 0, :], A["x_prompt"][0]).then_inc(sem("x_landed"), 16)
        sp.dma_start(x[:, 1:3, :], A["x_sample"][0].rearrange("(a p) n -> p a n", p=128)).then_inc(sem("x_landed"), 16)
        with sp.Fori(0, (ADA_P - 2) // 2) as i:
            for j in range(2):
                sp.wait_ge(sem("ada_product"), 2 * i + j + 1)
                load_panel(sp, j, panel_source("ada", 0, 2 * i + j + 2))
        for l in range(depth):
            f = first_panel["mix", l]
            n = (first_panel["ada", l + 1] if l + 1 < depth else len(panels)) - f
            if l % 3 == 2:
                for s in (f, f + 1):
                    sp.wait_ge(*released(s - 2))
                    load_panel(sp, s, ret_qkv_source(0) if s == f else ret_gate_source(0))
            else:
                for s in range(f, f + min(n, 2)):
                    sp.wait_ge(*released(s - 2))
                    load_panel(sp, s, panel_source(*panels[s]))
            if l:
                sp.wait_ge(sem("experts_read"), l)
            for e in range(2):
                load_expert(sp, "m", l, e, e)
                load_down(sp, "m", l, e, e)
            if l % 3 == 2:
                with sp.Fori(0, RH - 1) as h:
                    sp.wait_ge(sem("ret_qkv"), h + 1)
                    load_panel(sp, f, ret_qkv_source(h + 1))
                    sp.wait_ge(sem("ret_gate"), h + 1)
                    load_panel(sp, f + 1, ret_gate_source(h + 1))
                rest = range(f + 2 * RH, f + n)
            else:
                rest = range(f + min(n, 2), f + n)
            for s in rest:
                sp.wait_ge(*released(s - 2))
                load_panel(sp, s, panel_source(*panels[s]))
            nxt = l + 1 < depth
            a0 = first_panel["ada", l + 1] if nxt else 0
            if nxt:
                for j in range(2):
                    sp.wait_ge(*released(a0 + j - 2))
                    load_panel(sp, a0 + j, panel_source("ada", l + 1, j))
            with sp.Fori(0, EXPERTS // 2 - 1) as i:
                for j in range(2):
                    e = 2 * i + j + 2
                    sp.wait_ge(sem("m_gateup"), CREDIT["m_gateup"] + l * EXPERTS + e - 1)
                    load_expert(sp, "m", l, e, j)
                    sp.wait_ge(sem("m_down"), CREDIT["m_down"] + 2 * (l * EXPERTS + e - 1))
                    load_down(sp, "m", l, e, j)
                    if nxt:
                        sp.wait_ge(sem("ada_product"), (l + 1) * ADA_P + e - 1)
                        load_panel(sp, a0 + j, panel_source("ada", l + 1, e))
            sp.wait_ge(sem("routed"), l + 1)
            r = sp.value_load(extra[0:1, l:l + 1], min_val=0, max_val=PASSES - 1)
            done = sum(passes) if passes else 0
            with sp.If(r > 0):
                sp.wait_ge(sem("m_gateup"), CREDIT["m_gateup"] + (l + 1) * EXPERTS)
                sp.wait_ge(sem("m_down"), CREDIT["m_down"] + 2 * (l + 1) * EXPERTS)
                with sp.Fori(0, r) as p:
                    with sp.Fori(0, EXPERTS // 2) as i:
                        for j in range(2):
                            q = (done + p) * EXPERTS + 2 * i + j
                            atleast(sp, "o_gateup", q - 1)
                            load_expert(sp, "o", l, 2 * i + j, j)
                            atleast(sp, "o_down", 2 * q - 2)
                            load_down(sp, "o", l, 2 * i + j, j)
            passes.append(r)
        for t in range(TILES):
            sp.wait_ge(sem("final_ready"), t + 1)
            dst = O["y_prompt"][0] if t == 0 else O["y_sample"][0, (t - 1) * 128:t * 128]
            sp.dma_start(dst, ofin[:, t, :]).then_inc(sem("stored"), 16)
        sp.wait_ge(sem("stored"), 16 * TILES)
        sp.wait_ge(sem("cache_stored"), 32 * ((depth + 2) // 3))
        if depth > 2:
            atleast(sp, "state_stored", 16 * RH)

    def pe_norm(pe, n):
        pe.wait_ge(sem("xn_ready"), TILES * (n + 1))
        for k in range(KD):
            if k >= 4:
                pe.wait_ge(sem(("hT_dve", "hT_act")[k % 2]), KD // 2 * n + (k - 4) // 2 + 1)
            for t in range(TILES):
                last = PE.transpose(ps[k % 4][:, t * 128:(t + 1) * 128], xn[:, t, k * 128:(k + 1) * 128], ident)
            last.then_inc(sem("hT_ps"), 1)

    def pe_broadcast(bank, v, c, half):
        for q in range(4):
            last = PE.matmul(ps[bank][:, q * 128:(q + 1) * 128],
                             mods[:, v * KD + 4 * half + q, c:c + 1].broadcast_to([128, 128]), ident,
                             start=True, stop=True)
        return last

    def pe_gate_bc(pe, n, v):
        for c in range(2):
            for half in range(2):
                pe_broadcast(4 + 2 * c + half, v, c, half).then_inc(sem("gate_ps"), 1)

    def pe_ada_product(pe, idx, s, i=0, per=0):
        panel_landed(pe, s, i, per)
        atleast(pe, "ada_evac", idx)
        atleast(pe, "ada_mod", idx)
        for kk in range(2):
            for g in range(4):
                last = PE.matmul(ps[4][32 * g:32 * g + 32, 0:ADA_N], cond32[:, 2 * g + kk, :],
                                 panel[s % 2][:, 2 * g + kk, 0:ADA_N], start=kk == 0, stop=kk == 1)
        last.then_inc(sem("ada_product"), 1)

    def pe_ada_columns(pe, idx):
        atleast(pe, "ada_evac", idx + 1)
        for c in range(ADA_N // 128):
            last = PE.matmul(ps[4][:, ADA_N + 2 * c:ADA_N + 2 * c + 2], mpan[:, c * 128:(c + 1) * 128], sel, start=True, stop=True)
        last.then_inc(sem("ada_col"), 1)

    def pe_project(pe, l, i, s, nk, lhs, bank0, group=0, rhs_k=None, start=True, stop=True, signal=True):
        for t in range(TILES):
            for k in range(nk):
                last = PE.matmul(ps[bank0 + t][:], lhs(k, t), panel[s % 2][:, k, :],
                                 start=start and k == 0, stop=stop and k == nk - 1)
            if signal:
                last.then_inc(sem("proj_done"), 1)
        return last

    def pe_attention(pe, l):
        f, a = first_panel["mix", l], l // 3
        for i in range(3):
            panel_landed(pe, f + i)
            if i == 0:
                pe.wait_ge(sem("hT_dve"), KD // 2 * (2 * l + 1))
                pe.wait_ge(sem("hT_act"), KD // 2 * (2 * l + 1))
            if i == 1:
                pe.wait_ge(sem("gate_bc"), 4 * (2 * l + 1))
            if i == 2:
                pe.wait_ge(sem("qkv_sb"), 9 * a + 3)
            pe_project(pe, l, i, f + i, KD, lambda k, t: hT[:, k, t * 128:(t + 1) * 128], (0, 4, 0)[i])
        pe.wait_ge(sem("cache_landed"), 32 * (a + 1))
        pe.wait_ge(sem("qk_ready"), TILES * (a + 1))
        pe.wait_ge(sem("qkv_sb"), 9 * (a + 1))
        for h in range(HEADS + KV):
            if h >= 4:
                pe.wait_ge(sem("qkT_sb"), NQK * a + h - 3)
            b = ps[h % 4]
            for t in range(TILES):
                last = PE.transpose(b[:, t * 128:(t + 1) * 128], qkv[:, t, h * HD:(h + 1) * HD], ident)
            if h >= HEADS:
                last = PE.transpose(b[:, 384:512], ckv[:, 0, (h - HEADS) * HD:(h - HEADS + 1) * HD], ident)
            last.then_inc(sem("qkT_ps"), 1)
        pe.wait_ge(sem("qkT_sb"), NQK * (a + 1))

        def scores(h):
            b0, g = 2 * (h % 2), h // (HEADS // KV)
            if h >= 2:
                pe.wait_ge(sem("prob"), 3 * (HEADS * a + h - 1))
            PE.matmul(ps[b0][:, 0:128], qT[:, h, 0:128], kT[:, g, 0:128], start=True, stop=True)
            PE.matmul(ps[b0][:, 128:512], qT[:, h, 128:256], kT[:, g, 128:512], start=True, stop=True)
            PE.matmul(ps[b0 + 1][:, 0:384], qT[:, h, 256:384], kT[:, g, 128:512], start=True, stop=True)\
                .then_inc(sem("scores"), 1)

        def outputs(h):
            g = h // (HEADS // KV)
            n = HEADS * a + h
            pe.wait_ge(sem("prob_norm"), n + 1)
            if h:
                pe.wait_ge(sem("probT_sb"), 2 * n)
            for c in range(7):
                last = PE.transpose(ps[4 + c // 4][:, (c % 4) * 128:(c % 4) * 128 + 128],
                                    prob[:, h % 2, c * 128:(c + 1) * 128], ident)
                if c in (3, 6):
                    last.then_inc(sem("probT_ps"), 1)
            pe.wait_ge(sem("probT_sb"), 2 * (n + 1))
            if h >= 2:
                pe.wait_ge(sem("oT_sb"), n - 1)
            v = lambda t: qkv[:, t, (NQK + g) * HD:(NQK + g + 1) * HD]
            cv = ckv[:, 1, g * HD:(g + 1) * HD]
            b = ps[6 + h % 2]
            PE.matmul(b[:, 0:128], v(0), probT[:, h % 2, 0:128], start=True, stop=True)
            for t in (1, 2):
                for c, vals in enumerate((cv, v(1), v(2))):
                    at = 128 + (t - 1) * 384 + c * 128
                    last = PE.matmul(b[:, t * 128:(t + 1) * 128], vals, probT[:, h % 2, at:at + 128],
                                     start=c == 0, stop=c == 2)
            last.then_inc(sem("oT_ps"), 1)

        scores(0)
        for h in range(HEADS):
            if h + 1 < HEADS:
                scores(h + 1)
            outputs(h)
        for i in range(3, 5):
            panel_landed(pe, f + i)
            if i == 3:
                pe.wait_ge(sem("oT_sb"), HEADS * (a + 1))
            pe_project(pe, l, i, f + i, HEADS, lambda k, t: oT[:, k, t * 128:(t + 1) * 128], 0 if i == 3 else 3)

    def pe_pool(pe, l):
        f = first_panel["mix", l]
        panel_landed(pe, f)
        for half in range(2):
            pe.wait_ge(sem("pool_u"), 2 * half + 2)
            if half == 1:
                pe.wait_ge(sem("gate_bc"), 4 * (2 * l + 1))
            for t in range(TILES):
                for g in range(2):
                    for c in range(2):
                        q = 2 * (2 * half + g) + c
                        last = PE.matmul(ps[3 * half + t][:, g * 256:(g + 1) * 256],
                                         uT[:, q, POFF[t]:POFF[t] + 128], panel[f % 2][:, q, 0:256],
                                         start=c == 0, stop=c == 1)
                last.then_inc(sem("proj_done"), 1)

    def pe_retention(pe, l):
        f = first_panel["mix", l]
        pe.wait_ge(sem("hT_dve"), KD // 2 * (2 * l + 1))
        pe.wait_ge(sem("hT_act"), KD // 2 * (2 * l + 1))
        pe.wait_ge(sem("gate_bc"), 4 * (2 * l + 1))
        with pe.Fori(0, RH) as h:
            panel_landed(pe, f, h, 2)
            atleast(pe, "ret_in_sb", 3 * h)
            for t in range(TILES):
                for k in range(KD):
                    last = PE.matmul(ps[t][:], hT[:, k, t * 128:(t + 1) * 128], panel[f % 2][:, k, :],
                                     start=k == 0, stop=k == KD - 1)
            last.then_inc(sem("ret_qkv"), 1)
            panel_landed(pe, f + 1, h, 2)
            atleast(pe, "ret_gate_sb", h)
            for t in range(TILES):
                for k in range(KD):
                    last = PE.matmul(ps[3 + t // 2][:, (t % 2) * 256:(t % 2) * 256 + 256],
                                     hT[:, k, t * 128:(t + 1) * 128], panel[(f + 1) % 2][:, k, 0:256],
                                     start=k == 0, stop=k == KD - 1)
            last.then_inc(sem("ret_gate"), 1)
            atleast(pe, "ret_in_sb", 3 * h + 3)
            atleast(pe, "ret_yT_sb", 2 * h)
            for t in range(TILES):
                PE.transpose(ps[5][:, t * 128:(t + 1) * 128], rq[:, t, :], ident)
            for t in range(TILES):
                last = PE.transpose(ps[6][:, t * 128:(t + 1) * 128], rk[:, t, :], ident)
            last.then_inc(sem("ret_T_ps"), 1)
            pe.wait_ge(sem("ret_T_sb"), 4 * h + 4)
            for t in range(TILES):
                last = PE.matmul(ps[7][:, t * 128:(t + 1) * 128], rkT[:, t * 128:(t + 1) * 128],
                                 rqT[:, t * 128:(t + 1) * 128], start=True, stop=True)
            last.then_inc(sem("ret_S_ps"), 1)
            pe.wait_ge(sem("ret_kd"), h + 1)
            for n, t in enumerate((0, 0, 1, 2)):
                last = PE.matmul(ps[5 + n // 2][:, (n % 2) * 256:(n % 2) * 256 + 256], rkd[:, n, :], rv[:, t, :],
                                 start=True, stop=True)
            last.then_inc(sem("ret_U_ps"), 1)
            pe.wait_ge(sem("ret_S_sb"), h + 1)
            pe.wait_ge(sem("ret_mid"), h + 1)
            pe.wait_ge(sem("state_in"), 16 * h + 16)
            PE.matmul(ps[7][:, 0:256], rST[:, 0, :], rv[:, 0, :], start=True, stop=True)
            PE.matmul(ps[7][:, 256:512], rST[:, 1, :], rv[:, 1, :], start=True, stop=False)
            PE.matmul(ps[7][:, 256:512], rqf[:, 0, :], rs0[:, 0, :], start=False, stop=False)
            PE.matmul(ps[7][:, 256:512], rqb[:, 0, :], rs1[:, 1, :], start=False, stop=True)
            pe.wait_ge(sem("ret_state_out"), h + 1)
            PE.matmul(ps[5][:, 0:256], rST[:, 2, :], rv[:, 2, :], start=True, stop=False)
            PE.matmul(ps[5][:, 0:256], rqf[:, 1, :], rs1[:, 0, :], start=False, stop=False)
            PE.matmul(ps[5][:, 0:256], rqb[:, 1, :], rs0[:, 1, :], start=False, stop=True).then_inc(sem("ret_O_ps"), 1)
            pe.wait_ge(sem("ret_y"), h + 1)
            for c in range(2):
                for t in range(TILES):
                    last = PE.transpose(ps[6 - c][:, t * 128:(t + 1) * 128], rof[:, t, c * 128:(c + 1) * 128], ident)
                last.then_inc(sem("ret_yT_ps"), 1)
        atleast(pe, "ret_yT_sb", 2 * RH)
        s = f + 2 * RH
        for half in range(2):
            for part in range(2):
                panel_landed(pe, s)
                for t in range(TILES):
                    for k in range(8):
                        src = (yTe, yTo)[k % 2]
                        last = PE.matmul(ps[3 * half + t][:], src[:, 4 * part + k // 2, t * 128:(t + 1) * 128],
                                         panel[s % 2][:, k, :], start=part == 0 and k == 0,
                                         stop=part == 1 and k == 7)
                    if part == 1:
                        last.then_inc(sem("proj_done"), 1)
                s += 1

    def pe_route(pe, l):
        n = 2 * l + 1
        pe.wait_ge(sem("hT_dve"), KD // 2 * (n + 1))
        pe.wait_ge(sem("hT_act"), KD // 2 * (n + 1))
        for t in range(TILES):
            for k in range(KD):
                last = PE.matmul(ps[2][:, t * 20:(t + 1) * 20], hT[:, k, t * 128:(t + 1) * 128], wr[:, l, k, :],
                                 start=k == 0, stop=k == KD - 1)
        last.then_inc(sem("logits"), 1)
        for c in range(2):
            if c:
                pe.wait_ge(sem("h_tok"), 3 * l + 1)
            for half in range(2):
                pe_broadcast(4 + half, 4, c, half)
                last = pe_broadcast(6 + half, 3, c, half)
            last.then_inc(sem("mod_ps"), 1)
        pe.wait_ge(sem("h_tok"), 3 * l + 3)
        pe_gate_bc(pe, n, 5)
        pe.wait_ge(sem("assigned"), l + 1)
        asg = rt[:, 96:96 + TILES * EXPERTS].rearrange("p (t e) -> p t e", t=TILES)
        for t in range(TILES):
            PE.matmul(ps[3][:, t * 16:(t + 1) * 16], tri, asg[:, t, :], start=True, stop=t == 0)
            for u in range(t):
                PE.matmul(ps[3][:, t * 16:(t + 1) * 16], ones[:], asg[:, u, :], start=False, stop=u == t - 1)
        for t in range(TILES):
            last = PE.matmul(ps[3][:, 64:80], ones[:], asg[:, t, :], start=t == 0, stop=t == TILES - 1)
        last.then_inc(sem("ranks"), 1)
        pe.wait_ge(sem("gate_bc"), 4 * (n + 1))

    def pe_experts(pe, z, it, l, g, ada):
        def gather(j):
            q = it * PER + j
            atleast(pe, z + "_P", q + 1)
            atleast(pe, z + "_hg_act", q)
            atleast(pe, z + "_hg_dve", q)
            for k in range(KD):
                for t in range(TILES):
                    for n, part in enumerate((hhi, hlo)):
                        last = PE.matmul(ps[k // 4][:, (k % 4) * 128:(k % 4) * 128 + CAP],
                                         part[:, t, k * 128:(k + 1) * 128], Pm[:, j % 2, t, :],
                                         start=t == 0 and n == 0, stop=t == TILES - 1 and n == 1)
            last.then_inc(sem(z + "_gather"), 1)
            atleast(pe, z + "_PT_sb", q)
            for t in range(TILES):
                PE.matmul(ps[5][0:CAP, T:T + 2], Pm[:, j % 2, t, :], gates_r[:, t, ds(g * PER + j, 1), :],
                          start=t == 0, stop=t == TILES - 1)
            for t in range(TILES):
                last = PE.transpose(ps[5][0:CAP, t * 128:(t + 1) * 128], Pm[:, j % 2, t, :].bitcast(F), ident)
            last.then_inc(sem(z + "_PT"), 1)

        for j in range(PER):
            q = it * PER + j
            if j == 0:
                gather(0)
            atleast(pe, z + "_hg_act", q + 1)
            atleast(pe, z + "_hg_dve", q + 1)
            if z == "m":
                pe.wait_ge(sem(f"m_gu_landed{j % 2}"), 64 * it + 32 * (j // 2 + 1))
            else:
                pe.wait_ge(sem(f"o_gu_landed{j % 2}"), 64 * it + 32 * (j // 2 + 1))
            atleast(pe, z + "_act", q)
            for k in range(KD):
                last = PE.matmul(ps[2][0:CAP, :], hg[:, j % 2, k, :], gu_ring[j % 2][:, k, :],
                                 start=k == 0, stop=k == KD - 1)
            last.then_inc(sem(z + "_gateup"), 1)
            if j + 1 < PER:
                gather(j + 1)
            if ada is not None:
                pe_ada_product(pe, ada[0] + g * PER + j, ada[1] + j, g, PER)
            atleast(pe, z + "_act", q + 1)
            atleast(pe, z + "_actT_sb", q)
            for c in range(2):
                last = PE.transpose(ps[3][:, c * 128:c * 128 + CAP], act[0:CAP, c * 128:(c + 1) * 128], ident[0:CAP, 0:CAP])
            last.then_inc(sem(z + "_actT"), 1)
            if ada is not None:
                pe_ada_columns(pe, ada[0] + g * PER + j)
            atleast(pe, z + "_actT_sb", q + 1)
            pe.wait_ge(sem(f"{z}_dn_landed{j % 2}"), 32 * it + 16 * (j // 2 + 1))
            atleast(pe, z + "_y_hi", 2 * q)
            atleast(pe, z + "_y_lo", 2 * q)
            if j == 0:
                atleast(pe, z + "_term", 6 * it)
            for half in range(2):
                for c in range(2):
                    last = PE.matmul(ps[6 + half][0:CAP, :], actT[:, c, :], dn_ring[j % 2][:, c, half * 512:half * 512 + 512],
                                     start=c == 0, stop=c == 1)
                last.then_inc(sem(z + "_down"), 1)
        q = it * PER + PER
        atleast(pe, z + "_y_hi", 2 * q)
        atleast(pe, z + "_y_lo", 2 * q)
        atleast(pe, z + "_PT_sb", q)
        for m in range(2 * TILES):
            t, half = m // 2, m % 2
            if m >= 2:
                atleast(pe, z + "_term", 6 * it + m - 1)
            for j in range(PER):
                for n, part in enumerate((yhi, ylo)):
                    last = PE.matmul(ps[6 + half][:], PT[0:CAP, j, t * 128:(t + 1) * 128],
                                     part[0:CAP, j, half * 512:half * 512 + 512],
                                     start=j == 0 and n == 0, stop=j == PER - 1 and n == 1)
            last.then_inc(sem(z + "_scatter"), 1)

    def expert_passes(eng, body, passes, l, before=None):
        with eng.Fori(0, GROUPS) as g:
            body("m", l * GROUPS + g, g, True)
        r = eng.value_load(extra[0:1, l:l + 1], min_val=0, max_val=PASSES - 1)
        done = sum(passes) if passes else 0
        with eng.If(r > 0):
            with eng.Fori(0, r) as p:
                if before is not None:
                    before(done + p)
                with eng.Fori(0, GROUPS) as g:
                    body("o", (done + p) * GROUPS + g, g, False)
        passes.append(r)

    @block.tensor
    def _(pe):
        pe.wait_ge(sem("vec_landed"), 32)
        pe.wait_ge(sem("const_landed"), 16)
        for a in range(3):
            last = PE.transpose(ps[0][:, a * 96:(a + 1) * 96], vecs[0:96, a, :], ident[0:96, 0:96])
        last.then_inc(sem("vT_ps"), 1)
        pe.wait_ge(sem("cond_ready"), 1)
        with pe.Fori(0, ADA_P // 2) as i:
            for j in range(2):
                pe_ada_product(pe, 2 * i + j, j, i, 2)
                pe_ada_columns(pe, 2 * i + j)
        passes = []
        for l in range(depth):
            pe.wait_ge(sem("mods_ready"), l + 1)
            pe_norm(pe, 2 * l)
            pe_gate_bc(pe, 2 * l, 2)
            (pe_attention, pe_pool, pe_retention)[l % 3](pe, l)
            pe_norm(pe, 2 * l + 1)
            pe_route(pe, l)
            pe.wait_ge(sem("h_lo"), TILES * (l + 1))
            pe.wait_ge(sem("routed"), l + 1)
            ada = ((l + 1) * ADA_P, first_panel["ada", l + 1]) if l + 1 < depth else None
            expert_passes(pe, lambda z, it, g, first: pe_experts(pe, z, it, l, g, ada if first else None), passes, l)
            pe.drain().then_inc(sem("experts_read"), 1)
        for half in range(2):
            for q in range(4):
                last = PE.matmul(ps[4 + half][:, q * 128:(q + 1) * 128],
                                 vT[:, 72 + 4 * half + q:73 + 4 * half + q].broadcast_to([128, 128]), ident,
                                 start=True, stop=True)
        last.then_inc(sem("normf_ps"), 1)

    def mod_col(v, k, c):
        return mods[:, v * KD + k, c:c + 1]

    def hT_out(l, sub, k, c):
        if l % 3 == 1 and sub == 0:
            return hp[:, k, POFF[0]:POFF[0] + 128] if c == 0 else hp[:, k, POFF[1]:POFF[1] + DEC]
        return hT[:, k, 0:128] if c == 0 else hT[:, k, 128:T]

    @block.vector
    def _(dve):
        step = Order(dve, "dve_step")

        def finish_mods(l):
            for v in range(6):
                out, raw = mods[:, v * KD:(v + 1) * KD, :], mraw[:, v * KD:(v + 1) * KD, :]
                if v in (1, 4):
                    gain = vT[:, (0 if v == 1 else 32) + l * KD:(0 if v == 1 else 32) + (l + 1) * KD]
                    last = V.scalar_tensor_tensor(out, raw, 1.0, gain.unsqueeze(2).broadcast_to([128, KD, 2]), ALU.add, ALU.mult)
                elif v == 2 and l % 3 == 1:
                    last = V.tensor_tensor(out, raw, vT[:, 64:72].unsqueeze(2).broadcast_to([128, KD, 2]), ALU.mult)
                else:
                    last = V.tensor_copy(out, raw)
            last.then_inc(sem("mods_ready"), 1)
            dve.wait_ge(sem("mods_ready"), l + 1)

        def ada_mod(l, idx, p):
            atleast(dve, "ada_col", idx + 1)
            V.tensor_tensor(mraw[:, ds(3 * p, 3), :], ps[4][:, ADA_N:ADA_N + 6].rearrange("q (c o) -> q c o", c=3),
                            biasT[:, ds(l * 48 + 3 * p, 3)].unsqueeze(2).broadcast_to([128, 3, 2]), ALU.add)\
                .then_inc(sem("ada_mod"), 1)

        def mean_square(n):
            dve.wait_ge(sem("ssq"), TILES * (n + 1))
            V.tensor_scalar(msq[:, 0:3], ssq[:, 0:3], 1.0 / D, EPS, ALU.mult, ALU.add).then_inc(sem("msq"), 1)

        def norm(l, sub):
            n = 2 * l + sub
            mean_square(n)
            for k in range(0, KD, 2):
                dve.wait_ge(sem("hT_ps"), KD * n + k + 1)
                for c, src in enumerate((ps[k % 4][:, 0:128], ps[k % 4][:, 128:T])):
                    last = V.tensor_scalar(hT_out(l, sub, k, c), src, mod_col(1 + 3 * sub, k, c),
                                           mod_col(3 * sub, k, c), ALU.mult, ALU.add)
                last.then_inc(sem("hT_dve"), 1)

        def residual(l, order):
            b = prj_base[l] + (3 * TILES if l % 3 == 0 else 0)
            dve.wait_ge(sem("gate_bc"), 4 * (2 * l + 1))
            for m in range(2 * TILES):
                half, t = m // TILES, m % TILES
                dve.wait_ge(sem("proj_done"), b + m + 1)
                if 6 * l + m >= 2:
                    dve.wait_ge(sem("mix_added"), 6 * l + m - 1)
                if m == 0 and l:
                    dve.wait_ge(sem("layer_done"), l)
                V.tensor_tensor(tmp[:, m % 2, :], ps[3 * half + t][:], gate_bc[:, COND[t], half * 512:half * 512 + 512],
                                ALU.mult).then_inc(sem("mix_term"), 1)

        def attention(l):
            a = l // 3
            sums = stat[:, 0:30].rearrange("p (t h) -> p t h", t=TILES)
            means, rs = stat[:, 32:62], stat[:, 64:94].rearrange("p (t h) -> p t h", t=TILES)
            for t in range(TILES):
                dve.wait_ge(sem("qkv_sb"), 9 * a + 7 + t)
                qk = qkv[:, t, 0:NQK * HD]
                step(V.tensor_tensor(sqv[:], qk, qk, ALU.mult))
                step(V.tensor_reduce(sums[:, t, :], sqv[:].rearrange("p (h d) -> p h d", d=HD), AX.X, ALU.add))
            V.tensor_scalar(means, stat[:, 0:30], 1.0 / HD, EPS, ALU.mult, ALU.add).then_inc(sem("qk_ms"), 1)
            dve.wait_ge(sem("qk_rstd"), a + 1)
            dve.wait_ge(sem("attn_landed"), 64 * (a + 1))
            for t in range(TILES):
                qk3 = qkv[:, t, 0:NQK * HD].rearrange("p (h d) -> p h d", d=HD)
                step(V.tensor_tensor(qk3, qk3, rs[:, t, :].unsqueeze(2).broadcast_to([128, NQK, HD]), ALU.mult))
                last = V.tensor_tensor(qkv[:, t, 0:NQK * HD], qkv[:, t, 0:NQK * HD], gqk[:], ALU.mult)
                if t == 0:
                    last.then_inc(sem("qk_ready"), 1)
                    continue
                step(last)
                x5 = qkv[:, t, 0:NQK * HD].rearrange("p (h a b f) -> p h a b f", h=NQK, a=2, b=2)
                r5 = ropet[:].rearrange("p (h a b f) -> p h a b f", h=NQK, a=2, b=2)
                tab = rope[:, t - 1, :].rearrange("p (s a b f) -> p s a b f", s=2, a=2, b=2)
                for b in range(2):
                    for hh in range(2):
                        last = V.tensor_tensor(r5[:, :, hh, b, :], x5[:, :, hh, 1 - b, :],
                                               tab[:, 1, hh, b, :].unsqueeze(1).broadcast_to([128, NQK, 32]), ALU.mult)
                step(last)
                step(V.tensor_tensor(qk3, qk3, rope[:, t - 1, 0:128].unsqueeze(1).broadcast_to([128, NQK, HD]), ALU.mult))
                V.tensor_tensor(qkv[:, t, 0:NQK * HD], qkv[:, t, 0:NQK * HD], ropet[:], ALU.add).then_inc(sem("qk_ready"), 1)
                dve.wait_ge(sem("qk_ready"), TILES * a + t + 1)
            mx = stat[:, 0:12].rearrange("p (b c) -> p b c", b=4)
            den = stat[:, 12:24].rearrange("p (b c) -> p b c", b=4)
            inv = stat[:, 24:30].rearrange("p (b c) -> p b c", b=2)
            for h in range(HEADS):
                n, b0 = HEADS * a + h, 2 * (h % 2)
                units = ((ps[b0][:, 0:128], 0, 128), (ps[b0][:, 128:512], 128, 512), (ps[b0 + 1][:, 0:384], 512, 896))
                dve.wait_ge(sem("scores"), n + 1)
                for u, (src, lo, hi) in enumerate(units):
                    last = V.tensor_reduce(mx[:, h % 2, u:u + 1], src, AX.X, ALU.max)
                step(last)
                V.tensor_scalar(mx[:, 2 + h % 2, :], mx[:, h % 2, :], -float(HD) ** -0.5, None, ALU.mult).then_inc(sem("neg_max"), 1)
                dve.wait_ge(sem("prob"), 3 * n + 3)
                step(V.reciprocal(inv[:, h % 2, :], den[:, h % 2, :]))
                for u, (src, lo, hi) in enumerate(units):
                    last = V.tensor_scalar(prob[:, h % 2, lo:hi], prob[:, h % 2, lo:hi], inv[:, h % 2, u:u + 1], None, ALU.mult)
                last.then_inc(sem("prob_norm"), 1)

        def pool(l):
            dve.wait_ge(sem("pool_pads"), 1)
            dve.wait_ge(sem("hT_dve"), KD // 2 * (2 * l + 1))
            dve.wait_ge(sem("hT_act"), KD // 2 * (2 * l + 1))
            dve.wait_ge(sem("count_landed"), 16)
            for g, win in enumerate(WINDOWS):
                src = hp[:, 2 * g:2 * g + 2, :]
                bufs, m, lo, hi = (win_a, win_b), 1, 0, PW
                while m < win:
                    a, b = (1, 0) if m == 1 else (m // 2, m // 2)
                    lo, hi = lo + a, hi - b
                    dst = bufs[0][:]
                    step(V.tensor_tensor(dst[:, :, lo:hi], src[:, :, lo - a:hi - a], src[:, :, lo + b:hi + b], ALU.add))
                    src, bufs, m = dst, bufs[::-1], 2 * m
                dst = bufs[0][:]
                step(V.tensor_tensor(dst[:, :, PAD:PW - PAD], src[:, :, PAD:PW - PAD],
                                     icnt[:, g:g + 1, PAD:PW - PAD].broadcast_to([128, 2, PW - 2 * PAD]), ALU.mult))
                V.tensor_tensor(uT[:, 2 * g:2 * g + 2, PAD:PW - PAD], dst[:, :, PAD:PW - PAD],
                                hp[:, 2 * g:2 * g + 2, PAD:PW - PAD], ALU.subtract).then_inc(sem("pool_u"), 1)
                dve.wait_ge(sem("pool_u"), g + 1)

        def decay_tables():
            dve.wait_ge(sem("ret_const"), 48)
            z = rsm[:, 0:16]
            neg, e1, w, w2, acc, lg = (rsm[:, 16 * i:16 * i + 16] for i in range(1, 7))
            step(V.tensor_scalar(neg, z, -1.0, None, ALU.mult))
            V.tensor_tensor(neg, z, neg, ALU.min).then_inc(sem("decay_in"), 1)
            dve.wait_ge(sem("decay_exp"), 1)
            step(V.tensor_scalar(w, e1, 2.0, None, ALU.add))
            step(V.reciprocal(w, w))
            step(V.tensor_tensor(w, w, e1, ALU.mult))
            step(V.tensor_tensor(w2, w, w, ALU.mult))
            step(V.tensor_scalar(acc, w2, 1.0 / 17, 1.0 / 15, ALU.mult, ALU.add))
            for d in (13, 11, 9, 7, 5, 3, 1):
                step(V.tensor_tensor(acc, acc, w2, ALU.mult))
                step(V.tensor_scalar(acc, acc, 1.0 / d, None, ALU.add))
            step(V.tensor_tensor(acc, acc, w, ALU.mult))
            step(V.tensor_scalar(lg, z, 0.0, None, ALU.min))
            V.scalar_tensor_tensor(lg, acc, -2.0, lg, ALU.mult, ALU.add).then_inc(sem("log_decay"), 1)
            for h in range(RH):
                dve.wait_ge(sem("mask_exp"), 2 * h + 2)
                step(V.tensor_tensor(rMT[:, h, :], rMT[:, h, :], kret[:, 128:256], ALU.mult))
                step(V.tensor_tensor(rof[:, h % 2, 0:128], rof[:, h % 2, 0:128], kret[:, 384:512], ALU.mult))
                V.tensor_tensor(rMT[:, h, :], rMT[:, h, :], rof[:, h % 2, 0:128], ALU.add).then_inc(sem("mask_done"), 1)

        def retention(l):
            decay_tables()
            dve.wait_ge(sem("mask_exp"), 2 * RH + 1)
            dve.wait_ge(sem("mask_done"), RH)
            with dve.Fori(0, RH) as h:
                step.enter(h, 5)
                dve.wait_ge(sem("ret_qkv"), h + 1)
                V.tensor_copy(rqkv[:, 1, :], ps[1][:]).then_inc(sem("ret_in_sb"), 1)
                atleast(dve, "ret_in_sb", 3 * h + 3)
                for n, (t, d) in enumerate(((0, 0), (0, 1), (1, 0), (2, 1))):
                    last = V.tensor_scalar(rkd[:, n, :], rk[:, t, :], rsm[:, ds(112 + 8 * d + h, 1)], float(RK) ** -0.5,
                                           ALU.mult, ALU.mult)
                last.then_inc(sem("ret_kd"), 1)
                dve.wait_ge(sem("ret_T_ps"), h + 1)
                V.tensor_copy(rqT[:], ps[5][:, 0:T]).then_inc(sem("ret_T_sb"), 1)
                V.tensor_tensor(rqf[:].rearrange("p t i -> p t i"), ps[5][:, 128:T].rearrange("p (t i) -> p t i", t=2),
                                rdf[:, ds(h, 1), :].broadcast_to([128, 2, 128]), ALU.mult).then_inc(sem("ret_T_sb"), 1)
                V.tensor_tensor(rqb[:], ps[5][:, 128:T].rearrange("p (t i) -> p t i", t=2),
                                rdb[:, ds(h, 1), :].broadcast_to([128, 2, 128]), ALU.mult).then_inc(sem("ret_T_sb"), 1)
                dve.wait_ge(sem("ret_S_ps"), h + 1)
                V.tensor_tensor(rST[:], ps[7][:, 0:T].rearrange("p (t i) -> p t i", t=TILES),
                                rMT[:, ds(h, 1), :].broadcast_to([128, TILES, 128]), ALU.mult).then_inc(sem("ret_S_sb"), 1)
                dve.wait_ge(sem("ret_U_ps"), h + 1)
                dve.wait_ge(sem("state_in"), 16 * h + 16)
                V.scalar_tensor_tensor(rs1[:, 0, :], rs0[:, 0, :], rsm[:, ds(128 + h, 1)], ps[6][:, 0:256], ALU.mult, ALU.add)
                V.scalar_tensor_tensor(rs1[:, 1, :], rs0[:, 1, :], rsm[:, ds(136 + h, 1)], ps[6][:, 256:512], ALU.mult, ALU.add)\
                    .then_inc(sem("ret_mid"), 1)
                atleast(dve, "ret_O_ps", h + 1)
                outs = (ps[7][:, 0:256], ps[7][:, 256:512], ps[5][:, 0:256])
                bst, agg = rsm[:, 144:162], rsm[:, 164:170]
                for t in range(TILES):
                    last = V.bn_stats(bst[:, 6 * t:6 * t + 6], outs[t])
                step(last)
                atleast(dve, "ret_gate_sb", h + 1)
                V.tensor_tensor(rg[:], rg[:], rnorm[:, ds(h, 1), :].broadcast_to([128, TILES, RV]), ALU.mult)
                for t in range(TILES):
                    last = V.bn_aggr(agg[:, 2 * t:2 * t + 2], bst[:, 6 * t:6 * t + 6])
                step(last)
                V.tensor_scalar(rsm[:, 172:175], agg.rearrange("p (t c) -> p t c", c=2)[:, :, 1], EPS, None, ALU.add)\
                    .then_inc(sem("ret_var"), 1)
                dve.wait_ge(sem("ret_rstd"), h + 1)
                for t in range(TILES):
                    step(V.tensor_scalar(rof[:, t, :], outs[t], agg[:, 2 * t:2 * t + 1], rsm[:, 176 + t:177 + t],
                                         ALU.subtract, ALU.mult))
                V.tensor_tensor(rof[:], rof[:], rg[:], ALU.mult).then_inc(sem("ret_y"), 1)
            step.leave(RH)

        def pick(out, vals, mx, scratch):
            b = lambda a: a.unsqueeze(2).broadcast_to([128, TILES, 4])
            step(V.tensor_tensor(scratch, vals, b(mx), ALU.is_equal))
            step(V.tensor_tensor(scratch, scratch, tie.unsqueeze(1).broadcast_to([128, TILES, 4]), ALU.mult))
            step(V.tensor_reduce(scol, scratch, AX.X, ALU.max))
            step(V.tensor_tensor(out, scratch, b(scol), ALU.is_equal))

        scol = rt[:, 424:427]

        def route(l):
            g3 = lambda o, n: rt[:, o:o + 3 * n].rearrange("p (t e) -> p t e", t=TILES)
            lg, asg, gts, rk16 = g3(0, 20), g3(96, 16), g3(144, 16), g3(192, 16)
            gmax, ohg, scr, les = rt[:, 240:243], g3(243, 4), g3(255, 4), g3(267, 4)
            prod = rt[:, 280:328].rearrange("p (t g e) -> p t g e", t=TILES, g=4)
            m1, m2, oh1, oh2, les2 = rt[:, 328:331], rt[:, 331:334], g3(334, 4), g3(346, 4), g3(358, 4)
            ein, eout = g3(370, 5), g3(385, 5)
            den, w1, w2 = rt[:, 400:403], rt[:, 403:406], rt[:, 406:409]
            cmax, over, nx = rt[:, 409:410], rt[:, 410:410 + PASSES], rt[:, 420:421]
            b4 = lambda a: a.unsqueeze(2).broadcast_to([128, TILES, 4])
            dve.wait_ge(sem("logits"), l + 1)
            dve.wait_ge(sem("router_landed"), 64 * DEPTH)
            step(V.tensor_tensor(lg, ps[2][:, 0:60].rearrange("p (t e) -> p t e", t=TILES),
                                 rb[:, l:l + 1, :].broadcast_to([128, TILES, 20]), ALU.add))
            step(V.tensor_reduce(gmax, lg[:, :, 0:4], AX.X, ALU.max))
            pick(ohg, lg[:, :, 0:4], gmax, scr)
            for t in range(TILES):
                last = V.tensor_tensor(prod[:, t], lg[:, t, 4:20].rearrange("p (g e) -> p g e", g=4),
                                       ohg[:, t, :].unsqueeze(2).broadcast_to([128, 4, 4]), ALU.mult)
            step(last)
            for t in range(TILES):
                last = V.tensor_reduce(les[:, t, :], prod[:, t].rearrange("p g e -> p e g"), AX.X, ALU.add)
            step(last)
            step(V.tensor_reduce(m1, les, AX.X, ALU.max))
            pick(oh1, les, m1, scr)
            step(V.scalar_tensor_tensor(les2, oh1, -1e30, les, ALU.mult, ALU.add))
            step(V.tensor_reduce(m2, les2, AX.X, ALU.max))
            pick(oh2, les2, m2, scr)
            step(V.tensor_tensor(asg[:, :, 0:4], oh1, oh2, ALU.add))
            step(V.tensor_copy(les2, asg[:, :, 0:4]))
            for t in range(TILES):
                last = V.tensor_tensor(asg[:, t, :].rearrange("p (g e) -> p g e", g=4),
                                       ohg[:, t, :].unsqueeze(2).broadcast_to([128, 4, 4]),
                                       les2[:, t, :].unsqueeze(1).broadcast_to([128, 4, 4]), ALU.mult)
            last.then_inc(sem("assigned"), 1)
            step(V.tensor_tensor(ein[:, :, 0:4], lg[:, :, 0:4], b4(gmax), ALU.subtract))
            V.tensor_tensor(ein[:, :, 4], m2, m1, ALU.subtract).then_inc(sem("route_exp_in"), 1)
            dve.wait_ge(sem("route_exp"), l + 1)
            step(V.tensor_reduce(den, eout[:, :, 0:4], AX.X, ALU.add))
            step(V.tensor_scalar(w2, eout[:, :, 4], 1.0, None, ALU.add))
            step(V.tensor_tensor(den, den, w2, ALU.mult))
            step(V.reciprocal(w1, den))
            step(V.tensor_tensor(w2, w1, eout[:, :, 4], ALU.mult))
            step(V.tensor_tensor(les, oh1, b4(w1), ALU.mult))
            step(V.tensor_tensor(les2, oh2, b4(w2), ALU.mult))
            step(V.tensor_tensor(les, les, les2, ALU.add))
            for t in range(TILES):
                last = V.tensor_tensor(gts[:, t, :].rearrange("p (g e) -> p g e", g=4),
                                       ohg[:, t, :].unsqueeze(2).broadcast_to([128, 4, 4]),
                                       les[:, t, :].unsqueeze(1).broadcast_to([128, 4, 4]), ALU.mult)
            step(last)
            step(V.tensor_copy(gates_r[:, :, :, 0], gts))
            step(V.tensor_tensor(gates_r[:, :, :, 1], gts, gates_r[:, :, :, 0].bitcast(F), ALU.subtract))
            dve.wait_ge(sem("ranks"), l + 1)
            step(V.tensor_scalar(rk16, ps[3][:, 0:48].rearrange("p (t e) -> p t e", t=TILES), 1.0, None, ALU.add))
            step(V.tensor_tensor(rk16, rk16, asg, ALU.mult))
            step(V.tensor_scalar(rankm[:], rk16, -1.0, None, ALU.add))
            step(V.tensor_reduce(cmax, ps[3][:, 64:80], AX.X, ALU.max))
            step(V.tensor_tensor(over, cmax.broadcast_to([128, PASSES]), caps, ALU.is_gt))
            step(V.tensor_reduce(nx, over, AX.X, ALU.add))
            V.tensor_copy(extra[:, l:l + 1], nx).then_inc(sem("routed"), 1)
            dve.wait_ge(sem("routed"), l + 1)

        def token_major(l):
            if l % 3 == 0:
                dve.wait_ge(sem("cache_stored"), 32 * (l // 3 + 1))
            elif l % 3 == 2:
                atleast(dve, "state_stored", 16 * RH)
            for c in range(2):
                dve.wait_ge(sem("mod_ps"), 2 * l + c + 1)
                for t in range(TILES):
                    if COND[t] != c:
                        continue
                    for half in range(2):
                        o = slice(half * 512, half * 512 + 512)
                        last = V.tensor_tensor(htok[:, t, o], xn[:, t, o], ps[4 + half][:], ALU.mult)
                    step(last)
                    for half in range(2):
                        o = slice(half * 512, half * 512 + 512)
                        last = V.tensor_tensor(htok[:, t, o], htok[:, t, o], ps[6 + half][:], ALU.add)
                    last.then_inc(sem("h_tok"), 1)

        def experts(z, it, g, ada, order, shifts=0):
            def place_tokens(j):
                q = it * PER + j
                if z == "o":
                    dve.wait_ge(sem("rank_shift"), shifts)
                atleast(dve, z + "_PT", q - 1)
                for t in range(TILES):
                    last = V.tensor_scalar(Pm[:, j % 2, t, :], iota[:, 0:CAP], rankm[:, t, ds(g * PER + j, 1)], None, ALU.is_equal)
                last.then_inc(sem(z + "_P"), 1)

            def gathered(j):
                q = it * PER + j
                atleast(dve, z + "_gateup", q - 1)
                dve.wait_ge(sem(z + "_gather"), q + 1)
                V.tensor_copy(hg[:, j % 2, 4:8, :], ps[1][:].rearrange("p (k s) -> p k s", k=4)[:, :, 0:CAP])\
                    .then_inc(sem(z + "_hg_dve"), 1)

            for j in range(PER):
                q = it * PER + j
                if j == 0:
                    place_tokens(0)
                    gathered(0)
                if j + 1 < PER:
                    place_tokens(j + 1)
                atleast(dve, z + "_PT_sb", q + 1)
                order(V.tensor_reduce(gsum[0:CAP, 0:1], gslot[0:CAP, j % 2, :], AX.X, ALU.add))
                dve.wait_ge(sem(z + "_silu"), q + 1)
                atleast(dve, z + "_actT", q)
                V.scalar_tensor_tensor(act[0:CAP, :], ps[2][0:CAP, FE:2 * FE], gsum[0:CAP, 0:1], silu[0:CAP, :], ALU.mult, ALU.mult)\
                    .then_inc(sem(z + "_act"), 1)
                if j + 1 < PER:
                    gathered(j + 1)
                if ada is not None:
                    ada_mod(ada[0], ada[1] + g * PER + j, g * PER + j)
                atleast(dve, z + "_scatter", 6 * it)
                for half in range(2):
                    o = slice(half * 512, half * 512 + 512)
                    atleast(dve, z + "_y_hi", 2 * q + half + 1)
                    V.tensor_tensor(ylo[0:CAP, j, o], ps[6 + half][0:CAP, :], yhi[0:CAP, j, o].bitcast(F), ALU.subtract)\
                        .then_inc(sem(z + "_y_lo"), 1)
            for m in range(2 * TILES):
                t, half = m // 2, m % 2
                atleast(dve, z + "_scatter", 6 * it + m + 1)
                atleast(dve, z + "_added", 6 * it + m - 1)
                V.tensor_tensor(tmp[:, m % 2, :], ps[6 + half][:], gate_bc[:, COND[t], half * 512:half * 512 + 512],
                                ALU.mult).then_inc(sem(z + "_term"), 1)

        dve.wait_ge(sem("vT_ps"), 1)
        V.memset(cond32[:], 0.0)
        V.memset(ones[:], 1.0)
        V.tensor_copy(vT[:], ps[0][:, 0:288]).then_inc(sem("vT_sb"), 1)
        dve.wait_ge(sem("vT_sb"), 1)
        with dve.Fori(0, ADA_P) as i:
            ada_mod(0, i, i)
        atleast(dve, "ada_mod", ADA_P)
        passes = []
        pass_order = Order(dve, "dve_pass_step")
        for l in range(depth):
            finish_mods(l)
            norm(l, 0)
            if l % 3 == 0:
                attention(l)
            elif l % 3 == 1:
                pool(l)
            else:
                retention(l)
            residual(l, step)
            norm(l, 1)
            token_major(l)
            route(l)
            dve.wait_ge(sem("gate_bc"), 4 * (2 * l + 2))
            dve.wait_ge(sem("mix_added"), 6 * (l + 1))
            dve.wait_ge(sem("h_lo"), TILES * (l + 1))
            nxt = (l + 1, (l + 1) * ADA_P) if l + 1 < depth else None

            def body(z, it, g, first):
                if z == "m":
                    step.enter(g, PER)
                    experts(z, it, g, nxt, step)
                    step.leave(GROUPS)
                else:
                    pass_order.base, pass_order.n = it * PER, 0
                    experts(z, it, g, None, pass_order, shifted[0])

            shifted = [0]

            def next_ranks(n):
                atleast(dve, "m_added", 6 * GROUPS * (l + 1))
                V.tensor_scalar(rankm[:], rankm[:], float(-CAP), None, ALU.add).then_inc(sem("rank_shift"), 1)
                shifted[0] = n + 1

            expert_passes(dve, body, passes, l, next_ranks)
            if l + 1 < depth:
                atleast(dve, "ada_mod", (l + 2) * ADA_P)
        n = 2 * depth
        mean_square(n)
        dve.wait_ge(sem("rstd"), n + 1)
        dve.wait_ge(sem("normf_ps"), 1)
        for t in range(TILES):
            for half in range(2):
                o = slice(half * 512, half * 512 + 512)
                last = V.scalar_tensor_tensor(ofin[:, t, o], x[:, t, o], rstd[:, t:t + 1], ps[4 + half][:], ALU.mult, ALU.mult)
            last.then_inc(sem("final_ready"), 1)

    @block.scalar
    def _(act_e):
        e = act_e
        step = Order(e, "act_step")

        def sum_squares(n):
            if n == 0:
                e.wait_ge(sem("x_landed"), 32)
            elif n % 2:
                e.wait_ge(sem("mix_added"), 6 * (n // 2 + 1))
            else:
                e.wait_ge(sem("layer_done"), n // 2)
            if n:
                e.wait_ge(sem("msq"), n)
            for t in range(TILES):
                S.activation(xn[:, t, :], x[:, t, :], ACT.Square, accum_out=ssq[:, t:t + 1]).then_inc(sem("ssq"), 1)

        def norm(l, sub):
            n = 2 * l + sub
            sum_squares(n)
            e.wait_ge(sem("rstd"), n + 1)
            e.wait_ge(sem("ssq"), TILES * (n + 1))
            for t in range(TILES):
                S.activation(xn[:, t, :], x[:, t, :], ACT.Copy, scale=rstd[:, t:t + 1]).then_inc(sem("xn_ready"), 1)
            e.wait_ge(sem("mods_ready"), l + 1)
            for k in range(1, KD, 2):
                e.wait_ge(sem("hT_ps"), KD * n + k + 1)
                for c, src in enumerate((ps[k % 4][:, 0:128], ps[k % 4][:, 128:T])):
                    last = S.activation(hT_out(l, sub, k, c), src, ACT.Identity, bias=mod_col(3 * sub, k, c),
                                        scale=mod_col(1 + 3 * sub, k, c))
                last.then_inc(sem("hT_act"), 1)

        def gate(n):
            for c in range(2):
                for half in range(2):
                    e.wait_ge(sem("gate_ps"), 4 * n + 2 * c + half + 1)
                    S.activation(gate_bc[:, c, half * 512:half * 512 + 512], ps[4 + 2 * c + half][:], ACT.Copy)\
                        .then_inc(sem("gate_bc"), 1)

        def ada_copy(idx):
            e.wait_ge(sem("ada_product"), idx + 1)
            atleast(e, "ada_col", idx)
            S.activation(mpan[:], ps[4][:, 0:ADA_N], ACT.Copy).then_inc(sem("ada_evac"), 1)

        def attention(l):
            a = l // 3
            e.dma_start(ckv[:, 0, :], A["cache_k"][0, a].rearrange("s h d -> s (h d)")).then_inc(sem("cache_landed"), 16)
            e.dma_start(ckv[:, 1, :], A["cache_v"][0, a].rearrange("s h d -> s (h d)")).then_inc(sem("cache_landed"), 16)
            e.dma_start(gqk[:, 0:HEADS * HD].rearrange("p (h d) -> p h d", h=HEADS),
                        A["attn_q_norm"][a:a + 1, :].unsqueeze(1).broadcast_to([128, HEADS, HD])).then_inc(sem("attn_landed"), 16)
            e.dma_start(gqk[:, HEADS * HD:].rearrange("p (h d) -> p h d", h=KV),
                        A["attn_k_norm"][a:a + 1, :].unsqueeze(1).broadcast_to([128, KV, HD])).then_inc(sem("attn_landed"), 16)
            e.dma_start(rope[:], A["k_rope"]).then_inc(sem("attn_landed"), 32)
            for i in range(3):
                for t in range(TILES):
                    e.wait_ge(sem("proj_done"), prj_base[l] + 3 * i + t + 1)
                    S.activation(qkv[:, t, i * 512:(i + 1) * 512], ps[(0, 4, 0)[i] + t][:], ACT.Copy).then_inc(sem("qkv_sb"), 1)
            e.wait_ge(sem("qk_ready"), TILES * a + 1)
            e.dma_start(O["new_cache_k"][0, a].rearrange("s h d -> s (h d)"), qkv[:, 0, HEADS * HD:NQK * HD])\
                .then_inc(sem("cache_stored"), 16)
            e.wait_ge(sem("qkv_sb"), 9 * (a + 1))
            e.dma_start(O["new_cache_v"][0, a].rearrange("s h d -> s (h d)"), qkv[:, 0, NQK * HD:])\
                .then_inc(sem("cache_stored"), 16)
            for h in range(NQK):
                e.wait_ge(sem("qkT_ps"), NQK * a + h + 1)
                if h < HEADS:
                    S.activation(qT[:, h, :], ps[h % 4][:, 0:T], ACT.Copy).then_inc(sem("qkT_sb"), 1)
                else:
                    S.activation(kT[:, h - HEADS, 0:128], ps[h % 4][:, 0:128], ACT.Copy)
                    S.activation(kT[:, h - HEADS, 128:256], ps[h % 4][:, 384:512], ACT.Copy)
                    S.activation(kT[:, h - HEADS, 256:512], ps[h % 4][:, 128:384], ACT.Copy).then_inc(sem("qkT_sb"), 1)

            def soft(h):
                n, b0 = HEADS * a + h, 2 * (h % 2)
                units = ((ps[b0][:, 0:128], 0, 128), (ps[b0][:, 128:512], 128, 512), (ps[b0 + 1][:, 0:384], 512, 896))
                e.wait_ge(sem("neg_max"), n + 1)
                if h >= 2:
                    e.wait_ge(sem("probT_ps"), 2 * (n - 1))
                for u, (src, lo, hi) in enumerate(units):
                    S.activation(prob[:, h % 2, lo:hi], src, ACT.Exp, bias=stat[:, 6 + 3 * (h % 2) + u:7 + 3 * (h % 2) + u],
                                 scale=float(HD) ** -0.5, accum_out=stat[:, 12 + 3 * (h % 2) + u:13 + 3 * (h % 2) + u])\
                        .then_inc(sem("prob"), 1)

            def out_side(h):
                n = HEADS * a + h
                if h >= 2:
                    e.wait_ge(sem("oT_ps"), n - 1)
                e.wait_ge(sem("probT_ps"), 2 * n + 1)
                S.activation(probT[:, h % 2, 0:512], ps[4][:], ACT.Copy).then_inc(sem("probT_sb"), 1)
                e.wait_ge(sem("probT_ps"), 2 * n + 2)
                S.activation(probT[:, h % 2, 512:896], ps[5][:, 0:384], ACT.Copy).then_inc(sem("probT_sb"), 1)
                e.wait_ge(sem("oT_ps"), n + 1)
                S.activation(oT[:, h, :], ps[6 + h % 2][:, 0:T], ACT.Copy).then_inc(sem("oT_sb"), 1)

            soft(0)
            for h in range(HEADS):
                if h + 1 < HEADS:
                    soft(h + 1)
                out_side(h)

        def retention(l):
            kr = A["k_ret"]
            e.dma_start(kret[:], kr).then_inc(sem("ret_const"), 16)
            e.dma_start(rsm[:, 0:16], A["ret_decay_logit"].rearrange("l a h -> l (a h)").broadcast_to([128, 16])).then_inc(sem("ret_const"), 16)
            e.dma_start(rnorm[:].rearrange("p h v -> p (h v)"), A["ret_norm"].broadcast_to([128, RH * RV])).then_inc(sem("ret_const"), 16)
            e.wait_ge(sem("decay_in"), 1)
            S.activation(rsm[:, 32:48], rsm[:, 16:32], ACT.Exp).then_inc(sem("decay_exp"), 1)
            e.wait_ge(sem("log_decay"), 1)
            lgc = lambda d, h: rsm[:, 96 + 8 * d + h:97 + 8 * d + h]
            for h in range(RH):
                if h >= 2:
                    e.wait_ge(sem("mask_done"), h - 1)
                S.activation(rMT[:, h, :], kret[:, 0:128], ACT.Exp, scale=lgc(0, h)).then_inc(sem("mask_exp"), 1)
                S.activation(rof[:, h % 2, 0:128], kret[:, 256:384], ACT.Exp, scale=lgc(1, h)).then_inc(sem("mask_exp"), 1)
                S.activation(rdf[:, h, :], kret[:, 512:640], ACT.Exp, scale=lgc(0, h))
                S.activation(rdb[:, h, :], kret[:, 640:768], ACT.Exp, scale=lgc(1, h))
            S.activation(rsm[:, 112:120], rsm[:, 96:104], ACT.Exp, scale=kret[:, 768:769])
            S.activation(rsm[:, 120:128], rsm[:, 104:112], ACT.Exp, scale=kret[:, 769:770])
            S.activation(rsm[:, 128:144], rsm[:, 96:112], ACT.Exp, scale=128.0).then_inc(sem("mask_exp"), 1)
            st_in, st_out = A["state_ret"], O["new_state_ret"]
            e.wait_ge(sem("mask_done"), RH)
            with e.Fori(0, RH) as h:
                atleast(e, "ret_O_ps", h)
                e.dma_start(rs0[:], st_in[0, 0, :, ds(h, 1)].rearrange("a o k v -> k (a o) v")).then_inc(sem("state_in"), 16)
                e.wait_ge(sem("ret_qkv"), h + 1)
                for t in (0, 2):
                    S.activation(rqkv[:, t, :], ps[t][:], ACT.Copy).then_inc(sem("ret_in_sb"), 1)
                e.wait_ge(sem("ret_gate"), h + 1)
                S.activation(rg[:, 0:2, :], ps[3][:].rearrange("p (t v) -> p t v", t=2), ACT.Silu)
                S.activation(rg[:, 2, :], ps[4][:, 0:256], ACT.Silu).then_inc(sem("ret_gate_sb"), 1)
                e.wait_ge(sem("ret_T_ps"), h + 1)
                S.activation(rkT[:], ps[6][:, 0:T], ACT.Copy).then_inc(sem("ret_T_sb"), 1)
                e.wait_ge(sem("ret_U_ps"), h + 1)
                atleast(e, "state_stored", 16 * h)
                S.activation(rso[:], ps[5][:].rearrange("p (a v) -> p a v", a=2), ACT.Copy).then_inc(sem("ret_state_out"), 1)
                e.wait_ge(sem("ret_state_out"), h + 1)
                e.dma_start(st_out[0, 0, :, ds(h, 1)].rearrange("a o k v -> k (a o) v"), rso[:]).then_inc(sem("state_stored"), 16)
                for c in range(2):
                    e.wait_ge(sem("ret_yT_ps"), 2 * h + c + 1)
                    S.activation((yTe, yTo)[c][:, ds(h, 1), :].rearrange("p o t -> p (o t)"), ps[6 - c][:, 0:T], ACT.Copy)\
                        .then_inc(sem("ret_yT_sb"), 1)

        def route(l):
            n = 2 * l + 1
            for t in range(TILES):
                e.wait_ge(sem("h_tok"), TILES * l + t + 1)
                S.activation(hhi[:, t, :], htok[:, t, :], ACT.Copy).then_inc(sem("h_hi"), 1)
            gate(n)
            e.wait_ge(sem("route_exp_in"), l + 1)
            S.activation(rt[:, 385:400], rt[:, 370:385], ACT.Exp).then_inc(sem("route_exp"), 1)

        def experts(z, it, g, ada):
            def gathered(j):
                q = it * PER + j
                atleast(e, z + "_gateup", q - 1)
                e.wait_ge(sem(z + "_gather"), q + 1)
                S.activation(hg[:, j % 2, 0:4, :], ps[0][:].rearrange("p (k s) -> p k s", k=4)[:, :, 0:CAP], ACT.Copy)\
                    .then_inc(sem(z + "_hg_act"), 1)
                atleast(e, z + "_PT", q + 1)
                if j == 0:
                    atleast(e, z + "_scatter", 6 * it)
                S.activation(PT[0:CAP, j, :], ps[5][0:CAP, 0:T], ACT.Copy)
                atleast(e, z + "_act", q - 1)
                S.activation(gslot[0:CAP, j % 2, :], ps[5][0:CAP, T:T + 2], ACT.Copy).then_inc(sem(z + "_PT_sb"), 1)

            for j in range(PER):
                q = it * PER + j
                if j == 0:
                    gathered(0)
                atleast(e, z + "_gateup", q + 1)
                atleast(e, z + "_act", q)
                S.activation(silu[0:CAP, :], ps[2][0:CAP, 0:FE], ACT.Silu).then_inc(sem(z + "_silu"), 1)
                if j + 1 < PER:
                    gathered(j + 1)
                if ada is not None:
                    ada_copy(ada + g * PER + j)
                atleast(e, z + "_actT", q + 1)
                atleast(e, z + "_down", 2 * q)
                S.activation(actT[:], ps[3][:, 0:256].rearrange("p (c s) -> p c s", c=2)[:, :, 0:CAP], ACT.Copy)\
                    .then_inc(sem(z + "_actT_sb"), 1)
                for half in range(2):
                    atleast(e, z + "_down", 2 * q + half + 1)
                    S.activation(yhi[0:CAP, j, half * 512:half * 512 + 512], ps[6 + half][0:CAP, :], ACT.Copy)\
                        .then_inc(sem(z + "_y_hi"), 1)

        for l in range(DEPTH):
            e.dma_start(wr[:, l, :, 0:4], A["moe_w_router_g"][l].rearrange("(k p) g -> p k g", p=128)).then_inc(sem("router_landed"), 16)
            e.dma_start(wr[:, l, :, 4:20], A["moe_w_router_e"][l].rearrange("(k p) g -> p k g", p=128)).then_inc(sem("router_landed"), 16)
            e.dma_start(rb[:, l, 0:4], A["moe_b_router_g"][l:l + 1, :].broadcast_to([128, 4])).then_inc(sem("router_landed"), 16)
            e.dma_start(rb[:, l, 4:20], A["moe_b_router_e"][l:l + 1, :].broadcast_to([128, 16])).then_inc(sem("router_landed"), 16)
        e.wait_ge(sem("vT_sb"), 1)
        S.activation(cond32[:, :, 0], vT[:, 80:88], ACT.Silu)
        S.activation(cond32[:, :, 1], vT[:, 88:96], ACT.Silu).then_inc(sem("cond_ready"), 1)
        with e.Fori(0, ADA_P) as i:
            ada_copy(i)
        passes = []
        for l in range(depth):
            norm(l, 0)
            gate(2 * l)
            if l % 3 == 0:
                attention(l)
            elif l % 3 == 1:
                e.dma_start(icnt[:], A["k_cnt"].rearrange("(o g) w -> o g w", o=1).broadcast_to([128, 4, PW])).then_inc(sem("count_landed"), 16)
            else:
                retention(l)
            norm(l, 1)
            route(l)
            e.wait_ge(sem("routed"), l + 1)
            nxt = (l + 1) * ADA_P if l + 1 < depth else None
            expert_passes(e, lambda z, it, g, first: experts(z, it, g, nxt if first else None), passes, l)
        sum_squares(2 * depth)

    @block.gpsimd
    def _(pool):
        for name, c in CREDIT.items():
            pool.sem_inc(sem(name), c)

        def inverse_root(n):
            pool.wait_ge(sem("msq"), n + 1)
            G.tensor_tensor(rstd[:, 0:3], msq[:, 0:3], hpow[:, 0:3], ALU.pow).then_inc(sem("rstd"), 1)

        def experts(z, it):
            for m in range(2 * TILES):
                t, half = m // 2, m % 2
                o = slice(half * 512, half * 512 + 512)
                atleast(pool, z + "_term", 6 * it + m + 1)
                G.tensor_tensor(x[:, t, o], x[:, t, o], tmp[:, m % 2, :], ALU.add).then_inc(sem(z + "_added"), 1)

        passes = []
        pool.wait_ge(sem("const_landed"), 16)
        for l in range(depth):
            a = l // 3
            inverse_root(2 * l)
            if l % 3 == 0:
                pool.wait_ge(sem("qk_ms"), a + 1)
                G.tensor_tensor(stat[:, 64:94], stat[:, 32:62], hpow[:, 0:30], ALU.pow).then_inc(sem("qk_rstd"), 1)
            elif l % 3 == 1:
                for lo, hi in ((0, POFF[0]), (POFF[0] + SEQ, POFF[1]), (POFF[1] + DEC, PW)):
                    last = G.memset(hp[:, :, lo:hi], 0.0)
                last.then_inc(sem("pool_pads"), 1)
            else:
                with pool.Fori(0, RH) as h:
                    pool.wait_ge(sem("ret_var"), h + 1)
                    G.tensor_tensor(rsm[:, 176:179], rsm[:, 172:175], hpow[:, 0:3], ALU.pow).then_inc(sem("ret_rstd"), 1)
            for m in range(2 * TILES):
                half, t = m // TILES, m % TILES
                o = slice(half * 512, half * 512 + 512)
                pool.wait_ge(sem("mix_term"), 6 * l + m + 1)
                G.tensor_tensor(x[:, t, o], x[:, t, o], tmp[:, m % 2, :], ALU.add).then_inc(sem("mix_added"), 1)
            inverse_root(2 * l + 1)
            for t in range(TILES):
                pool.wait_ge(sem("h_hi"), TILES * l + t + 1)
                G.tensor_tensor(hlo[:, t, :], htok[:, t, :], hhi[:, t, :].bitcast(F), ALU.subtract).then_inc(sem("h_lo"), 1)
            pool.wait_ge(sem("routed"), l + 1)
            expert_passes(pool, lambda z, it, g, first: experts(z, it), passes, l)
            pool.drain().then_inc(sem("layer_done"), 1)
        inverse_root(2 * depth)

    ctx.close()


_INS = ["x_prompt", "x_sample", "cache_k", "cache_v", "state_ret", "w_ada", "b_ada", "attn_w_qkv", "attn_q_norm",
        "attn_k_norm", "attn_w_o", "pool_w", "ret_w_in", "ret_decay_logit", "ret_norm", "ret_w_out",
        "moe_w_router_g", "moe_b_router_g", "moe_w_router_e", "moe_b_router_e", "moe_w_gate", "moe_w_up", "moe_w_down"]
_OUTS = {"y_prompt": (1, SEQ, D), "y_sample": (1, DEC, D), "new_cache_k": (1, 2, SEQ, KV, HD),
         "new_cache_v": (1, 2, SEQ, KV, HD), "new_state_ret": (1, 1, 2, RH, RK, RV)}


def kernel(**inputs):
    import concourse.bacc as bacc
    from concourse import mybir
    from concourse.bass_utils import run_bass_kernel_spmd as run

    nc = bacc.Bacc("TRN2", target_bir_lowering=False, num_devices=1)
    arrays = {n: np.ascontiguousarray(inputs[n]) for n in _INS}
    arrays["vectors"] = np.concatenate([np.asarray(inputs[n]).reshape(-1, 128) for n in
                                        ("norm1", "norm2", "pool_scale", "norm_f", "c_ctx", "c")])
    arrays.update(shape_constants())
    feeds, A, O = {}, {}, {}
    for n, a in arrays.items():
        feeds["in_" + n] = a
        A[n] = nc.dram_tensor("in_" + n, a.shape, mybir.dt.from_np(a.dtype), kind="ExternalInput").ap()
    for n, shape in _OUTS.items():
        O[n] = nc.dram_tensor("out_" + n, shape, mybir.dt.float32, kind="ExternalOutput").ap()
    build_trunk(nc, A, O)
    r = run(nc, [feeds], core_ids=[0])
    return tuple(r.results[0]["out_" + n] for n in _OUTS)
```

```python
from contextlib import ExitStack

import numpy as np

D = 1024
KD = D // 128
SEQ, DEC, PAST = 128, 256, 128
TILES = (SEQ + DEC) // 128
T = TILES * 128
COND = (0, 1, 1)
DEPTH = 4
HEADS, KV, HD = 8, 2, 128
NQKV = (HEADS + 2 * KV) * HD
NQK = HEADS + KV
RH, RK, RV = 8, 128, 256
GROUPS, PER = 4, 4
EXPERTS = GROUPS * PER
FE = 256
CAP = 128
PASSES = -(-T // CAP)
EPS = 1e-6
ADA_N = 384
ADA_P = 6 * D // ADA_N
PAD = 8
PW = PAD + SEQ + PAD + PAD + DEC + PAD
POFF = (PAD, 3 * PAD + SEQ, 3 * PAD + SEQ + 128)
WINDOWS = (2, 4, 8, 16)


def shape_constants():
    p = np.arange(128, dtype=np.float32)
    ident = np.eye(128, dtype=np.float32)
    tri = (p[:, None] < p[None, :]).astype(np.float32)
    iota = np.broadcast_to(p, (128, 128))
    sel = (p[:, None] % 32 == np.arange(2)[None, :]).astype(np.float32)
    tie = np.broadcast_to(np.float32(4) - np.arange(4, dtype=np.float32), (128, 4))
    caps = np.broadcast_to(CAP * np.arange(1, PASSES + 1, dtype=np.float32), (128, PASSES))
    halfpow = np.full((128, 32), -0.5, np.float32)
    quad = (p[:, None] % 32 == np.arange(32)[None, :]).astype(np.float32)
    base = np.concatenate([ident, tri, iota, sel, tie, caps, halfpow, quad], axis=1).astype(np.float32)
    j, i = p[:, None], p[None, :]
    scale = np.float32(RK ** -0.5)
    ret = np.concatenate([np.maximum(i - j, 0), (i >= j) * scale, np.maximum(j - i, 0), (j >= i) * scale,
                          np.broadcast_to(i + 1, (128, 128)), np.broadcast_to(128 - i, (128, 128)),
                          127 - j, j], axis=1).astype(np.float32)
    nf = HD // 4
    inv = np.float32(10000.0) ** (-np.arange(nf, dtype=np.float32) / np.float32(nf))
    t = np.arange(DEC)
    ang = np.stack([(t // 64).astype(np.float32)[:, None] * inv, (t % 64).astype(np.float32)[:, None] * inv], 1)
    cos, sin = np.cos(ang).astype(np.float32), np.sin(ang).astype(np.float32)
    rope = np.stack([np.stack([cos, cos], 2), np.stack([-sin, sin], 2)], 1).reshape(2, 128, 2 * 128)
    rope = np.ascontiguousarray(rope.transpose(1, 0, 2))
    cnt = np.ones((4, PW), np.float32)
    for g, win in enumerate(WINDOWS):
        for off, n in ((POFF[0], SEQ), (POFF[1], DEC)):
            s = np.arange(n)
            cnt[g, off:off + n] = np.clip(s + win - win // 2, 0, n) - np.clip(s - win // 2, 0, n)
    return {"k_base": base, "k_ret": ret, "k_rope": rope, "k_cnt": (np.float32(1) / cnt)}


def build_trunk(nc, A, O, depth=DEPTH):
    import concourse.bass as bass
    from concourse import mybir

    F, R, I32 = mybir.dt.float32, mybir.dt.float32r, mybir.dt.int32
    ALU, ACT, AX = mybir.AluOpType, mybir.ActivationFunctionType, mybir.AxisListType
    ds = bass.ds
    PE, V, S, G = nc.tensor, nc.vector, nc.scalar, nc.gpsimd

    size = lambda shape: 4 * int(np.prod(shape))
    top = [-(-nc.sbuf_base // 64) * 64]

    def place(name, shape, dt=F, at=None):
        off = top[0] if at is None else at
        if at is None:
            top[0] = off + -(-size(shape) // 32) * 32
        return nc.alloc_sbuf_tensor_at(name, [128] + list(shape), dt, offset=off), off + -(-size(shape) // 32) * 32

    def keep(name, shape, dt=F):
        return place(name, shape, dt)[0]

    x = keep("x", [TILES, D])
    gu_ring = [keep(f"gate_up_weights{i}", [KD, 2 * FE]) for i in range(2)]
    dn_at = top[0]
    dn_ring = [keep(f"down_weights{i}", [2, D]) for i in range(2)]
    panel = [keep(f"panel{i}", [KD, 512]) for i in range(2)]
    gate_bc = keep("gate_bc", [2, D])
    tmp = keep("residual_term", [2, 512])
    mraw = keep("ada_raw", [48, 2])
    mods = keep("mods", [48, 2])
    kb = keep("const_base", [3 * 128 + 2 + 4 + PASSES + 64])
    vecs = keep("vector_rows", [3, 128])
    vT = keep("vectors", [96 + 192])
    cond32 = keep("cond_columns", [KD, 32])
    wr = keep("router_weights", [DEPTH, KD, 32])
    rb = keep("router_bias", [DEPTH, 20])
    mpan = keep("ada_panel_rows", [ADA_N])
    ssq = keep("sum_squares", [4])
    msq = keep("mean_squares", [4])
    rstd = keep("rstd", [4])
    rankm = keep("rank_in_expert", [TILES, EXPERTS + 1])
    gates_r = keep("gates_pair", [TILES, EXPERTS + 1, 2], R)
    extra = keep("extra_passes", [4], I32)
    ones = keep("ones", [128])
    mod_at = top[0]
    mod_bc = keep("mod_bc", [4, D])
    lpart = keep("logit_parts", [T])
    rt = keep("route_scratch", [480])
    base = top[0]

    def region(*items, start=base):
        out, at = [], start
        for name, shape, *dt in items:
            t, at = place(name, shape, *(dt or [F]), at=at)
            out.append(t)
        assert at <= nc.sbuf_usable_end, (at, nc.sbuf_usable_end)
        return out, at

    (xn, hT), mix0 = region(("xn", [TILES, D]), ("hT", [KD, T]))
    (qkv, kT, ckv, rope, gqk, stat), att0 = region(
        ("qkv", [TILES, NQKV]), ("kT", [KV, 512]), ("cache_rows", [2, KV * HD]), ("rope_tab", [2, 256]),
        ("qk_gain", [NQK * HD]), ("attn_stat", [96]), start=mix0)
    (prob, probT), _ = region(("prob", [2, 896]), ("probT", [2, 896]), start=att0)
    (sqv, ropet), _ = region(("qk_sq", [NQK * HD]), ("rope_t", [NQK * HD]), start=att0)
    (oT, qT), _ = region(("oT", [HEADS, T]), ("qT", [HEADS, T]))
    (hp, win_a, win_b, uT, icnt), _ = region(("h_padded", [KD, PW]), ("win_a", [2, PW]), ("win_b", [2, PW]),
                                            ("pool_u", [KD, PW]), ("inv_count", [4, PW]), start=mix0)
    (yTo, rqkv, rg, rkd, rqT, rkT, rqf, rqb, rST, rs0, rs1, rso, rof, rMT, kret,
     rsm), _ = region(
        ("yT_odd", [RH, T]), ("ret_qkv_sb", [TILES, 512]), ("ret_gate", [TILES, RV]), ("ret_k_decayed", [4, RK]), ("ret_qT", [T]), ("ret_kT", [T]),
        ("ret_q_fwd", [2, 128]), ("ret_q_bwd", [2, 128]), ("ret_scoresT", [TILES, 128]),
        ("ret_state_in", [2, RV]), ("ret_state_mid", [2, RV]), ("ret_state_out", [2, RV]),
        ("ret_o", [TILES, RV]), ("ret_mask", [RH, 128]), ("k_ret_sb", [6 * 128 + 2]), ("ret_small", [192]), start=mix0)
    rq, rk, rv = rqkv[:, :, 0:RK], rqkv[:, :, RK:2 * RK], rqkv[:, :, 2 * RK:512]
    (rnorm, rdf, rdb), dn_end = region(("ret_gain", [RH, RV]), ("ret_dec_f", [RH, 128]), ("ret_dec_b", [RH, 128]),
                                       start=dn_at)
    assert dn_end <= dn_at + 2 * size([2, D])
    (yTe,), _ = region(("yT_even", [RH, T]))
    (yhi, ylo, PT), moe0 = region(("y_hi", [PER, D], R), ("y_lo", [PER, D], R), ("PT", [PER, T], R))
    (htok,), _ = region(("h_tok", [TILES, D]), start=mix0)
    assert moe0 - base >= 3 * size([TILES, D])
    (hhi, hlo, Pm, silu, act, actT, gsum, gslot), _ = region(
        ("h_hi", [TILES, D], R), ("h_lo", [TILES, D], R), ("P", [2, TILES, CAP], R),
        ("silu", [FE]), ("act", [FE]), ("actT", [2, CAP]), ("gate_slot", [1]), ("gate_pair", [2, 2]), start=moe0)
    (hgt, hg), hg_end = region(("h_gathered", [D]), ("hT_gathered", [2, KD, CAP]), start=mod_at)
    assert hg_end <= mod_at + size([4, D])
    (ofin,), _ = region(("y_final", [TILES, D]), start=mix0)

    ident, tri, iota = kb[:, 0:128], kb[:, 128:256], kb[:, 256:384]
    sel = kb[:, 384:386]
    tie = kb[:, 386:390]
    caps = kb[:, 390:390 + PASSES]
    hpow = kb[:, 390 + PASSES:422 + PASSES]
    quad = kb[:, 422 + PASSES:454 + PASSES]
    biasT = vT[:, 96:288]

    ps = [nc.alloc_psum_tensor(f"bank{i}", [128, 512], F) for i in range(8)]
    sems = {}

    def sem(name):
        if name not in sems:
            sems[name] = nc.alloc_semaphore(name)
        return sems[name]

    panels = [("ada", 0, i) for i in range(ADA_P)]
    first_panel = {("ada", 0): 0}
    prj_base = {}
    prj = 0
    for l in range(depth):
        kind = l % 3
        first_panel["mix", l] = len(panels)
        prj_base[l] = prj
        if kind == 0:
            panels += [("attn", l, i) for i in range(5)]
            prj += 5 * TILES
        elif kind == 1:
            panels += [("pool", l, 0)]
            prj += 2 * TILES
        else:
            panels += [("ret", l, i) for i in range(2 * RH)] + [("rout", l, i) for i in range(4)]
            prj += 2 * TILES
        if l + 1 < depth:
            first_panel["ada", l + 1] = len(panels)
            panels += [("ada", l + 1, i) for i in range(ADA_P)]

    def released(s):
        kind, l, i = panels[s]
        if kind == "ada":
            return sem("ada_product"), l * ADA_P + i + 1
        if kind == "attn":
            return sem("proj_done"), prj_base[l] + TILES * (i + 1)
        if kind == "pool":
            return sem("proj_done"), prj_base[l] + 2 * TILES
        if kind == "ret":
            return (sem("ret_qkv"), i // 2 + 1) if i % 2 == 0 else (sem("ret_gate"), i // 2 + 1)
        return sem("proj_done"), prj_base[l] + (TILES if i < 2 else 2 * TILES)

    def slot_of(s):
        return s % 2

    def panel_landed(eng, s, i=0, per=0):
        eng.wait_ge(sem(f"panel_landed{s % 2}"), 48 * (s // 2 + 1) + i * (48 * per // 2))

    ada_w = A["w_ada"].rearrange("l (k p) n -> l p k n", p=128)
    qkv_w = A["attn_w_qkv"].rearrange("l (k p) n -> l p k n", p=128)
    wo_w = A["attn_w_o"].rearrange("l (k p) n -> l p k n", p=128)
    rin_w = A["ret_w_in"].rearrange("l (k p) n -> l p k n", p=128)
    rout_w = A["ret_w_out"].rearrange("l (k p) n -> l p k n", p=128)
    wg_w = A["moe_w_gate"].rearrange("l e (k p) f -> l e p k f", p=128)
    wu_w = A["moe_w_up"].rearrange("l e (k p) f -> l e p k f", p=128)
    wd_w = A["moe_w_down"].rearrange("l e (c p) n -> l e p c n", p=128)

    CREDIT = {"ada_evac": 1, "ada_col": 1, "ada_mod": 1}
    if depth > 2:
        CREDIT.update(ret_in_sb=1, ret_gate_sb=1, ret_yT_sb=1, ret_O_ps=1, state_stored=16)
    for z in ("m", "o"):
        CREDIT.update({z + "_hg_act": 1, z + "_hg_dve": 1, z + "_hT": 1, z + "_act": 2, z + "_PT_sb": 1, z + "_actT_sb": 1,
                       z + "_actT": 1, z + "_scatter": 1, z + "_term": 1, z + "_PT": 2, z + "_gateup": 2,
                       z + "_down": 4, z + "_y_hi": 1, z + "_y_lo": 1, z + "_added": 2})
    for n in CREDIT:
        sem(n)

    def atleast(eng, name, n):
        eng.wait_ge(sem(name), n + CREDIT.get(name, 0))

    class Order:

        def __init__(self, eng, name):
            self.eng, self.sem, self.n, self.base = eng, sem(name), 0, 0

        def __call__(self, ins):
            self.n += 1
            ins.then_inc(self.sem, 1)
            self.eng.wait_ge(self.sem, self.base + self.n)

        def enter(self, i, per):
            self.kept, self.per = self.n, per
            self.base, self.n = i * per + self.n, 0

        def leave(self, times):
            assert self.n == self.per, (self.n, self.per)
            self.n, self.base = self.kept + times * self.per, 0

    block = nc.Block()
    ctx = ExitStack()
    ctx.enter_context(block)

    def load_panel(sp, s, src_of, i=0, per=0):
        dst = panel[s % 2]
        parts = src_of(dst)
        for n, (d, a) in enumerate(parts):
            sp.dma_start(d, a).then_inc(sem(f"panel_landed{s % 2}"), 48 - 16 * (len(parts) - 1) if n == 0 else 16)

    def panel_source(kind, l, i):
        a = l // 3
        if kind == "ada":
            return lambda d: [(d[:, :, 0:ADA_N], ada_w[l, :, :, ds(i * ADA_N, ADA_N)])]
        if kind == "attn" and not isinstance(i, int) or kind == "attn" and i < 3:
            return lambda d: [(d[:, :, :], qkv_w[a, :, :, i * 512:(i + 1) * 512])]
        if kind == "attn":
            return lambda d: [(d[:, :, :], wo_w[a, :, :, (i - 3) * 512:(i - 2) * 512])]
        if kind == "pool":
            pw = A["pool_w"][a].rearrange("g (c p) n -> p (g c) n", p=128)
            return lambda d: [(d[:, :, 0:256], pw)]
        if kind == "rout":
            return lambda d: [(d[:, :, :], rout_w[0, :, (i % 2) * 8:(i % 2) * 8 + 8, (i // 2) * 512:(i // 2) * 512 + 512])]
        raise ValueError(kind)

    def ret_qkv_source(h):
        return lambda d: [(d[:, :, 0:RK], rin_w[0, :, :, ds(h * RK, RK)]),
                          (d[:, :, RK:2 * RK], rin_w[0, :, :, ds(h * RK + RH * RK, RK)]),
                          (d[:, :, 2 * RK:512], rin_w[0, :, :, ds(h * RV + 2 * RH * RK, RV)])]

    def ret_gate_source(h):
        return lambda d: [(d[:, :, 0:RV], rin_w[0, :, :, ds(h * RV + 2 * RH * RK + RH * RV, RV)])]

    def at_e(w, l, e):
        return w[l, e] if isinstance(e, int) else w[l, ds(e, 1)].rearrange("o p k f -> (o p) k f")

    def load_expert(sp, z, l, e, slot):
        sp.dma_start(gu_ring[slot][:, :, 0:FE], at_e(wg_w, l, e)).then_inc(sem(f"{z}_gu_landed{slot}"), 16)
        sp.dma_start(gu_ring[slot][:, :, FE:2 * FE], at_e(wu_w, l, e)).then_inc(sem(f"{z}_gu_landed{slot}"), 16)

    def load_down(sp, z, l, e, slot):
        sp.dma_start(dn_ring[slot][:], at_e(wd_w, l, e)).then_inc(sem(f"{z}_dn_landed{slot}"), 16)

    @block.sync
    def _(sp):
        sp.dma_start(vecs[0:96, 0, :], A["vectors"]).then_inc(sem("vec_landed"), 16)
        sp.dma_start(vecs[0:96, 1:3, :], A["b_ada"].rearrange("l (c n) -> (l c) n", n=128)
                     .rearrange("(a r) n -> r a n", a=2)).then_inc(sem("vec_landed"), 16)
        sp.dma_start(kb[:], A["k_base"]).then_inc(sem("const_landed"), 16)
        passes = []
        for s in range(2):
            load_panel(sp, s, panel_source("ada", 0, s))
        sp.dma_start(x[:, 0, :], A["x_prompt"][0]).then_inc(sem("x_landed"), 16)
        sp.dma_start(x[:, 1:3, :], A["x_sample"][0].rearrange("(a p) n -> p a n", p=128)).then_inc(sem("x_landed"), 16)
        with sp.Fori(0, (ADA_P - 2) // 2) as i:
            for j in range(2):
                sp.wait_ge(sem("ada_product"), 2 * i + j + 1)
                load_panel(sp, j, panel_source("ada", 0, 2 * i + j + 2))
        for l in range(depth):
            f = first_panel["mix", l]
            n = (first_panel["ada", l + 1] if l + 1 < depth else len(panels)) - f
            if l % 3 == 2:
                for s in (f, f + 1):
                    sp.wait_ge(*released(s - 2))
                    load_panel(sp, s, ret_qkv_source(0) if s == f else ret_gate_source(0))
            else:
                for s in range(f, f + min(n, 2)):
                    sp.wait_ge(*released(s - 2))
                    load_panel(sp, s, panel_source(*panels[s]))
            if l:
                sp.wait_ge(sem("experts_read"), l)
            for e in range(2):
                load_expert(sp, "m", l, e, e)
                if l % 3 != 2:
                    load_down(sp, "m", l, e, e)
            if l % 3 == 2:
                with sp.Fori(0, RH - 1) as h:
                    sp.wait_ge(sem("ret_qkv"), h + 1)
                    load_panel(sp, f, ret_qkv_source(h + 1))
                    sp.wait_ge(sem("ret_gate"), h + 1)
                    load_panel(sp, f + 1, ret_gate_source(h + 1))
                rest = range(f + 2 * RH, f + n)
            else:
                rest = range(f + min(n, 2), f + n)
            for s in rest:
                sp.wait_ge(*released(s - 2))
                load_panel(sp, s, panel_source(*panels[s]))
            if l % 3 == 2:
                sp.wait_ge(sem("ret_y"), RH)
                for e in range(2):
                    load_down(sp, "m", l, e, e)
            nxt = l + 1 < depth
            a0 = first_panel["ada", l + 1] if nxt else 0
            if nxt:
                for j in range(2):
                    sp.wait_ge(*released(a0 + j - 2))
                    load_panel(sp, a0 + j, panel_source("ada", l + 1, j))
            with sp.Fori(0, EXPERTS // 2 - 1) as i:
                for j in range(2):
                    e = 2 * i + j + 2
                    sp.wait_ge(sem("m_gateup"), CREDIT["m_gateup"] + l * EXPERTS + e - 1)
                    load_expert(sp, "m", l, e, j)
                    sp.wait_ge(sem("m_down"), CREDIT["m_down"] + 2 * (l * EXPERTS + e - 1))
                    load_down(sp, "m", l, e, j)
                    if nxt:
                        sp.wait_ge(sem("ada_product"), (l + 1) * ADA_P + e - 1)
                        load_panel(sp, a0 + j, panel_source("ada", l + 1, e))
            sp.wait_ge(sem("routed"), l + 1)
            r = sp.value_load(extra[0:1, l:l + 1], min_val=0, max_val=PASSES - 1)
            done = sum(passes) if passes else 0
            with sp.If(r > 0):
                sp.wait_ge(sem("m_gateup"), CREDIT["m_gateup"] + (l + 1) * EXPERTS)
                sp.wait_ge(sem("m_down"), CREDIT["m_down"] + 2 * (l + 1) * EXPERTS)
                with sp.Fori(0, r) as p:
                    with sp.Fori(0, EXPERTS // 2) as i:
                        for j in range(2):
                            q = (done + p) * EXPERTS + 2 * i + j
                            atleast(sp, "o_gateup", q - 1)
                            load_expert(sp, "o", l, 2 * i + j, j)
                            atleast(sp, "o_down", 2 * q - 2)
                            load_down(sp, "o", l, 2 * i + j, j)
            passes.append(r)
        for t in range(TILES):
            sp.wait_ge(sem("final_ready"), t + 1)
            dst = O["y_prompt"][0] if t == 0 else O["y_sample"][0, (t - 1) * 128:t * 128]
            sp.dma_start(dst, ofin[:, t, :]).then_inc(sem("stored"), 16)
        sp.wait_ge(sem("stored"), 16 * TILES)
        sp.wait_ge(sem("cache_stored"), 32 * ((depth + 2) // 3))
        if depth > 2:
            atleast(sp, "state_stored", 16 * RH)

    def pe_norm(pe, n):
        pe.wait_ge(sem("xn_ready"), TILES * (n + 1))
        for k in range(KD):
            if k >= 4:
                pe.wait_ge(sem(("hT_dve", "hT_act")[k % 2]), KD // 2 * n + (k - 4) // 2 + 1)
            for t in range(TILES):
                last = PE.transpose(ps[k % 4][:, t * 128:(t + 1) * 128], xn[:, t, k * 128:(k + 1) * 128], ident)
            last.then_inc(sem("hT_ps"), 1)

    def pe_broadcast(bank, v, c, half):
        for q in range(4):
            last = PE.matmul(ps[bank][:, q * 128:(q + 1) * 128],
                             mods[:, v * KD + 4 * half + q, c:c + 1].broadcast_to([128, 128]), ident,
                             start=True, stop=True)
        return last

    def pe_gate_bc(pe, n, v):
        for c in range(2):
            for half in range(2):
                pe_broadcast(4 + 2 * c + half, v, c, half).then_inc(sem("gate_ps"), 1)

    def pe_mod_bc(pe, l):
        for i in range(8):
            if i >= 4:
                pe.wait_ge(sem("mod_bc"), 8 * l + i - 3)
            pe_broadcast(4 + i % 4, (4, 3)[i // 4], (i // 2) % 2, i % 2).then_inc(sem("mod_ps"), 1)

    def pe_ada_product(pe, idx, s, i=0, per=0):
        panel_landed(pe, s, i, per)
        atleast(pe, "ada_evac", idx)
        atleast(pe, "ada_mod", idx)
        for kk in range(2):
            for g in range(4):
                last = PE.matmul(ps[4][32 * g:32 * g + 32, 0:ADA_N], cond32[:, 2 * g + kk, :],
                                 panel[s % 2][:, 2 * g + kk, 0:ADA_N], start=kk == 0, stop=kk == 1)
        last.then_inc(sem("ada_product"), 1)

    def pe_ada_columns(pe, idx):
        atleast(pe, "ada_evac", idx + 1)
        for c in range(ADA_N // 128):
            last = PE.matmul(ps[4][:, ADA_N + 2 * c:ADA_N + 2 * c + 2], mpan[:, c * 128:(c + 1) * 128], sel, start=True, stop=True)
        last.then_inc(sem("ada_col"), 1)

    def pe_project(pe, l, i, s, nk, lhs, bank0, group=0, rhs_k=None, start=True, stop=True, signal=True):
        for t in range(TILES):
            for k in range(nk):
                last = PE.matmul(ps[bank0 + t][:], lhs(k, t), panel[s % 2][:, k, :],
                                 start=start and k == 0, stop=stop and k == nk - 1)
            if signal:
                last.then_inc(sem("proj_done"), 1)
        return last

    def pe_attention(pe, l):
        f, a = first_panel["mix", l], l // 3
        def turn(heads, banks):
            for h in heads:
                b = ps[banks[h % len(banks)]]
                done = NQK * a + h
                if h - heads[0] >= len(banks):
                    pe.wait_ge(sem("qkT_sb"), done + 1 - len(banks))
                for t in range(TILES):
                    last = PE.transpose(b[:, t * 128:(t + 1) * 128], qkv[:, t, h * HD:(h + 1) * HD], ident)
                if h >= HEADS:
                    last = PE.transpose(b[:, 384:512], ckv[:, 0, (h - HEADS) * HD:(h - HEADS + 1) * HD], ident)
                last.then_inc(sem("qkT_ps"), 1)

        pe.wait_ge(sem("hT_dve"), KD // 2 * (2 * l + 1))
        pe.wait_ge(sem("hT_act"), KD // 2 * (2 * l + 1))
        for i in range(3):
            panel_landed(pe, f + i)
            if i == 1:
                pe.wait_ge(sem("gate_bc"), 4 * (2 * l + 1))
            if i == 2:
                pe.wait_ge(sem("qkv_sb"), 9 * a + 3)
            pe_project(pe, l, i, f + i, KD, lambda k, t: hT[:, k, t * 128:(t + 1) * 128], (0, 4, 0)[i])
        pe.wait_ge(sem("qkv_sb"), 9 * a + 6)
        pe_mod_bc(pe, l)
        pe.wait_ge(sem("mod_bc"), 8 * (l + 1))
        pe.wait_ge(sem("cache_landed"), 32 * (a + 1))
        pe.wait_ge(sem("qk_ready"), 3 * TILES * a + 2 * TILES)
        turn(range(0, HEADS), (4, 5, 6, 7))
        pe.wait_ge(sem("qk_ready"), 3 * TILES * (a + 1))
        turn(range(HEADS, NQK), (0, 1))
        pe.wait_ge(sem("qkT_sb"), NQK * (a + 1))

        def scores(h):
            b0, g = 2 * (h % 2), h // (HEADS // KV)
            if h >= 2:
                pe.wait_ge(sem("prob"), 3 * (HEADS * a + h - 1))
            PE.matmul(ps[b0][:, 0:128], qT[:, h, 0:128], kT[:, g, 0:128], start=True, stop=True)
            PE.matmul(ps[b0][:, 128:512], qT[:, h, 128:256], kT[:, g, 128:512], start=True, stop=True)
            PE.matmul(ps[b0 + 1][:, 0:384], qT[:, h, 256:384], kT[:, g, 128:512], start=True, stop=True)\
                .then_inc(sem("scores"), 1)

        def turn_probs(h):
            n = HEADS * a + h
            pe.wait_ge(sem("prob_norm"), n + 1)
            if h:
                pe.wait_ge(sem("probT_sb"), 2 * n)
            for c in range(7):
                last = PE.transpose(ps[4 + c // 4][:, (c % 4) * 128:(c % 4) * 128 + 128],
                                    prob[:, h % 2, c * 128:(c + 1) * 128], ident)
                if c in (3, 6):
                    last.then_inc(sem("probT_ps"), 1)

        def outputs(h):
            g = h // (HEADS // KV)
            n = HEADS * a + h
            pe.wait_ge(sem("probT_sb"), 2 * (n + 1))
            if h >= 2:
                pe.wait_ge(sem("oT_sb"), n - 1)
            v = lambda t: qkv[:, t, (NQK + g) * HD:(NQK + g + 1) * HD]
            cv = ckv[:, 1, g * HD:(g + 1) * HD]
            b = ps[6 + h % 2]
            PE.matmul(b[:, 0:128], v(0), probT[:, h % 2, 0:128], start=True, stop=True)
            for t in (1, 2):
                for c, vals in enumerate((cv, v(1), v(2))):
                    at = 128 + (t - 1) * 384 + c * 128
                    last = PE.matmul(b[:, t * 128:(t + 1) * 128], vals, probT[:, h % 2, at:at + 128],
                                     start=c == 0, stop=c == 2)
            last.then_inc(sem("oT_ps"), 1)

        scores(0)
        scores(1)
        turn_probs(0)
        for h in range(HEADS):
            if h + 2 < HEADS:
                scores(h + 2)
            if h + 1 < HEADS:
                turn_probs(h + 1)
            outputs(h)
        for i in range(3, 5):
            panel_landed(pe, f + i)
            if i == 3:
                pe.wait_ge(sem("oT_sb"), HEADS * (a + 1))
            pe_project(pe, l, i, f + i, HEADS, lambda k, t: oT[:, k, t * 128:(t + 1) * 128], 0 if i == 3 else 3)

    def pe_pool(pe, l):
        f = first_panel["mix", l]
        pe.wait_ge(sem("gate_bc"), 4 * (2 * l + 1))
        pe_mod_bc(pe, l)
        pe.wait_ge(sem("mod_bc"), 8 * (l + 1))
        panel_landed(pe, f)
        for half in range(2):
            pe.wait_ge(sem("pool_u"), 2 * half + 2)
            for t in range(TILES):
                for g in range(2):
                    for c in range(2):
                        q = 2 * (2 * half + g) + c
                        last = PE.matmul(ps[3 * half + t][:, g * 256:(g + 1) * 256],
                                         uT[:, q, POFF[t]:POFF[t] + 128], panel[f % 2][:, q, 0:256],
                                         start=c == 0, stop=c == 1)
                last.then_inc(sem("proj_done"), 1)

    def pe_retention(pe, l):
        f = first_panel["mix", l]
        pe.wait_ge(sem("hT_dve"), KD // 2 * (2 * l + 1))
        pe.wait_ge(sem("hT_act"), KD // 2 * (2 * l + 1))
        pe.wait_ge(sem("gate_bc"), 4 * (2 * l + 1))
        pe_mod_bc(pe, l)
        pe.wait_ge(sem("mod_bc"), 8 * (l + 1))

        def project_qkv(h):
            panel_landed(pe, f, h, 2)
            atleast(pe, "ret_in_sb", 3 * h)
            for t in range(TILES):
                for k in range(KD):
                    last = PE.matmul(ps[t][:], hT[:, k, t * 128:(t + 1) * 128], panel[f % 2][:, k, :],
                                     start=k == 0, stop=k == KD - 1)
            last.then_inc(sem("ret_qkv"), 1)

        def project_gate(h):
            panel_landed(pe, f + 1, h, 2)
            atleast(pe, "ret_gate_sb", h)
            for t in range(TILES):
                for k in range(KD):
                    last = PE.matmul(ps[3 + t // 2][:, (t % 2) * 256:(t % 2) * 256 + 256],
                                     hT[:, k, t * 128:(t + 1) * 128], panel[(f + 1) % 2][:, k, 0:256],
                                     start=k == 0, stop=k == KD - 1)
            last.then_inc(sem("ret_gate"), 1)

        def mix(h):
            atleast(pe, "ret_in_sb", 3 * h + 3)
            atleast(pe, "ret_yT_sb", 2 * h)
            for t in range(TILES):
                PE.transpose(ps[5][:, t * 128:(t + 1) * 128], rq[:, t, :], ident)
            for t in range(TILES):
                last = PE.transpose(ps[6][:, t * 128:(t + 1) * 128], rk[:, t, :], ident)
            last.then_inc(sem("ret_T_ps"), 1)
            pe.wait_ge(sem("ret_T_sb"), 4 * h + 4)
            for t in range(TILES):
                last = PE.matmul(ps[7][:, t * 128:(t + 1) * 128], rkT[:, t * 128:(t + 1) * 128],
                                 rqT[:, t * 128:(t + 1) * 128], start=True, stop=True)
            last.then_inc(sem("ret_S_ps"), 1)
            pe.wait_ge(sem("ret_kd"), h + 1)
            for n, t in enumerate((0, 0, 1, 2)):
                last = PE.matmul(ps[5 + n // 2][:, (n % 2) * 256:(n % 2) * 256 + 256], rkd[:, n, :], rv[:, t, :],
                                 start=True, stop=True)
            last.then_inc(sem("ret_U_ps"), 1)
            pe.wait_ge(sem("ret_S_sb"), h + 1)
            pe.wait_ge(sem("ret_mid"), h + 1)
            pe.wait_ge(sem("state_in"), 16 * h + 16)
            PE.matmul(ps[7][:, 0:256], rST[:, 0, :], rv[:, 0, :], start=True, stop=True)
            PE.matmul(ps[7][:, 256:512], rST[:, 1, :], rv[:, 1, :], start=True, stop=False)
            PE.matmul(ps[7][:, 256:512], rqf[:, 0, :], rs0[:, 0, :], start=False, stop=False)
            PE.matmul(ps[7][:, 256:512], rqb[:, 0, :], rs1[:, 1, :], start=False, stop=True)
            pe.wait_ge(sem("ret_state_out"), h + 1)
            PE.matmul(ps[5][:, 0:256], rST[:, 2, :], rv[:, 2, :], start=True, stop=False)
            PE.matmul(ps[5][:, 0:256], rqf[:, 1, :], rs1[:, 0, :], start=False, stop=False)
            PE.matmul(ps[5][:, 0:256], rqb[:, 1, :], rs0[:, 1, :], start=False, stop=True).then_inc(sem("ret_O_ps"), 1)

        def turn_y(h):
            pe.wait_ge(sem("ret_y"), h + 1)
            for c in range(2):
                for t in range(TILES):
                    last = PE.transpose(ps[6 - c][:, t * 128:(t + 1) * 128], rof[:, t, c * 128:(c + 1) * 128], ident)
                last.then_inc(sem("ret_yT_ps"), 1)

        project_qkv(0)
        project_gate(0)
        with pe.Fori(0, RH - 1) as h:
            mix(h)
            project_qkv(h + 1)
            turn_y(h)
            project_gate(h + 1)
        mix(RH - 1)
        turn_y(RH - 1)
        atleast(pe, "ret_yT_sb", 2 * RH)
        s = f + 2 * RH
        for half in range(2):
            for part in range(2):
                panel_landed(pe, s)
                for t in range(TILES):
                    for k in range(8):
                        src = (yTe, yTo)[k % 2]
                        last = PE.matmul(ps[3 * half + t][:], src[:, 4 * part + k // 2, t * 128:(t + 1) * 128],
                                         panel[s % 2][:, k, :], start=part == 0 and k == 0,
                                         stop=part == 1 and k == 7)
                    if part == 1:
                        last.then_inc(sem("proj_done"), 1)
                s += 1

    def pe_route(pe, l):
        n = 2 * l + 1
        pe.wait_ge(sem("hT_dve"), KD // 2 * (n + 1))
        pe.wait_ge(sem("hT_act"), KD // 2 * (n + 1))
        pe.wait_ge(sem("router_pad"), 1)
        pe.wait_ge(sem("router_landed"), 64 * DEPTH)
        for kk in range(2):
            for g in range(4):
                last = PE.matmul(ps[2][32 * g:32 * g + 32, 0:T], wr[:, l, 2 * g + kk, :], hT[:, 2 * g + kk, :],
                                 start=kk == 0, stop=kk == 1)
        last.then_inc(sem("logit_parts_ps"), 1)
        pe.wait_ge(sem("logit_parts"), l + 1)
        for t in range(TILES):
            last = PE.matmul(ps[3][:, t * 20:(t + 1) * 20], lpart[:, t * 128:(t + 1) * 128], quad[:, 0:20], start=True, stop=True)
        last.then_inc(sem("logits"), 1)
        pe_gate_bc(pe, n, 5)
        pe.wait_ge(sem("assigned"), l + 1)
        asg = rt[:, 96:96 + TILES * EXPERTS].rearrange("p (t e) -> p t e", t=TILES)
        for t in range(TILES):
            PE.matmul(ps[2][:, t * 16:(t + 1) * 16], tri, asg[:, t, :], start=True, stop=t == 0)
            for u in range(t):
                PE.matmul(ps[2][:, t * 16:(t + 1) * 16], ones[:], asg[:, u, :], start=False, stop=u == t - 1)
        for t in range(TILES):
            last = PE.matmul(ps[2][:, 64:80], ones[:], asg[:, t, :], start=t == 0, stop=t == TILES - 1)
        last.then_inc(sem("ranks"), 1)
        pe.wait_ge(sem("gate_bc"), 4 * (n + 1))

    def pe_gather(pe, z, r, e, j):
        atleast(pe, z + "_P", r + 1)
        atleast(pe, z + "_hg_act", r)
        atleast(pe, z + "_hg_dve", r)
        for t in range(TILES):
            for n, part in enumerate((hhi, hlo)):
                for half in range(2):
                    last = PE.matmul(ps[half][0:CAP, :], Pm[:, j % 2, t, :], part[:, t, half * 512:half * 512 + 512],
                                     start=t == 0 and n == 0, stop=t == TILES - 1 and n == 1)
        last.then_inc(sem(z + "_gather"), 1)

    def pe_gathered_T(pe, z, r):
        pe.wait_ge(sem(z + "_hgt_act"), r + 1)
        pe.wait_ge(sem(z + "_hgt_dve"), r + 1)
        for k in range(KD):
            last = PE.transpose(ps[k // 4][:, (k % 4) * 128:(k % 4) * 128 + CAP], hgt[0:CAP, k * 128:(k + 1) * 128],
                                ident[0:CAP, 0:CAP])
        last.then_inc(sem(z + "_hT"), 1)

    def pe_slots(pe, z, r, e, j):
        atleast(pe, z + "_PT_sb", r)
        for t in range(TILES):
            PE.matmul(ps[5][0:CAP, T:T + 2], Pm[:, j % 2, t, :], gates_r[:, t, ds(e, 1), :], start=t == 0, stop=t == TILES - 1)
        for t in range(TILES):
            last = PE.transpose(ps[5][0:CAP, t * 128:(t + 1) * 128], Pm[:, j % 2, t, :].bitcast(F), ident)
        last.then_inc(sem(z + "_PT"), 1)

    def pe_experts(pe, z, P, g, ada):
        it = P * GROUPS + g
        for j in range(PER):
            e = g * PER + j
            q, r = P * EXPERTS + e, P * (EXPERTS + 1) + e
            atleast(pe, z + "_hg_act", r + 1)
            atleast(pe, z + "_hg_dve", r + 1)
            pe.wait_ge(sem(f"{z}_gu_landed{j % 2}"), 64 * it + 32 * (j // 2 + 1))
            atleast(pe, z + "_act", q)
            for k in range(KD):
                last = PE.matmul(ps[2][0:CAP, :], hg[:, j % 2, k, :], gu_ring[j % 2][:, k, :],
                                 start=k == 0, stop=k == KD - 1)
            last.then_inc(sem(z + "_gateup"), 1)
            pe_gather(pe, z, r + 1, e + 1, j + 1)
            atleast(pe, z + "_act", q + 1)
            atleast(pe, z + "_actT_sb", q)
            for c in range(2):
                last = PE.transpose(ps[3][:, c * 128:c * 128 + CAP], act[0:CAP, c * 128:(c + 1) * 128], ident[0:CAP, 0:CAP])
            last.then_inc(sem(z + "_actT"), 1)
            if ada is not None:
                pe_ada_product(pe, ada[0] + e, ada[1] + j, g, PER)
            atleast(pe, z + "_actT_sb", q + 1)
            pe.wait_ge(sem(f"{z}_dn_landed{j % 2}"), 32 * it + 16 * (j // 2 + 1))
            atleast(pe, z + "_y_hi", 2 * q)
            atleast(pe, z + "_y_lo", 2 * q)
            if j == 0:
                atleast(pe, z + "_term", 6 * it)
            for half in range(2):
                for c in range(2):
                    last = PE.matmul(ps[6 + half][0:CAP, :], actT[:, c, :], dn_ring[j % 2][:, c, half * 512:half * 512 + 512],
                                     start=c == 0, stop=c == 1)
                last.then_inc(sem(z + "_down"), 1)
            pe_gathered_T(pe, z, r + 1)
            if ada is not None:
                pe_ada_columns(pe, ada[0] + e)
            pe_slots(pe, z, r + 1, e + 1, j + 1)
        q = it * PER + PER
        atleast(pe, z + "_y_hi", 2 * q)
        atleast(pe, z + "_y_lo", 2 * q)
        for m in range(2 * TILES):
            t, half = m // 2, m % 2
            if m >= 2:
                atleast(pe, z + "_term", 6 * it + m - 1)
            for j in range(PER):
                for n, part in enumerate((yhi, ylo)):
                    last = PE.matmul(ps[6 + half][:], PT[0:CAP, j, t * 128:(t + 1) * 128],
                                     part[0:CAP, j, half * 512:half * 512 + 512],
                                     start=j == 0 and n == 0, stop=j == PER - 1 and n == 1)
            last.then_inc(sem(z + "_scatter"), 1)

    def pe_first(pe, z, P):
        r = P * (EXPERTS + 1)
        pe_gather(pe, z, r, 0, 0)
        pe_gathered_T(pe, z, r)
        pe_slots(pe, z, r, 0, 0)

    def expert_passes(eng, first, group, passes, l, before=None):
        first("m", l)
        with eng.Fori(0, GROUPS) as g:
            group("m", l, g)
        r = eng.value_load(extra[0:1, l:l + 1], min_val=0, max_val=PASSES - 1)
        done = sum(passes) if passes else 0
        with eng.If(r > 0):
            with eng.Fori(0, r) as p:
                if before is not None:
                    before(done + p)
                first("o", done + p)
                with eng.Fori(0, GROUPS) as g:
                    group("o", done + p, g)
        passes.append(r)

    @block.tensor
    def _(pe):
        pe.wait_ge(sem("vec_landed"), 32)
        pe.wait_ge(sem("const_landed"), 16)
        for a in range(3):
            last = PE.transpose(ps[0][:, a * 96:(a + 1) * 96], vecs[0:96, a, :], ident[0:96, 0:96])
        last.then_inc(sem("vT_ps"), 1)
        pe.wait_ge(sem("cond_ready"), 1)
        with pe.Fori(0, ADA_P // 2) as i:
            for j in range(2):
                pe_ada_product(pe, 2 * i + j, j, i, 2)
                pe_ada_columns(pe, 2 * i + j)
        passes = []
        for l in range(depth):
            pe.wait_ge(sem("mods_ready"), l + 1)
            pe_norm(pe, 2 * l)
            pe_gate_bc(pe, 2 * l, 2)
            (pe_attention, pe_pool, pe_retention)[l % 3](pe, l)
            pe_norm(pe, 2 * l + 1)
            pe_route(pe, l)
            pe.wait_ge(sem("h_lo"), TILES * (l + 1))
            pe.wait_ge(sem("routed"), l + 1)
            ada = ((l + 1) * ADA_P, first_panel["ada", l + 1]) if l + 1 < depth else None

            def first_pass_read(_):
                for name in ("m_hg_act", "m_hg_dve", "m_PT_sb"):
                    atleast(pe, name, (EXPERTS + 1) * (l + 1))

            expert_passes(pe, lambda z, P: pe_first(pe, z, P),
                          lambda z, P, g: pe_experts(pe, z, P, g, ada if z == "m" else None), passes, l, first_pass_read)
            pe.drain().then_inc(sem("experts_read"), 1)
        pe.wait_ge(sem("rstd"), TILES * (2 * depth + 1))
        for half in range(2):
            for q in range(4):
                last = PE.matmul(ps[4 + half][:, q * 128:(q + 1) * 128],
                                 vT[:, 72 + 4 * half + q:73 + 4 * half + q].broadcast_to([128, 128]), ident,
                                 start=True, stop=True)
        last.then_inc(sem("normf_ps"), 1)

    def mod_col(v, k, c):
        return mods[:, v * KD + k, c:c + 1]

    def hT_out(l, sub, k, c):
        if l % 3 == 1 and sub == 0:
            return hp[:, k, POFF[0]:POFF[0] + 128] if c == 0 else hp[:, k, POFF[1]:POFF[1] + DEC]
        return hT[:, k, 0:128] if c == 0 else hT[:, k, 128:T]

    @block.vector
    def _(dve):
        step = Order(dve, "dve_step")

        def finish_mods(l):
            for v in range(6):
                out, raw = mods[:, v * KD:(v + 1) * KD, :], mraw[:, v * KD:(v + 1) * KD, :]
                if v in (1, 4):
                    gain = vT[:, (0 if v == 1 else 32) + l * KD:(0 if v == 1 else 32) + (l + 1) * KD]
                    last = V.scalar_tensor_tensor(out, raw, 1.0, gain.unsqueeze(2).broadcast_to([128, KD, 2]), ALU.add, ALU.mult)
                elif v == 2 and l % 3 == 1:
                    last = V.tensor_tensor(out, raw, vT[:, 64:72].unsqueeze(2).broadcast_to([128, KD, 2]), ALU.mult)
                else:
                    last = V.tensor_copy(out, raw)
            last.then_inc(sem("mods_ready"), 1)
            dve.wait_ge(sem("mods_ready"), l + 1)

        def ada_mod(l, idx, p):
            atleast(dve, "ada_col", idx + 1)
            V.tensor_tensor(mraw[:, ds(3 * p, 3), :], ps[4][:, ADA_N:ADA_N + 6].rearrange("q (c o) -> q c o", c=3),
                            biasT[:, ds(l * 48 + 3 * p, 3)].unsqueeze(2).broadcast_to([128, 3, 2]), ALU.add)\
                .then_inc(sem("ada_mod"), 1)

        def mean_square(n):
            for t in range(TILES):
                dve.wait_ge(sem("ssq"), TILES * n + t + 1)
                V.tensor_scalar(msq[:, t:t + 1], ssq[:, t:t + 1], 1.0 / D, EPS, ALU.mult, ALU.add).then_inc(sem("msq"), 1)

        def norm(l, sub):
            n = 2 * l + sub
            mean_square(n)
            if sub == 1:
                token_major(l, 0)
            for k in range(0, KD, 2):
                dve.wait_ge(sem("hT_ps"), KD * n + k + 1)
                for c, src in enumerate((ps[k % 4][:, 0:128], ps[k % 4][:, 128:T])):
                    last = V.tensor_scalar(hT_out(l, sub, k, c), src, mod_col(1 + 3 * sub, k, c),
                                           mod_col(3 * sub, k, c), ALU.mult, ALU.add)
                last.then_inc(sem("hT_dve"), 1)

        def residual(l, order):
            b = prj_base[l] + (3 * TILES if l % 3 == 0 else 0)
            dve.wait_ge(sem("gate_bc"), 4 * (2 * l + 1))
            for m in range(2 * TILES):
                half, t = m // TILES, m % TILES
                dve.wait_ge(sem("proj_done"), b + m + 1)
                if 6 * l + m >= 2:
                    dve.wait_ge(sem("mix_added"), 6 * l + m - 1)
                if m == 0 and l:
                    dve.wait_ge(sem("layer_done"), l)
                V.tensor_tensor(tmp[:, m % 2, :], ps[3 * half + t][:], gate_bc[:, COND[t], half * 512:half * 512 + 512],
                                ALU.mult).then_inc(sem("mix_term"), 1)

        def attention(l):
            a = l // 3
            sums = stat[:, 0:30].rearrange("p (h t) -> p h t", t=TILES)
            means = stat[:, 32:62]
            rs = stat[:, 64:94].rearrange("p (h t) -> p h t", t=TILES)
            dve.wait_ge(sem("attn_landed"), 64 * (a + 1))
            for i, (h0, h1) in enumerate(((0, 4), (4, 8), (8, NQK))):
                o, nh = slice(h0 * HD, h1 * HD), h1 - h0
                for t in range(TILES):
                    dve.wait_ge(sem("qkv_sb"), 9 * a + 3 * i + t + 1)
                    step(V.tensor_tensor(sqv[:, o], qkv[:, t, o], qkv[:, t, o], ALU.mult))
                    step(V.tensor_reduce(sums[:, h0:h1, t], sqv[:, o].rearrange("p (h d) -> p h d", d=HD), AX.X, ALU.add))
                V.tensor_scalar(stat[:, 32 + 3 * h0:32 + 3 * h1], stat[:, 3 * h0:3 * h1], 1.0 / HD, EPS, ALU.mult, ALU.add)\
                    .then_inc(sem("qk_ms"), 1)
                dve.wait_ge(sem("qk_rstd"), 3 * a + i + 1)
                for t in range(TILES):
                    qk3 = qkv[:, t, o].rearrange("p (h d) -> p h d", d=HD)
                    step(V.tensor_tensor(qk3, qk3, rs[:, h0:h1, t:t + 1].broadcast_to([128, nh, HD]), ALU.mult))
                    last = V.tensor_tensor(qkv[:, t, o], qkv[:, t, o], gqk[:, o], ALU.mult)
                    if t == 0:
                        last.then_inc(sem("qk_ready"), 1)
                        continue
                    step(last)
                    x5 = qkv[:, t, o].rearrange("p (h a b f) -> p h a b f", h=nh, a=2, b=2)
                    r5 = ropet[:, o].rearrange("p (h a b f) -> p h a b f", h=nh, a=2, b=2)
                    tab = rope[:, t - 1, :].rearrange("p (s a b f) -> p s a b f", s=2, a=2, b=2)
                    for b in range(2):
                        for hh in range(2):
                            last = V.tensor_tensor(r5[:, :, hh, b, :], x5[:, :, hh, 1 - b, :],
                                                   tab[:, 1, hh, b, :].unsqueeze(1).broadcast_to([128, nh, 32]), ALU.mult)
                    step(last)
                    step(V.tensor_tensor(qk3, qk3, rope[:, t - 1, 0:128].unsqueeze(1).broadcast_to([128, nh, HD]), ALU.mult))
                    V.tensor_tensor(qkv[:, t, o], qkv[:, t, o], ropet[:, o], ALU.add).then_inc(sem("qk_ready"), 1)
                    dve.wait_ge(sem("qk_ready"), 9 * a + 3 * i + t + 1)
            mx = stat[:, 0:12].rearrange("p (b c) -> p b c", b=4)
            den = stat[:, 12:24].rearrange("p (b c) -> p b c", b=4)
            inv = stat[:, 24:30].rearrange("p (b c) -> p b c", b=2)
            def maxima(h):
                n, b0 = HEADS * a + h, 2 * (h % 2)
                units = (ps[b0][:, 0:128], ps[b0][:, 128:512], ps[b0 + 1][:, 0:384])
                dve.wait_ge(sem("scores"), n + 1)
                for u, src in enumerate(units):
                    last = V.tensor_reduce(mx[:, h % 2, u:u + 1], src, AX.X, ALU.max)
                step(last)
                V.tensor_scalar(mx[:, 2 + h % 2, :], mx[:, h % 2, :], -float(HD) ** -0.5, None, ALU.mult).then_inc(sem("neg_max"), 1)

            maxima(0)
            for h in range(HEADS):
                if h + 1 < HEADS:
                    maxima(h + 1)
                dve.wait_ge(sem("prob"), 3 * (HEADS * a + h + 1))
                step(V.reciprocal(inv[:, h % 2, :], den[:, h % 2, :]))
                for u, (lo, hi) in enumerate(((0, 128), (128, 512), (512, 896))):
                    last = V.tensor_scalar(prob[:, h % 2, lo:hi], prob[:, h % 2, lo:hi], inv[:, h % 2, u:u + 1], None, ALU.mult)
                last.then_inc(sem("prob_norm"), 1)

        def pool(l):
            dve.wait_ge(sem("pool_pads"), 1)
            dve.wait_ge(sem("hT_dve"), KD // 2 * (2 * l + 1))
            dve.wait_ge(sem("hT_act"), KD // 2 * (2 * l + 1))
            dve.wait_ge(sem("count_landed"), 16)
            for g, win in enumerate(WINDOWS):
                src = hp[:, 2 * g:2 * g + 2, :]
                bufs, m, lo, hi = (win_a, win_b), 1, 0, PW
                while m < win:
                    a, b = (1, 0) if m == 1 else (m // 2, m // 2)
                    lo, hi = lo + a, hi - b
                    dst = bufs[0][:]
                    step(V.tensor_tensor(dst[:, :, lo:hi], src[:, :, lo - a:hi - a], src[:, :, lo + b:hi + b], ALU.add))
                    src, bufs, m = dst, bufs[::-1], 2 * m
                dst = bufs[0][:]
                step(V.tensor_tensor(dst[:, :, PAD:PW - PAD], src[:, :, PAD:PW - PAD],
                                     icnt[:, g:g + 1, PAD:PW - PAD].broadcast_to([128, 2, PW - 2 * PAD]), ALU.mult))
                V.tensor_tensor(uT[:, 2 * g:2 * g + 2, PAD:PW - PAD], dst[:, :, PAD:PW - PAD],
                                hp[:, 2 * g:2 * g + 2, PAD:PW - PAD], ALU.subtract).then_inc(sem("pool_u"), 1)
                dve.wait_ge(sem("pool_u"), g + 1)

        def decay_tables():
            dve.wait_ge(sem("ret_const"), 48)
            z = rsm[:, 0:16]
            neg, e1, w, w2, acc, lg = (rsm[:, 16 * i:16 * i + 16] for i in range(1, 7))
            step(V.tensor_scalar(neg, z, -1.0, None, ALU.mult))
            V.tensor_tensor(neg, z, neg, ALU.min).then_inc(sem("decay_in"), 1)
            dve.wait_ge(sem("decay_exp"), 1)
            step(V.tensor_scalar(w, e1, 2.0, None, ALU.add))
            step(V.reciprocal(w, w))
            step(V.tensor_tensor(w, w, e1, ALU.mult))
            step(V.tensor_tensor(w2, w, w, ALU.mult))
            step(V.tensor_scalar(acc, w2, 1.0 / 17, 1.0 / 15, ALU.mult, ALU.add))
            for d in (13, 11, 9, 7, 5, 3, 1):
                step(V.tensor_tensor(acc, acc, w2, ALU.mult))
                step(V.tensor_scalar(acc, acc, 1.0 / d, None, ALU.add))
            step(V.tensor_tensor(acc, acc, w, ALU.mult))
            step(V.tensor_scalar(lg, z, 0.0, None, ALU.min))
            V.scalar_tensor_tensor(lg, acc, -2.0, lg, ALU.mult, ALU.add).then_inc(sem("log_decay"), 1)
            for h in range(RH):
                dve.wait_ge(sem("mask_exp"), 2 * h + 2)
                step(V.tensor_tensor(rMT[:, h, :], rMT[:, h, :], kret[:, 128:256], ALU.mult))
                step(V.tensor_tensor(rof[:, h % 2, 0:128], rof[:, h % 2, 0:128], kret[:, 384:512], ALU.mult))
                V.tensor_tensor(rMT[:, h, :], rMT[:, h, :], rof[:, h % 2, 0:128], ALU.add).then_inc(sem("mask_done"), 1)

        def retention(l):
            decay_tables()
            dve.wait_ge(sem("mask_exp"), 2 * RH + 1)
            dve.wait_ge(sem("mask_done"), RH)
            with dve.Fori(0, RH) as h:
                step.enter(h, 5)
                dve.wait_ge(sem("ret_qkv"), h + 1)
                V.tensor_copy(rqkv[:, 1, :], ps[1][:]).then_inc(sem("ret_in_sb"), 1)
                atleast(dve, "ret_in_sb", 3 * h + 3)
                for n, (t, d) in enumerate(((0, 0), (0, 1), (1, 0), (2, 1))):
                    last = V.tensor_scalar(rkd[:, n, :], rk[:, t, :], rsm[:, ds(112 + 8 * d + h, 1)], float(RK) ** -0.5,
                                           ALU.mult, ALU.mult)
                last.then_inc(sem("ret_kd"), 1)
                dve.wait_ge(sem("ret_T_ps"), h + 1)
                V.tensor_copy(rqT[:], ps[5][:, 0:T]).then_inc(sem("ret_T_sb"), 1)
                V.tensor_tensor(rqf[:].rearrange("p t i -> p t i"), ps[5][:, 128:T].rearrange("p (t i) -> p t i", t=2),
                                rdf[:, ds(h, 1), :].broadcast_to([128, 2, 128]), ALU.mult).then_inc(sem("ret_T_sb"), 1)
                V.tensor_tensor(rqb[:], ps[5][:, 128:T].rearrange("p (t i) -> p t i", t=2),
                                rdb[:, ds(h, 1), :].broadcast_to([128, 2, 128]), ALU.mult).then_inc(sem("ret_T_sb"), 1)
                dve.wait_ge(sem("ret_S_ps"), h + 1)
                V.tensor_tensor(rST[:], ps[7][:, 0:T].rearrange("p (t i) -> p t i", t=TILES),
                                rMT[:, ds(h, 1), :].broadcast_to([128, TILES, 128]), ALU.mult).then_inc(sem("ret_S_sb"), 1)
                dve.wait_ge(sem("ret_U_ps"), h + 1)
                dve.wait_ge(sem("state_in"), 16 * h + 16)
                V.scalar_tensor_tensor(rs1[:, 0, :], rs0[:, 0, :], rsm[:, ds(128 + h, 1)], ps[6][:, 0:256], ALU.mult, ALU.add)
                V.scalar_tensor_tensor(rs1[:, 1, :], rs0[:, 1, :], rsm[:, ds(136 + h, 1)], ps[6][:, 256:512], ALU.mult, ALU.add)\
                    .then_inc(sem("ret_mid"), 1)
                atleast(dve, "ret_O_ps", h + 1)
                outs = (ps[7][:, 0:256], ps[7][:, 256:512], ps[5][:, 0:256])
                bst, agg = rsm[:, 144:162], rsm[:, 164:170]
                for t in range(TILES):
                    last = V.bn_stats(bst[:, 6 * t:6 * t + 6], outs[t])
                step(last)
                atleast(dve, "ret_gate_sb", h + 1)
                V.tensor_tensor(rg[:], rg[:], rnorm[:, ds(h, 1), :].broadcast_to([128, TILES, RV]), ALU.mult)
                for t in range(TILES):
                    last = V.bn_aggr(agg[:, 2 * t:2 * t + 2], bst[:, 6 * t:6 * t + 6])
                step(last)
                V.tensor_scalar(rsm[:, 172:175], agg.rearrange("p (t c) -> p t c", c=2)[:, :, 1], EPS, None, ALU.add)\
                    .then_inc(sem("ret_var"), 1)
                dve.wait_ge(sem("ret_rstd"), h + 1)
                for t in range(TILES):
                    step(V.tensor_scalar(rof[:, t, :], outs[t], agg[:, 2 * t:2 * t + 1], rsm[:, 176 + t:177 + t],
                                         ALU.subtract, ALU.mult))
                V.tensor_tensor(rof[:], rof[:], rg[:], ALU.mult).then_inc(sem("ret_y"), 1)
            step.leave(RH)

        def pick(out, vals, mx, scratch):
            b = lambda a: a.unsqueeze(2).broadcast_to([128, TILES, 4])
            step(V.tensor_tensor(scratch, vals, b(mx), ALU.is_equal))
            step(V.tensor_tensor(scratch, scratch, tie.unsqueeze(1).broadcast_to([128, TILES, 4]), ALU.mult))
            step(V.tensor_reduce(scol, scratch, AX.X, ALU.max))
            step(V.tensor_tensor(out, scratch, b(scol), ALU.is_equal))

        scol = rt[:, 424:427]

        def route(l):
            g3 = lambda o, n: rt[:, o:o + 3 * n].rearrange("p (t e) -> p t e", t=TILES)
            lg, asg, gts, rk16 = g3(0, 20), g3(96, 16), g3(144, 16), g3(192, 16)
            gmax, ohg, scr, les = rt[:, 240:243], g3(243, 4), g3(255, 4), g3(267, 4)
            prod = rt[:, 280:328].rearrange("p (t g e) -> p t g e", t=TILES, g=4)
            m1, m2, oh1, oh2, les2 = rt[:, 328:331], rt[:, 331:334], g3(334, 4), g3(346, 4), g3(358, 4)
            ein, eout = g3(370, 5), g3(385, 5)
            den, w1, w2 = rt[:, 400:403], rt[:, 403:406], rt[:, 406:409]
            cmax, over, nx = rt[:, 409:410], rt[:, 410:410 + PASSES], rt[:, 420:421]
            b4 = lambda a: a.unsqueeze(2).broadcast_to([128, TILES, 4])
            dve.wait_ge(sem("logits"), l + 1)
            dve.wait_ge(sem("router_landed"), 64 * DEPTH)
            step(V.tensor_tensor(lg, ps[3][:, 0:60].rearrange("p (t e) -> p t e", t=TILES),
                                 rb[:, l:l + 1, :].broadcast_to([128, TILES, 20]), ALU.add))
            step(V.tensor_reduce(gmax, lg[:, :, 0:4], AX.X, ALU.max))
            pick(ohg, lg[:, :, 0:4], gmax, scr)
            for t in range(TILES):
                last = V.tensor_tensor(prod[:, t], lg[:, t, 4:20].rearrange("p (g e) -> p g e", g=4),
                                       ohg[:, t, :].unsqueeze(2).broadcast_to([128, 4, 4]), ALU.mult)
            step(last)
            for t in range(TILES):
                last = V.tensor_reduce(les[:, t, :], prod[:, t].rearrange("p g e -> p e g"), AX.X, ALU.add)
            step(last)
            step(V.tensor_reduce(m1, les, AX.X, ALU.max))
            pick(oh1, les, m1, scr)
            step(V.scalar_tensor_tensor(les2, oh1, -1e30, les, ALU.mult, ALU.add))
            step(V.tensor_reduce(m2, les2, AX.X, ALU.max))
            pick(oh2, les2, m2, scr)
            step(V.tensor_tensor(asg[:, :, 0:4], oh1, oh2, ALU.add))
            step(V.tensor_copy(les2, asg[:, :, 0:4]))
            for t in range(TILES):
                last = V.tensor_tensor(asg[:, t, :].rearrange("p (g e) -> p g e", g=4),
                                       ohg[:, t, :].unsqueeze(2).broadcast_to([128, 4, 4]),
                                       les2[:, t, :].unsqueeze(1).broadcast_to([128, 4, 4]), ALU.mult)
            last.then_inc(sem("assigned"), 1)
            dve.wait_ge(sem("h_hi"), TILES * (l + 1))
            V.tensor_tensor(hlo[:, 2, :], htok[:, 2, :], hhi[:, 2, :].bitcast(F), ALU.subtract).then_inc(sem("h_lo"), 1)
            step(V.tensor_tensor(ein[:, :, 0:4], lg[:, :, 0:4], b4(gmax), ALU.subtract))
            V.tensor_tensor(ein[:, :, 4], m2, m1, ALU.subtract).then_inc(sem("route_exp_in"), 1)
            dve.wait_ge(sem("route_exp"), l + 1)
            step(V.tensor_reduce(den, eout[:, :, 0:4], AX.X, ALU.add))
            step(V.tensor_scalar(w2, eout[:, :, 4], 1.0, None, ALU.add))
            step(V.tensor_tensor(den, den, w2, ALU.mult))
            step(V.reciprocal(w1, den))
            step(V.tensor_tensor(w2, w1, eout[:, :, 4], ALU.mult))
            step(V.tensor_tensor(les, oh1, b4(w1), ALU.mult))
            step(V.tensor_tensor(les2, oh2, b4(w2), ALU.mult))
            step(V.tensor_tensor(les, les, les2, ALU.add))
            for t in range(TILES):
                last = V.tensor_tensor(gts[:, t, :].rearrange("p (g e) -> p g e", g=4),
                                       ohg[:, t, :].unsqueeze(2).broadcast_to([128, 4, 4]),
                                       les[:, t, :].unsqueeze(1).broadcast_to([128, 4, 4]), ALU.mult)
            step(last)
            step(V.tensor_copy(gates_r[:, :, 0:EXPERTS, 0], gts))
            step(V.tensor_tensor(gates_r[:, :, 0:EXPERTS, 1], gts, gates_r[:, :, 0:EXPERTS, 0].bitcast(F), ALU.subtract))
            dve.wait_ge(sem("ranks"), l + 1)
            step(V.tensor_scalar(rk16, ps[2][:, 0:48].rearrange("p (t e) -> p t e", t=TILES), 1.0, None, ALU.add))
            step(V.tensor_tensor(rk16, rk16, asg, ALU.mult))
            step(V.tensor_scalar(rankm[:, :, 0:EXPERTS], rk16, -1.0, None, ALU.add))
            step(V.tensor_reduce(cmax, ps[2][:, 64:80], AX.X, ALU.max))
            step(V.tensor_tensor(over, cmax.broadcast_to([128, PASSES]), caps, ALU.is_gt))
            step(V.tensor_reduce(nx, over, AX.X, ALU.add))
            V.tensor_copy(extra[:, l:l + 1], nx).then_inc(sem("routed"), 1)
            dve.wait_ge(sem("routed"), l + 1)

        def token_major(l, t):
            if t == 0:
                if l % 3 == 0:
                    dve.wait_ge(sem("cache_stored"), 32 * (l // 3 + 1))
                elif l % 3 == 2:
                    atleast(dve, "state_stored", 16 * RH)
                dve.wait_ge(sem("mod_bc"), 8 * (l + 1))
            dve.wait_ge(sem("xn_ready"), TILES * (2 * l + 1) + t + 1)
            step(V.tensor_tensor(htok[:, t, :], xn[:, t, :], mod_bc[:, COND[t], :], ALU.mult))
            V.tensor_tensor(htok[:, t, :], htok[:, t, :], mod_bc[:, 2 + COND[t], :], ALU.add).then_inc(sem("h_tok"), 1)

        def place_tokens(z, r, e, j, shifts):
            if z == "o":
                dve.wait_ge(sem("rank_shift"), shifts)
            atleast(dve, z + "_PT", r - 1)
            for t in range(TILES):
                last = V.tensor_scalar(Pm[:, j % 2, t, :], iota[:, 0:CAP], rankm[:, t, ds(e, 1)], None, ALU.is_equal)
            last.then_inc(sem(z + "_P"), 1)

        def gathered_rows(z, r):
            dve.wait_ge(sem(z + "_gather"), r + 1)
            atleast(dve, z + "_hT", r)
            V.tensor_copy(hgt[0:CAP, 512:1024], ps[1][0:CAP, :]).then_inc(sem(z + "_hgt_dve"), 1)

        def gathered_cols(z, r, q, j):
            atleast(dve, z + "_hT", r + 1)
            atleast(dve, z + "_gateup", q - 1)
            V.tensor_copy(hg[:, j % 2, 4:8, :], ps[1][:].rearrange("p (k s) -> p k s", k=4)[:, :, 0:CAP])\
                .then_inc(sem(z + "_hg_dve"), 1)

        def experts(z, P, g, ada, order, shifts=0):
            it = P * GROUPS + g
            for j in range(PER):
                e = g * PER + j
                q, r = P * EXPERTS + e, P * (EXPERTS + 1) + e
                place_tokens(z, r + 1, e + 1, j + 1, shifts)
                atleast(dve, z + "_PT_sb", r + 1)
                order(V.tensor_reduce(gsum[0:CAP, 0:1], gslot[0:CAP, j % 2, :], AX.X, ALU.add))
                dve.wait_ge(sem(z + "_silu"), q + 1)
                atleast(dve, z + "_actT", q)
                V.scalar_tensor_tensor(act[0:CAP, :], ps[2][0:CAP, FE:2 * FE], gsum[0:CAP, 0:1], silu[0:CAP, :], ALU.mult, ALU.mult)\
                    .then_inc(sem(z + "_act"), 1)
                gathered_rows(z, r + 1)
                atleast(dve, z + "_scatter", 6 * it)
                for half in range(2):
                    o = slice(half * 512, half * 512 + 512)
                    atleast(dve, z + "_y_hi", 2 * q + half + 1)
                    V.tensor_tensor(ylo[0:CAP, j, o], ps[6 + half][0:CAP, :], yhi[0:CAP, j, o].bitcast(F), ALU.subtract)\
                        .then_inc(sem(z + "_y_lo"), 1)
                gathered_cols(z, r + 1, q + 1, j + 1)
                if ada is not None:
                    ada_mod(ada[0], ada[1] + e, e)
            for m in range(2 * TILES):
                t, half = m // 2, m % 2
                atleast(dve, z + "_scatter", 6 * it + m + 1)
                atleast(dve, z + "_added", 6 * it + m - 1)
                V.tensor_tensor(tmp[:, m % 2, :], ps[6 + half][:], gate_bc[:, COND[t], half * 512:half * 512 + 512],
                                ALU.mult).then_inc(sem(z + "_term"), 1)

        dve.wait_ge(sem("vT_ps"), 1)
        V.memset(cond32[:], 0.0)
        V.memset(ones[:], 1.0)
        V.tensor_copy(vT[:], ps[0][:, 0:288]).then_inc(sem("vT_sb"), 1)
        dve.wait_ge(sem("vT_sb"), 1)
        with dve.Fori(0, ADA_P) as i:
            ada_mod(0, i, i)
        atleast(dve, "ada_mod", ADA_P)
        passes = []
        pass_order = Order(dve, "dve_pass_step")
        for l in range(depth):
            finish_mods(l)
            norm(l, 0)
            if l % 3 == 0:
                attention(l)
            elif l % 3 == 1:
                pool(l)
            else:
                retention(l)
            residual(l, step)
            norm(l, 1)
            token_major(l, 1)
            token_major(l, 2)
            route(l)
            dve.wait_ge(sem("gate_bc"), 4 * (2 * l + 2))
            dve.wait_ge(sem("mix_added"), 6 * (l + 1))
            dve.wait_ge(sem("h_lo"), TILES * (l + 1))
            nxt = (l + 1, (l + 1) * ADA_P) if l + 1 < depth else None

            def group(z, P, g):
                if z == "m":
                    step.enter(g, PER)
                    experts(z, P, g, nxt, step)
                    step.leave(GROUPS)
                else:
                    pass_order.base, pass_order.n = (P * GROUPS + g) * PER, 0
                    experts(z, P, g, None, pass_order, shifted[0])

            def first(z, P):
                r = P * (EXPERTS + 1)
                place_tokens(z, r, 0, 0, shifted[0])
                gathered_rows(z, r)
                gathered_cols(z, r, P * EXPERTS, 0)

            shifted = [0]

            def next_ranks(n):
                atleast(dve, "m_added", 6 * GROUPS * (l + 1))
                atleast(dve, "m_PT", (EXPERTS + 1) * (l + 1))
                V.tensor_scalar(rankm[:], rankm[:], float(-CAP), None, ALU.add).then_inc(sem("rank_shift"), 1)
                shifted[0] = n + 1

            expert_passes(dve, first, group, passes, l, next_ranks)
            if l + 1 < depth:
                atleast(dve, "ada_mod", (l + 2) * ADA_P)
        n = 2 * depth
        mean_square(n)
        dve.wait_ge(sem("rstd"), TILES * (n + 1))
        dve.wait_ge(sem("normf_ps"), 1)
        for t in range(TILES):
            for half in range(2):
                o = slice(half * 512, half * 512 + 512)
                last = V.scalar_tensor_tensor(ofin[:, t, o], x[:, t, o], rstd[:, t:t + 1], ps[4 + half][:], ALU.mult, ALU.mult)
            last.then_inc(sem("final_ready"), 1)

    @block.scalar
    def _(act_e):
        e = act_e
        step = Order(e, "act_step")

        def sum_squares(n):
            if n == 0:
                e.wait_ge(sem("x_landed"), 32)
            elif n % 2 == 0:
                e.wait_ge(sem("layer_done"), n // 2)
            if n:
                e.wait_ge(sem("msq"), TILES * n)
            for t in range(TILES):
                if n % 2:
                    e.wait_ge(sem("mix_added"), 6 * (n // 2) + TILES + t + 1)
                squares = xn[:, t, :] if n % 2 == 0 else \
                    (kT.rearrange("p g s -> p (g s)"), hp[:, 0:4].rearrange("p k s -> p (k s)"),
                     rqkv[:, 0:2].rearrange("p t n -> p (t n)"))[n // 2 % 3][:, 0:D]
                if n % 2 and t:
                    e.wait_ge(sem("ssq"), TILES * n + t)
                S.activation(squares, x[:, t, :], ACT.Square, accum_out=ssq[:, t:t + 1]).then_inc(sem("ssq"), 1)

        def norm(l, sub):
            n = 2 * l + sub
            sum_squares(n)
            e.wait_ge(sem("ssq"), TILES * (n + 1))
            for t in range(TILES):
                e.wait_ge(sem("rstd"), TILES * n + t + 1)
                S.activation(xn[:, t, :], x[:, t, :], ACT.Copy, scale=rstd[:, t:t + 1]).then_inc(sem("xn_ready"), 1)
            e.wait_ge(sem("mods_ready"), l + 1)
            for k in range(1, KD, 2):
                e.wait_ge(sem("hT_ps"), KD * n + k + 1)
                for c, src in enumerate((ps[k % 4][:, 0:128], ps[k % 4][:, 128:T])):
                    last = S.activation(hT_out(l, sub, k, c), src, ACT.Identity, bias=mod_col(3 * sub, k, c),
                                        scale=mod_col(1 + 3 * sub, k, c))
                last.then_inc(sem("hT_act"), 1)

        def gate(n):
            for c in range(2):
                for half in range(2):
                    e.wait_ge(sem("gate_ps"), 4 * n + 2 * c + half + 1)
                    S.activation(gate_bc[:, c, half * 512:half * 512 + 512], ps[4 + 2 * c + half][:], ACT.Copy)\
                        .then_inc(sem("gate_bc"), 1)

        def mod_copies(l):
            for i in range(8):
                e.wait_ge(sem("mod_ps"), 8 * l + i + 1)
                S.activation(mod_bc[:, i // 2, (i % 2) * 512:(i % 2) * 512 + 512], ps[4 + i % 4][:], ACT.Copy)\
                    .then_inc(sem("mod_bc"), 1)

        def ada_copy(idx):
            e.wait_ge(sem("ada_product"), idx + 1)
            atleast(e, "ada_col", idx)
            S.activation(mpan[:], ps[4][:, 0:ADA_N], ACT.Copy).then_inc(sem("ada_evac"), 1)

        def attention(l):
            a = l // 3
            e.dma_start(ckv[:, 0, :], A["cache_k"][0, a].rearrange("s h d -> s (h d)")).then_inc(sem("cache_landed"), 16)
            e.dma_start(ckv[:, 1, :], A["cache_v"][0, a].rearrange("s h d -> s (h d)")).then_inc(sem("cache_landed"), 16)
            e.dma_start(gqk[:, 0:HEADS * HD].rearrange("p (h d) -> p h d", h=HEADS),
                        A["attn_q_norm"][a:a + 1, :].unsqueeze(1).broadcast_to([128, HEADS, HD])).then_inc(sem("attn_landed"), 16)
            e.dma_start(gqk[:, HEADS * HD:].rearrange("p (h d) -> p h d", h=KV),
                        A["attn_k_norm"][a:a + 1, :].unsqueeze(1).broadcast_to([128, KV, HD])).then_inc(sem("attn_landed"), 16)
            e.dma_start(rope[:], A["k_rope"]).then_inc(sem("attn_landed"), 32)
            def panel_rows(i):
                for t in range(TILES):
                    e.wait_ge(sem("proj_done"), prj_base[l] + 3 * i + t + 1)
                    S.activation(qkv[:, t, i * 512:(i + 1) * 512], ps[(0, 4, 0)[i] + t][:], ACT.Copy).then_inc(sem("qkv_sb"), 1)

            for i in range(3):
                panel_rows(i)
            mod_copies(l)
            for h in range(NQK):
                b = ps[4 + h % 4] if h < HEADS else ps[h % 2]
                e.wait_ge(sem("qkT_ps"), NQK * a + h + 1)
                if h < HEADS:
                    S.activation(qT[:, h, :], b[:, 0:T], ACT.Copy).then_inc(sem("qkT_sb"), 1)
                else:
                    S.activation(kT[:, h - HEADS, 0:128], b[:, 0:128], ACT.Copy)
                    S.activation(kT[:, h - HEADS, 128:256], b[:, 384:512], ACT.Copy)
                    S.activation(kT[:, h - HEADS, 256:512], b[:, 128:384], ACT.Copy).then_inc(sem("qkT_sb"), 1)
            e.dma_start(O["new_cache_k"][0, a].rearrange("s h d -> s (h d)"), qkv[:, 0, HEADS * HD:NQK * HD])\
                .then_inc(sem("cache_stored"), 16)
            e.dma_start(O["new_cache_v"][0, a].rearrange("s h d -> s (h d)"), qkv[:, 0, NQK * HD:])\
                .then_inc(sem("cache_stored"), 16)

            def soft(h):
                n, b0 = HEADS * a + h, 2 * (h % 2)
                units = ((ps[b0][:, 0:128], 0, 128), (ps[b0][:, 128:512], 128, 512), (ps[b0 + 1][:, 0:384], 512, 896))
                e.wait_ge(sem("neg_max"), n + 1)
                if h >= 2:
                    e.wait_ge(sem("probT_ps"), 2 * (n - 1))
                for u, (src, lo, hi) in enumerate(units):
                    S.activation(prob[:, h % 2, lo:hi], src, ACT.Exp, bias=stat[:, 6 + 3 * (h % 2) + u:7 + 3 * (h % 2) + u],
                                 scale=float(HD) ** -0.5, accum_out=stat[:, 12 + 3 * (h % 2) + u:13 + 3 * (h % 2) + u])\
                        .then_inc(sem("prob"), 1)

            def probs_T(h):
                n = HEADS * a + h
                if h >= 2:
                    e.wait_ge(sem("oT_ps"), n - 1)
                e.wait_ge(sem("probT_ps"), 2 * n + 1)
                S.activation(probT[:, h % 2, 0:512], ps[4][:], ACT.Copy).then_inc(sem("probT_sb"), 1)
                e.wait_ge(sem("probT_ps"), 2 * n + 2)
                S.activation(probT[:, h % 2, 512:896], ps[5][:, 0:384], ACT.Copy).then_inc(sem("probT_sb"), 1)

            soft(0)
            soft(1)
            probs_T(0)
            for h in range(HEADS):
                if h + 2 < HEADS:
                    soft(h + 2)
                if h + 1 < HEADS:
                    probs_T(h + 1)
                e.wait_ge(sem("oT_ps"), HEADS * a + h + 1)
                S.activation(oT[:, h, :], ps[6 + h % 2][:, 0:T], ACT.Copy).then_inc(sem("oT_sb"), 1)

        def retention(l):
            kr = A["k_ret"]
            mod_copies(l)
            e.dma_start(kret[:], kr).then_inc(sem("ret_const"), 16)
            e.dma_start(rsm[:, 0:16], A["ret_decay_logit"].rearrange("l a h -> l (a h)").broadcast_to([128, 16])).then_inc(sem("ret_const"), 16)
            e.dma_start(rnorm[:].rearrange("p h v -> p (h v)"), A["ret_norm"].broadcast_to([128, RH * RV])).then_inc(sem("ret_const"), 16)
            e.wait_ge(sem("decay_in"), 1)
            S.activation(rsm[:, 32:48], rsm[:, 16:32], ACT.Exp).then_inc(sem("decay_exp"), 1)
            e.wait_ge(sem("log_decay"), 1)
            lgc = lambda d, h: rsm[:, 96 + 8 * d + h:97 + 8 * d + h]
            for h in range(RH):
                if h >= 2:
                    e.wait_ge(sem("mask_done"), h - 1)
                S.activation(rMT[:, h, :], kret[:, 0:128], ACT.Exp, scale=lgc(0, h)).then_inc(sem("mask_exp"), 1)
                S.activation(rof[:, h % 2, 0:128], kret[:, 256:384], ACT.Exp, scale=lgc(1, h)).then_inc(sem("mask_exp"), 1)
                S.activation(rdf[:, h, :], kret[:, 512:640], ACT.Exp, scale=lgc(0, h))
                S.activation(rdb[:, h, :], kret[:, 640:768], ACT.Exp, scale=lgc(1, h))
            S.activation(rsm[:, 112:120], rsm[:, 96:104], ACT.Exp, scale=kret[:, 768:769])
            S.activation(rsm[:, 120:128], rsm[:, 104:112], ACT.Exp, scale=kret[:, 769:770])
            S.activation(rsm[:, 128:144], rsm[:, 96:112], ACT.Exp, scale=128.0).then_inc(sem("mask_exp"), 1)
            st_in, st_out = A["state_ret"], O["new_state_ret"]
            e.wait_ge(sem("mask_done"), RH)
            with e.Fori(0, RH) as h:
                atleast(e, "ret_O_ps", h)
                e.dma_start(rs0[:], st_in[0, 0, :, ds(h, 1)].rearrange("a o k v -> k (a o) v")).then_inc(sem("state_in"), 16)
                e.wait_ge(sem("ret_qkv"), h + 1)
                for t in (0, 2):
                    S.activation(rqkv[:, t, :], ps[t][:], ACT.Copy).then_inc(sem("ret_in_sb"), 1)
                e.wait_ge(sem("ret_gate"), h + 1)
                S.activation(rg[:, 0:2, :], ps[3][:].rearrange("p (t v) -> p t v", t=2), ACT.Silu)
                S.activation(rg[:, 2, :], ps[4][:, 0:256], ACT.Silu).then_inc(sem("ret_gate_sb"), 1)
                e.wait_ge(sem("ret_T_ps"), h + 1)
                S.activation(rkT[:], ps[6][:, 0:T], ACT.Copy).then_inc(sem("ret_T_sb"), 1)
                e.wait_ge(sem("ret_U_ps"), h + 1)
                atleast(e, "state_stored", 16 * h)
                S.activation(rso[:], ps[5][:].rearrange("p (a v) -> p a v", a=2), ACT.Copy).then_inc(sem("ret_state_out"), 1)
                e.wait_ge(sem("ret_state_out"), h + 1)
                e.dma_start(st_out[0, 0, :, ds(h, 1)].rearrange("a o k v -> k (a o) v"), rso[:]).then_inc(sem("state_stored"), 16)
                for c in range(2):
                    e.wait_ge(sem("ret_yT_ps"), 2 * h + c + 1)
                    S.activation((yTe, yTo)[c][:, ds(h, 1), :].rearrange("p o t -> p (o t)"), ps[6 - c][:, 0:T], ACT.Copy)\
                        .then_inc(sem("ret_yT_sb"), 1)

        def route(l):
            n = 2 * l + 1
            e.wait_ge(sem("logit_parts_ps"), l + 1)
            S.activation(lpart[:], ps[2][:, 0:T], ACT.Copy).then_inc(sem("logit_parts"), 1)
            for t in range(TILES):
                e.wait_ge(sem("h_tok"), TILES * l + t + 1)
                S.activation(hhi[:, t, :], htok[:, t, :], ACT.Copy).then_inc(sem("h_hi"), 1)
            gate(n)
            e.wait_ge(sem("route_exp_in"), l + 1)
            S.activation(rt[:, 385:400], rt[:, 370:385], ACT.Exp).then_inc(sem("route_exp"), 1)

        def gathered_rows(z, r):
            e.wait_ge(sem(z + "_gather"), r + 1)
            atleast(e, z + "_hT", r)
            S.activation(hgt[0:CAP, 0:512], ps[0][0:CAP, :], ACT.Copy).then_inc(sem(z + "_hgt_act"), 1)

        def gathered_cols(z, r, q, j):
            atleast(e, z + "_hT", r + 1)
            atleast(e, z + "_gateup", q - 1)
            S.activation(hg[:, j % 2, 0:4, :], ps[0][:].rearrange("p (k s) -> p k s", k=4)[:, :, 0:CAP], ACT.Copy)\
                .then_inc(sem(z + "_hg_act"), 1)

        def slots(z, r, q, j, scatters):
            atleast(e, z + "_PT", r + 1)
            if scatters is not None:
                atleast(e, z + "_scatter", scatters)
            S.activation(PT[0:CAP, j % PER, :], ps[5][0:CAP, 0:T], ACT.Copy)
            atleast(e, z + "_act", q - 1)
            S.activation(gslot[0:CAP, j % 2, :], ps[5][0:CAP, T:T + 2], ACT.Copy).then_inc(sem(z + "_PT_sb"), 1)

        def first(z, P):
            r = P * (EXPERTS + 1)
            gathered_rows(z, r)
            gathered_cols(z, r, P * EXPERTS, 0)
            slots(z, r, P * EXPERTS, 0, 6 * GROUPS * P)

        def experts(z, P, g, ada):
            it = P * GROUPS + g
            for j in range(PER):
                x_ = g * PER + j
                q, r = P * EXPERTS + x_, P * (EXPERTS + 1) + x_
                atleast(e, z + "_gateup", q + 1)
                atleast(e, z + "_act", q)
                S.activation(silu[0:CAP, :], ps[2][0:CAP, 0:FE], ACT.Silu).then_inc(sem(z + "_silu"), 1)
                gathered_rows(z, r + 1)
                atleast(e, z + "_actT", q + 1)
                atleast(e, z + "_down", 2 * q)
                S.activation(actT[:], ps[3][:, 0:256].rearrange("p (c s) -> p c s", c=2)[:, :, 0:CAP], ACT.Copy)\
                    .then_inc(sem(z + "_actT_sb"), 1)
                if ada is not None:
                    ada_copy(ada + x_)
                for half in range(2):
                    atleast(e, z + "_down", 2 * q + half + 1)
                    S.activation(yhi[0:CAP, j, half * 512:half * 512 + 512], ps[6 + half][0:CAP, :], ACT.Copy)\
                        .then_inc(sem(z + "_y_hi"), 1)
                gathered_cols(z, r + 1, q + 1, j + 1)
                slots(z, r + 1, q + 1, j + 1, 6 * it + 6 if j == PER - 1 else None)

        for l in range(DEPTH):
            e.dma_start(wr[:, l, :, 0:4], A["moe_w_router_g"][l].rearrange("(k p) g -> p k g", p=128)).then_inc(sem("router_landed"), 16)
            e.dma_start(wr[:, l, :, 4:20], A["moe_w_router_e"][l].rearrange("(k p) g -> p k g", p=128)).then_inc(sem("router_landed"), 16)
            e.dma_start(rb[:, l, 0:4], A["moe_b_router_g"][l:l + 1, :].broadcast_to([128, 4])).then_inc(sem("router_landed"), 16)
            e.dma_start(rb[:, l, 4:20], A["moe_b_router_e"][l:l + 1, :].broadcast_to([128, 16])).then_inc(sem("router_landed"), 16)
        e.wait_ge(sem("vT_sb"), 1)
        S.activation(cond32[:, :, 0], vT[:, 80:88], ACT.Silu)
        S.activation(cond32[:, :, 1], vT[:, 88:96], ACT.Silu).then_inc(sem("cond_ready"), 1)
        with e.Fori(0, ADA_P) as i:
            ada_copy(i)
        passes = []
        for l in range(depth):
            norm(l, 0)
            gate(2 * l)
            if l % 3 == 0:
                attention(l)
            elif l % 3 == 1:
                e.dma_start(icnt[:], A["k_cnt"].rearrange("(o g) w -> o g w", o=1).broadcast_to([128, 4, PW])).then_inc(sem("count_landed"), 16)
                mod_copies(l)
            else:
                retention(l)
            norm(l, 1)
            route(l)
            e.wait_ge(sem("routed"), l + 1)
            nxt = (l + 1) * ADA_P if l + 1 < depth else None
            S.preload_act_table(ACT.Silu)
            expert_passes(e, first, lambda z, P, g: experts(z, P, g, nxt if z == "m" else None), passes, l)
        sum_squares(2 * depth)

    @block.gpsimd
    def _(pool):
        for name, c in CREDIT.items():
            pool.sem_inc(sem(name), c)

        def inverse_root(n):
            for t in range(TILES):
                pool.wait_ge(sem("msq"), TILES * n + t + 1)
                G.tensor_tensor(rstd[:, t:t + 1], msq[:, t:t + 1], hpow[:, 0:1], ALU.pow).then_inc(sem("rstd"), 1)

        def experts(z, it):
            for m in range(2 * TILES):
                t, half = m // 2, m % 2
                o = slice(half * 512, half * 512 + 512)
                atleast(pool, z + "_term", 6 * it + m + 1)
                G.tensor_tensor(x[:, t, o], x[:, t, o], tmp[:, m % 2, :], ALU.add).then_inc(sem(z + "_added"), 1)

        passes = []
        G.memset(wr[:, :, :, 20:32], 0.0)
        G.memset(gates_r[:, :, EXPERTS:EXPERTS + 1, :].bitcast(F), 0.0)
        G.memset(rankm[:, :, EXPERTS:EXPERTS + 1], -1.0).then_inc(sem("router_pad"), 1)
        pool.wait_ge(sem("const_landed"), 16)
        for l in range(depth):
            a = l // 3
            inverse_root(2 * l)
            if l % 3 == 0:
                for i, (h0, h1) in enumerate(((0, 4), (4, 8), (8, NQK))):
                    pool.wait_ge(sem("qk_ms"), 3 * a + i + 1)
                    G.tensor_tensor(stat[:, 64 + 3 * h0:64 + 3 * h1], stat[:, 32 + 3 * h0:32 + 3 * h1],
                                    hpow[:, 0:3 * (h1 - h0)], ALU.pow).then_inc(sem("qk_rstd"), 1)
            elif l % 3 == 1:
                for lo, hi in ((0, POFF[0]), (POFF[0] + SEQ, POFF[1]), (POFF[1] + DEC, PW)):
                    last = G.memset(hp[:, :, lo:hi], 0.0)
                last.then_inc(sem("pool_pads"), 1)
            else:
                with pool.Fori(0, RH) as h:
                    pool.wait_ge(sem("ret_var"), h + 1)
                    G.tensor_tensor(rsm[:, 176:179], rsm[:, 172:175], hpow[:, 0:3], ALU.pow).then_inc(sem("ret_rstd"), 1)
            for m in range(2 * TILES):
                half, t = m // TILES, m % TILES
                o = slice(half * 512, half * 512 + 512)
                pool.wait_ge(sem("mix_term"), 6 * l + m + 1)
                G.tensor_tensor(x[:, t, o], x[:, t, o], tmp[:, m % 2, :], ALU.add).then_inc(sem("mix_added"), 1)
            inverse_root(2 * l + 1)
            for t in range(2):
                pool.wait_ge(sem("h_hi"), TILES * l + t + 1)
                G.tensor_tensor(hlo[:, t, :], htok[:, t, :], hhi[:, t, :].bitcast(F), ALU.subtract).then_inc(sem("h_lo"), 1)
            pool.wait_ge(sem("routed"), l + 1)
            expert_passes(pool, lambda z, P: None, lambda z, P, g: experts(z, P * GROUPS + g), passes, l)
            pool.drain().then_inc(sem("layer_done"), 1)
        inverse_root(2 * depth)

    ctx.close()


_INS = ["x_prompt", "x_sample", "cache_k", "cache_v", "state_ret", "w_ada", "b_ada", "attn_w_qkv", "attn_q_norm",
        "attn_k_norm", "attn_w_o", "pool_w", "ret_w_in", "ret_decay_logit", "ret_norm", "ret_w_out",
        "moe_w_router_g", "moe_b_router_g", "moe_w_router_e", "moe_b_router_e", "moe_w_gate", "moe_w_up", "moe_w_down"]
_OUTS = {"y_prompt": (1, SEQ, D), "y_sample": (1, DEC, D), "new_cache_k": (1, 2, SEQ, KV, HD),
         "new_cache_v": (1, 2, SEQ, KV, HD), "new_state_ret": (1, 1, 2, RH, RK, RV)}


def kernel(**inputs):
    import concourse.bacc as bacc
    from concourse import mybir
    from concourse.bass_utils import run_bass_kernel_spmd as run

    nc = bacc.Bacc("TRN2", target_bir_lowering=False, num_devices=1)
    arrays = {n: np.ascontiguousarray(inputs[n]) for n in _INS}
    arrays["vectors"] = np.concatenate([np.asarray(inputs[n]).reshape(-1, 128) for n in
                                        ("norm1", "norm2", "pool_scale", "norm_f", "c_ctx", "c")])
    arrays.update(shape_constants())
    feeds, A, O = {}, {}, {}
    for n, a in arrays.items():
        feeds["in_" + n] = a
        A[n] = nc.dram_tensor("in_" + n, a.shape, mybir.dt.from_np(a.dtype), kind="ExternalInput").ap()
    for n, shape in _OUTS.items():
        O[n] = nc.dram_tensor("out_" + n, shape, mybir.dt.float32, kind="ExternalOutput").ap()
    build_trunk(nc, A, O)
    r = run(nc, [feeds], core_ids=[0])
    return tuple(r.results[0]["out_" + n] for n in _OUTS)
```

```python
from contextlib import ExitStack

import numpy as np

D = 1024
KD = D // 128
SEQ, DEC, PAST = 128, 256, 128
TILES = (SEQ + DEC) // 128
T = TILES * 128
COND = (0, 1, 1)
DEPTH = 4
HEADS, KV, HD = 8, 2, 128
NQKV = (HEADS + 2 * KV) * HD
NQK = HEADS + KV
RH, RK, RV = 8, 128, 256
GROUPS, PER = 4, 4
EXPERTS = GROUPS * PER
FE = 256
CAP = 64
SLOTS = 2 * CAP
PAIRS = EXPERTS // 2
MAIN, MORE = 4, 2
MAIN_GROUPS = PAIRS // MAIN
MORE_GROUPS = -(-((2 * T - 1) // CAP) // (2 * MORE))
UNITS = 2 * MORE * MORE_GROUPS + 2
EPS = 1e-6
ADA_N = 384
ADA_P = 6 * D // ADA_N
PAD = 8
PW = PAD + SEQ + PAD + PAD + DEC + PAD
POFF = (PAD, 3 * PAD + SEQ, 3 * PAD + SEQ + 128)
WINDOWS = (2, 4, 8, 16)


def shape_constants():
    p = np.arange(128, dtype=np.float32)
    ident = np.eye(128, dtype=np.float32)
    tri = (p[:, None] < p[None, :]).astype(np.float32)
    iota = np.broadcast_to(p, (128, 128))
    sel = (p[:, None] % 32 == np.arange(2)[None, :]).astype(np.float32)
    tie = np.broadcast_to(np.float32(4) - np.arange(4, dtype=np.float32), (128, 4))
    caps = np.broadcast_to(2 * MORE * np.arange(MORE_GROUPS, dtype=np.float32), (128, MORE_GROUPS))
    past = CAP * (p // EXPERTS + 1)
    unit = np.stack([past, p % EXPERTS, past - 4096], axis=1)
    halfpow = np.full((128, 32), -0.5, np.float32)
    quad = (p[:, None] % 32 == np.arange(32)[None, :]).astype(np.float32)
    base = np.concatenate([ident, tri, iota, sel, tie, caps, halfpow, quad, unit], axis=1).astype(np.float32)
    j, i = p[:, None], p[None, :]
    scale = np.float32(RK ** -0.5)
    ret = np.concatenate([np.maximum(i - j, 0), (i >= j) * scale, np.maximum(j - i, 0), (j >= i) * scale,
                          np.broadcast_to(i + 1, (128, 128)), np.broadcast_to(128 - i, (128, 128)),
                          127 - j, j], axis=1).astype(np.float32)
    nf = HD // 4
    inv = np.float32(10000.0) ** (-np.arange(nf, dtype=np.float32) / np.float32(nf))
    t = np.arange(DEC)
    ang = np.stack([(t // 64).astype(np.float32)[:, None] * inv, (t % 64).astype(np.float32)[:, None] * inv], 1)
    cos, sin = np.cos(ang).astype(np.float32), np.sin(ang).astype(np.float32)
    rope = np.stack([np.stack([cos, cos], 2), np.stack([-sin, sin], 2)], 1).reshape(2, 128, 2 * 128)
    rope = np.ascontiguousarray(rope.transpose(1, 0, 2))
    cnt = np.ones((4, PW), np.float32)
    for g, win in enumerate(WINDOWS):
        for off, n in ((POFF[0], SEQ), (POFF[1], DEC)):
            s = np.arange(n)
            cnt[g, off:off + n] = np.clip(s + win - win // 2, 0, n) - np.clip(s - win // 2, 0, n)
    return {"k_base": base, "k_ret": ret, "k_rope": rope, "k_cnt": (np.float32(1) / cnt)}


def build_trunk(nc, A, O, depth=DEPTH):
    import concourse.bass as bass
    from concourse import mybir

    F, R, I32 = mybir.dt.float32, mybir.dt.float32r, mybir.dt.int32
    ALU, ACT, AX = mybir.AluOpType, mybir.ActivationFunctionType, mybir.AxisListType
    ds = bass.ds
    PE, V, S, G = nc.tensor, nc.vector, nc.scalar, nc.gpsimd

    size = lambda shape: 4 * int(np.prod(shape))
    top = [-(-nc.sbuf_base // 64) * 64]

    def place(name, shape, dt=F, at=None):
        off = top[0] if at is None else at
        if at is None:
            top[0] = off + -(-size(shape) // 32) * 32
        return nc.alloc_sbuf_tensor_at(name, [128] + list(shape), dt, offset=off), off + -(-size(shape) // 32) * 32

    def keep(name, shape, dt=F):
        return place(name, shape, dt)[0]

    x = keep("x", [TILES, D])
    gu_ring = [keep(f"gate_up_weights{i}", [KD, 2 * FE]) for i in range(2)]
    dn_at = top[0]
    dn_ring = [keep(f"down_weights{i}", [2, D]) for i in range(2)]
    panel = [keep(f"panel{i}", [KD, 512]) for i in range(2)]
    gate_bc = keep("gate_bc", [2, D])
    tmp = keep("residual_term", [2, 512])
    mraw = keep("ada_raw", [48, 2])
    mods = keep("mods", [48, 2])
    kb = keep("const_base", [3 * 128 + 2 + 4 + MORE_GROUPS + 64 + 3])
    vecs = keep("vector_rows", [3, 128])
    vT = keep("vectors", [96 + 192])
    cond32 = keep("cond_columns", [KD, 32])
    wr = keep("router_weights", [DEPTH, KD, 32])
    rb = keep("router_bias", [DEPTH, 20])
    mpan = keep("ada_panel_rows", [ADA_N])
    ssq = keep("sum_squares", [4])
    msq = keep("mean_squares", [4])
    rstd = keep("rstd", [4])
    rankm = keep("rank_in_expert", [TILES, EXPERTS + 2])
    gates_r = keep("gates_pair", [TILES, EXPERTS + 2, 2], R)
    extra = keep("more_groups", [4], I32)
    unit_ids = keep("unit_experts", [DEPTH, UNITS], I32)
    ones = keep("ones", [128])
    mod_at = top[0]
    mod_bc = keep("mod_bc", [4, D])
    lpart = keep("logit_parts", [T])
    rt = keep("route_scratch", [480])
    base = top[0]

    def region(*items, start=base):
        out, at = [], start
        for name, shape, *dt in items:
            t, at = place(name, shape, *(dt or [F]), at=at)
            out.append(t)
        assert at <= nc.sbuf_usable_end, (at, nc.sbuf_usable_end)
        return out, at

    (xn, hT), mix0 = region(("xn", [TILES, D]), ("hT", [KD, T]))
    (qkv, kT, ckv, rope, gqk, stat), att0 = region(
        ("qkv", [TILES, NQKV]), ("kT", [KV, 512]), ("cache_rows", [2, KV * HD]), ("rope_tab", [2, 256]),
        ("qk_gain", [NQK * HD]), ("attn_stat", [96]), start=mix0)
    (prob, probT), _ = region(("prob", [2, 896]), ("probT", [2, 896]), start=att0)
    (sqv, ropet), _ = region(("qk_sq", [NQK * HD]), ("rope_t", [NQK * HD]), start=att0)
    (oT, qT), _ = region(("oT", [HEADS, T]), ("qT", [HEADS, T]))
    (hp, win_a, win_b, uT, icnt), _ = region(("h_padded", [KD, PW]), ("win_a", [2, PW]), ("win_b", [2, PW]),
                                            ("pool_u", [KD, PW]), ("inv_count", [4, PW]), start=mix0)
    (yTo, rqkv, rg, rkd, rqT, rkT, rqf, rqb, rST, rs0, rs1, rso, rof, rMT, kret,
     rsm), _ = region(
        ("yT_odd", [RH, T]), ("ret_qkv_sb", [TILES, 512]), ("ret_gate", [TILES, RV]), ("ret_k_decayed", [4, RK]), ("ret_qT", [T]), ("ret_kT", [T]),
        ("ret_q_fwd", [2, 128]), ("ret_q_bwd", [2, 128]), ("ret_scoresT", [TILES, 128]),
        ("ret_state_in", [2, RV]), ("ret_state_mid", [2, RV]), ("ret_state_out", [2, RV]),
        ("ret_o", [TILES, RV]), ("ret_mask", [RH, 128]), ("k_ret_sb", [6 * 128 + 2]), ("ret_small", [192]), start=mix0)
    rq, rk, rv = rqkv[:, :, 0:RK], rqkv[:, :, RK:2 * RK], rqkv[:, :, 2 * RK:512]
    (rnorm, rdf, rdb), dn_end = region(("ret_gain", [RH, RV]), ("ret_dec_f", [RH, 128]), ("ret_dec_b", [RH, 128]),
                                       start=dn_at)
    assert dn_end <= dn_at + 2 * size([2, D])
    (yTe,), _ = region(("yT_even", [RH, T]))
    (yhi, ylo, PT), moe0 = region(("y_hi", [MAIN, D], R), ("y_lo", [MAIN, D], R), ("PT", [MAIN, T], R))
    (htok,), _ = region(("h_tok", [TILES, D]), start=mix0)
    assert moe0 - base >= 3 * size([TILES, D])
    (hhi, hlo, Pm, silu, act, actT, gsum, gslot, uhot, uoff, ue, rank_u, gates_u), _ = region(
        ("h_hi", [TILES, D], R), ("h_lo", [TILES, D], R), ("P", [2, TILES, SLOTS], R),
        ("silu", [FE]), ("act", [FE]), ("actT", [2, SLOTS]), ("gate_slot", [1]),
        ("gate_pair", [2, 2, 2]), ("unit_one_hot", [UNITS + 2]), ("unit_offset", [UNITS]),
        ("unit_expert_hot", [UNITS, EXPERTS]), ("unit_rank", [TILES, UNITS]),
        ("unit_gates", [TILES, UNITS, 2], R), start=moe0)
    wide = lpart[:, 0:T].rearrange("p (t c) -> p t c", t=TILES)
    uprod = lpart[:, 0:UNITS * EXPERTS].rearrange("p (u e) -> p u e", e=EXPERTS)
    (hgt, hg), hg_end = region(("h_gathered", [D]), ("hT_gathered", [2, KD, SLOTS]), start=mod_at)
    assert hg_end <= mod_at + size([4, D])
    (ofin,), _ = region(("y_final", [TILES, D]), start=mix0)

    ident, tri, iota = kb[:, 0:128], kb[:, 128:256], kb[:, 256:384]
    sel = kb[:, 384:386]
    tie = kb[:, 386:390]
    c0 = 390 + MORE_GROUPS
    caps, hpow, quad = kb[:, 390:c0], kb[:, c0:c0 + 32], kb[:, c0 + 32:c0 + 64]
    past, expert_of, past_less = (kb[:, c0 + 64 + i:c0 + 65 + i] for i in range(3))
    biasT = vT[:, 96:288]

    ps = [nc.alloc_psum_tensor(f"bank{i}", [128, 512], F) for i in range(8)]
    sems = {}

    def sem(name):
        if name not in sems:
            sems[name] = nc.alloc_semaphore(name)
        return sems[name]

    ring4 = panel + gu_ring
    panels = [("ada", 0, i) for i in range(ADA_P) if i % 4 < 2]
    in_heads = lambda l: l == 0 and depth > 1
    in_retention = lambda l: l % 3 == 2 and l + 1 < depth
    early = lambda l: in_heads(l) or in_retention(l)
    first_panel = {("ada", 0): 0}
    prj_base = {}
    prj = 0
    for l in range(depth):
        kind = l % 3
        first_panel["mix", l] = len(panels)
        prj_base[l] = prj
        if kind == 0:
            panels += [("attn", l, i) for i in range(3)]
            if in_heads(l):
                first_panel["ada", l + 1] = len(panels)
                panels += [("ada", l + 1, i) for i in range(ADA_P)]
            first_panel["out", l] = len(panels)
            panels += [("attn", l, i) for i in range(3, 5)]
            prj += 5 * TILES
        elif kind == 1:
            panels += [("pool", l, 0)]
            prj += 2 * TILES
        else:
            panels += [("ret", l, i) for i in range(2 * RH)] + [("rout", l, i) for i in range(4)]
            prj += 2 * TILES
        first_panel["end", l] = len(panels)
        if l + 1 < depth and not early(l):
            first_panel["ada", l + 1] = len(panels)
            panels += [("ada", l + 1, i) for i in range(ADA_P)]

    def released(s):
        kind, l, i = panels[s]
        if kind == "ada":
            return sem("ada_product"), l * ADA_P + i + 1
        if kind == "attn":
            return sem("proj_done"), prj_base[l] + TILES * (i + 1)
        if kind == "pool":
            return sem("proj_done"), prj_base[l] + 2 * TILES
        if kind == "ret":
            return (sem("ret_qkv"), i // 2 + 1) if i % 2 == 0 else (sem("ret_gate"), i // 2 + 1)
        return sem("proj_done"), prj_base[l] + (TILES if i < 2 else 2 * TILES)

    def slot_of(s):
        return s % 2

    def panel_landed(eng, s, i=0, per=0):
        eng.wait_ge(sem(f"panel_landed{s % 2}"), 48 * (s // 2 + 1) + i * (48 * per // 2))

    ada_w = A["w_ada"].rearrange("l (k p) n -> l p k n", p=128)
    qkv_w = A["attn_w_qkv"].rearrange("l (k p) n -> l p k n", p=128)
    wo_w = A["attn_w_o"].rearrange("l (k p) n -> l p k n", p=128)
    rin_w = A["ret_w_in"].rearrange("l (k p) n -> l p k n", p=128)
    rout_w = A["ret_w_out"].rearrange("l (k p) n -> l p k n", p=128)
    wg_w = A["moe_w_gate"].rearrange("l e (k p) f -> l e p k f", p=128)
    wu_w = A["moe_w_up"].rearrange("l e (k p) f -> l e p k f", p=128)
    wd_w = A["moe_w_down"].rearrange("l e (c p) n -> l e p c n", p=128)

    CREDIT = {"ada_evac": 1, "ada_col": 1, "ada_mod": 1}
    if depth > 2:
        CREDIT.update(ret_in_sb=1, ret_gate_sb=1, ret_yT_sb=1, ret_O_ps=1, state_stored=16)
    for z in ("m", "o"):
        CREDIT.update({z + "_hg_act": 1, z + "_hg_dve": 1, z + "_hT": 1, z + "_act": 2, z + "_PT_sb": 1, z + "_actT_sb": 1,
                       z + "_actT": 1, z + "_scatter": 1, z + "_term": 1, z + "_PT": 2, z + "_gateup": 2, z + "_gateup_half": 1,
                       z + "_down": 4, z + "_y_hi": 1, z + "_y_lo": 1, z + "_added": 2})
    for n in CREDIT:
        sem(n)

    def atleast(eng, name, n):
        eng.wait_ge(sem(name), n + CREDIT.get(name, 0))

    class Order:

        def __init__(self, eng, name):
            self.eng, self.sem, self.n, self.base = eng, sem(name), 0, 0

        def __call__(self, ins):
            self.n += 1
            ins.then_inc(self.sem, 1)
            self.eng.wait_ge(self.sem, self.base + self.n)

        def enter(self, i, per):
            self.kept, self.per = self.n, per
            self.base, self.n = i * per + self.n, 0

        def leave(self, times):
            assert self.n == self.per, (self.n, self.per)
            self.n, self.base = self.kept + times * self.per, 0

    block = nc.Block()
    ctx = ExitStack()
    ctx.enter_context(block)

    def load_panel(sp, s, src_of, i=0, per=0):
        dst = panel[s % 2]
        parts = src_of(dst)
        for n, (d, a) in enumerate(parts):
            sp.dma_start(d, a).then_inc(sem(f"panel_landed{s % 2}"), 48 - 16 * (len(parts) - 1) if n == 0 else 16)

    def panel_source(kind, l, i):
        a = l // 3
        if kind == "ada":
            return lambda d: [(d[:, :, 0:ADA_N], ada_w[l, :, :, ds(i * ADA_N, ADA_N)])]
        if kind == "attn" and not isinstance(i, int) or kind == "attn" and i < 3:
            return lambda d: [(d[:, :, :], qkv_w[a, :, :, i * 512:(i + 1) * 512])]
        if kind == "attn":
            return lambda d: [(d[:, :, :], wo_w[a, :, :, (i - 3) * 512:(i - 2) * 512])]
        if kind == "pool":
            pw = A["pool_w"][a].rearrange("g (c p) n -> p (g c) n", p=128)
            return lambda d: [(d[:, :, 0:256], pw)]
        if kind == "rout":
            return lambda d: [(d[:, :, :], rout_w[0, :, (i % 2) * 8:(i % 2) * 8 + 8, (i // 2) * 512:(i // 2) * 512 + 512])]
        raise ValueError(kind)

    def ret_qkv_source(h):
        return lambda d: [(d[:, :, 0:RK], rin_w[0, :, :, ds(h * RK, RK)]),
                          (d[:, :, RK:2 * RK], rin_w[0, :, :, ds(h * RK + RH * RK, RK)]),
                          (d[:, :, 2 * RK:512], rin_w[0, :, :, ds(h * RV + 2 * RH * RK, RV)])]

    def ret_gate_source(h):
        return lambda d: [(d[:, :, 0:RV], rin_w[0, :, :, ds(h * RV + 2 * RH * RK + RH * RV, RV)])]

    def at_e(w, l, e):
        return w[l, e] if isinstance(e, int) else w[l, ds(e, 1)].rearrange("o p k f -> (o p) k f")

    def load_expert(sp, z, l, e, slot, half):
        k = slice(half * KD // 2, (half + 1) * KD // 2)
        sp.dma_start(gu_ring[slot][:, k, 0:FE], at_e(wg_w, l, e)[:, k, :]).then_inc(sem(f"{z}_gu{half}_landed"), 16)
        sp.dma_start(gu_ring[slot][:, k, FE:2 * FE], at_e(wu_w, l, e)[:, k, :]).then_inc(sem(f"{z}_gu{half}_landed"), 16)

    def load_down(sp, z, l, e, slot):
        sp.dma_start(dn_ring[slot][:], at_e(wd_w, l, e)).then_inc(sem(f"{z}_dn_landed{slot}"), 16)

    def load_pair(sp, z, l, e0, e1, read=None):
        for half in range(2):
            if read is not None:
                sp.wait_ge(sem(z + ("_gateup_half", "_gateup")[half]), read + CREDIT[z + ("_gateup_half", "_gateup")[half]])
            load_expert(sp, z, l, e0, 0, half)
            load_expert(sp, z, l, e1, 1, half)

    def load_pair_down(sp, z, l, e0, e1):
        load_down(sp, z, l, e0, 0)
        load_down(sp, z, l, e1, 1)

    @block.sync
    def _(sp):
        sp.dma_start(vecs[0:96, 0, :], A["vectors"]).then_inc(sem("vec_landed"), 16)
        sp.dma_start(vecs[0:96, 1:3, :], A["b_ada"].rearrange("l (c n) -> (l c) n", n=128)
                     .rearrange("(a r) n -> r a n", a=2)).then_inc(sem("vec_landed"), 16)
        sp.dma_start(kb[:], A["k_base"]).then_inc(sem("const_landed"), 16)
        passes = []
        def load_beside(l, j, i):
            d, a = panel_source("ada", l, i)(ring4[j])[0]
            sp.dma_start(d, a).then_inc(sem(f"panel_landed{j}" if j < 2 else f"ada_landed{j}"), 48)

        for j in range(4):
            load_beside(0, j, j)
        sp.dma_start(x[:, 0, :], A["x_prompt"][0]).then_inc(sem("x_landed"), 16)
        sp.dma_start(x[:, 1:3, :], A["x_sample"][0].rearrange("(a p) n -> p a n", p=128)).then_inc(sem("x_landed"), 16)
        with sp.Fori(1, ADA_P // 4) as i:
            for j in range(4):
                sp.wait_ge(sem("ada_product"), 4 * i + j - 3)
                load_beside(0, j, 4 * i + j)
        for l in range(depth):
            f = first_panel["mix", l]
            n = first_panel["end", l] - f
            if l % 3 == 2:
                for s in (f, f + 1):
                    sp.wait_ge(*released(s - 2))
                    load_panel(sp, s, ret_qkv_source(0) if s == f else ret_gate_source(0))
            else:
                for s in range(f, f + min(n, 2)):
                    sp.wait_ge(*released(s - 2))
                    load_panel(sp, s, panel_source(*panels[s]))
            if l:
                sp.wait_ge(sem("experts_read"), l)
            else:
                sp.wait_ge(sem("ada_product"), ADA_P)
            if in_retention(l):
                for j in range(2):
                    load_beside(l + 1, 2 + j, j)
            else:
                load_pair(sp, "m", l, 0, 1)
            if l % 3 != 2:
                load_pair_down(sp, "m", l, 0, 1)
            if l % 3 == 2:
                with sp.Fori(0, RH - 1) as h:
                    sp.wait_ge(sem("ret_qkv"), h + 1)
                    load_panel(sp, f, ret_qkv_source(h + 1))
                    sp.wait_ge(sem("ret_gate"), h + 1)
                    load_panel(sp, f + 1, ret_gate_source(h + 1))
                    if in_retention(l):
                        for j in range(2):
                            sp.wait_ge(sem("ada_product"), (l + 1) * ADA_P + 2 * h + j + 1)
                            load_beside(l + 1, 2 + j, 2 * h + j + 2)
                rest = range(f + 2 * RH, f + n)
            else:
                rest = range(f + min(n, 2), f + n)
            if in_heads(l):
                a0 = first_panel["ada", l + 1]
                for s in range(f + 2, a0 + 2):
                    sp.wait_ge(*released(s - 2))
                    load_panel(sp, s, panel_source(*panels[s]))
                with sp.Fori(1, ADA_P // 2) as i:
                    for j in range(2):
                        sp.wait_ge(sem("ada_product"), (l + 1) * ADA_P + 2 * i + j - 1)
                        load_panel(sp, a0 + j, panel_source("ada", l + 1, 2 * i + j))
                rest = range(a0 + ADA_P, f + n)
            for s in rest:
                sp.wait_ge(*released(s - 2))
                load_panel(sp, s, panel_source(*panels[s]))
            if in_retention(l):
                sp.wait_ge(sem("ada_product"), (l + 2) * ADA_P)
                load_pair(sp, "m", l, 0, 1)
            if l % 3 == 2:
                sp.wait_ge(sem("ret_y"), RH)
                load_pair_down(sp, "m", l, 0, 1)
            nxt = l + 1 < depth and not early(l)
            a0 = first_panel["ada", l + 1] if nxt else 0
            if nxt:
                for j in range(2):
                    sp.wait_ge(*released(a0 + j - 2))
                    load_panel(sp, a0 + j, panel_source("ada", l + 1, j))
            with sp.Fori(1, PAIRS) as i:
                load_pair(sp, "m", l, 2 * i, 2 * i + 1, l * PAIRS + i)
                if nxt:
                    sp.wait_ge(sem("ada_product"), (l + 1) * ADA_P + 2 * i - 1)
                    load_panel(sp, a0, panel_source("ada", l + 1, 2 * i))
                sp.wait_ge(sem("m_down"), CREDIT["m_down"] + 2 * (l * PAIRS + i))
                load_pair_down(sp, "m", l, 2 * i, 2 * i + 1)
                if nxt:
                    sp.wait_ge(sem("ada_product"), (l + 1) * ADA_P + 2 * i)
                    load_panel(sp, a0 + 1, panel_source("ada", l + 1, 2 * i + 1))
            sp.wait_ge(sem("routed"), l + 1)
            r = sp.value_load(extra[0:1, l:l + 1], min_val=0, max_val=MORE_GROUPS)
            done = sum(passes) if passes else 0
            for p in range(MORE_GROUPS):
                with sp.If(r > p):
                    if p == 0:
                        sp.wait_ge(sem("m_gateup"), CREDIT["m_gateup"] + (l + 1) * PAIRS)
                    for j in range(MORE):
                        u = 2 * (p * MORE + j)
                        e0, e1 = (sp.value_load(unit_ids[0:1, l, u + i:u + i + 1], min_val=0, max_val=EXPERTS - 1)
                                  for i in range(2))
                        q = (done + p) * MORE + j
                        load_pair(sp, "o", l, e0, e1, q)
                        if p == 0 and j == 0:
                            sp.wait_ge(sem("m_down"), CREDIT["m_down"] + 2 * (l + 1) * PAIRS)
                        atleast(sp, "o_down", 2 * q)
                        load_pair_down(sp, "o", l, e0, e1)
            passes.append(r)
        for t in range(TILES):
            sp.wait_ge(sem("final_ready"), t + 1)
            dst = O["y_prompt"][0] if t == 0 else O["y_sample"][0, (t - 1) * 128:t * 128]
            sp.dma_start(dst, ofin[:, t, :]).then_inc(sem("stored"), 16)
        sp.wait_ge(sem("stored"), 16 * TILES)
        sp.wait_ge(sem("cache_stored"), 32 * ((depth + 2) // 3))
        if depth > 2:
            atleast(sp, "state_stored", 16 * RH)

    def pe_norm(pe, n):
        pe.wait_ge(sem("xn_ready"), TILES * (n + 1))
        for k in range(KD):
            if k >= 4:
                pe.wait_ge(sem(("hT_dve", "hT_act")[k % 2]), KD // 2 * n + (k - 4) // 2 + 1)
            for t in range(TILES):
                last = PE.transpose(ps[k % 4][:, t * 128:(t + 1) * 128], xn[:, t, k * 128:(k + 1) * 128], ident)
            last.then_inc(sem("hT_ps"), 1)

    def pe_broadcast(bank, v, c, half):
        for q in range(4):
            last = PE.matmul(ps[bank][:, q * 128:(q + 1) * 128],
                             mods[:, v * KD + 4 * half + q, c:c + 1].broadcast_to([128, 128]), ident,
                             start=True, stop=True)
        return last

    def pe_gate_bc(pe, n, v):
        for c in range(2):
            for half in range(2):
                pe_broadcast(4 + 2 * c + half, v, c, half).then_inc(sem("gate_ps"), 1)

    def pe_mod_bc(pe, l):
        for i in range(8):
            if i >= 4:
                pe.wait_ge(sem("mod_bc"), 8 * l + i - 3)
            pe_broadcast(4 + i % 4, (4, 3)[i // 4], (i // 2) % 2, i % 2).then_inc(sem("mod_ps"), 1)

    def pe_ada_product(pe, idx, src, bank=4):
        atleast(pe, "ada_evac", idx)
        atleast(pe, "ada_mod", idx)
        for kk in range(2):
            for g in range(4):
                last = PE.matmul(ps[bank][32 * g:32 * g + 32, 0:ADA_N], cond32[:, 2 * g + kk, :],
                                 src[:, 2 * g + kk, 0:ADA_N], start=kk == 0, stop=kk == 1)
        last.then_inc(sem("ada_product"), 1)

    def pe_ada_columns(pe, idx, bank=4):
        atleast(pe, "ada_evac", idx + 1)
        for c in range(ADA_N // 128):
            last = PE.matmul(ps[bank][:, ADA_N + 2 * c:ADA_N + 2 * c + 2], mpan[:, c * 128:(c + 1) * 128], sel, start=True, stop=True)
        last.then_inc(sem("ada_col"), 1)

    def pe_project(pe, l, i, s, nk, lhs, bank0, group=0, rhs_k=None, start=True, stop=True, signal=True):
        for t in range(TILES):
            for k in range(nk):
                last = PE.matmul(ps[bank0 + t][:], lhs(k, t), panel[s % 2][:, k, :],
                                 start=start and k == 0, stop=stop and k == nk - 1)
            if signal:
                last.then_inc(sem("proj_done"), 1)
        return last

    def pe_attention(pe, l):
        f, a = first_panel["mix", l], l // 3
        def turn(heads, banks):
            for h in heads:
                b = ps[banks[h % len(banks)]]
                done = NQK * a + h
                if h - heads[0] >= len(banks):
                    pe.wait_ge(sem("qkT_sb"), done + 1 - len(banks))
                for t in range(TILES):
                    last = PE.transpose(b[:, t * 128:(t + 1) * 128], qkv[:, t, h * HD:(h + 1) * HD], ident)
                if h >= HEADS:
                    last = PE.transpose(b[:, 384:512], ckv[:, 0, (h - HEADS) * HD:(h - HEADS + 1) * HD], ident)
                last.then_inc(sem("qkT_ps"), 1)

        pe.wait_ge(sem("hT_dve"), KD // 2 * (2 * l + 1))
        pe.wait_ge(sem("hT_act"), KD // 2 * (2 * l + 1))
        for i in range(3):
            panel_landed(pe, f + i)
            if i == 1:
                pe.wait_ge(sem("gate_bc"), 4 * (2 * l + 1))
            if i == 2:
                pe.wait_ge(sem("qkv_sb"), 9 * a + 3)
            pe_project(pe, l, i, f + i, KD, lambda k, t: hT[:, k, t * 128:(t + 1) * 128], (0, 4, 0)[i])
        pe.wait_ge(sem("qkv_sb"), 9 * a + 6)
        pe_mod_bc(pe, l)
        pe.wait_ge(sem("mod_bc"), 8 * (l + 1))
        pe.wait_ge(sem("cache_landed"), 32 * (a + 1))
        pe.wait_ge(sem("qk_ready"), 3 * TILES * a + 2 * TILES)
        turn(range(0, HEADS), (4, 5, 6, 7))
        pe.wait_ge(sem("qk_ready"), 3 * TILES * (a + 1))
        turn(range(HEADS, NQK), (0, 1))
        pe.wait_ge(sem("qkT_sb"), NQK * (a + 1))

        def scores(h):
            b0, g = 2 * (h % 2), h // (HEADS // KV)
            if h >= 2:
                pe.wait_ge(sem("prob"), 3 * (HEADS * a + h - 1))
            PE.matmul(ps[b0][:, 0:128], qT[:, h, 0:128], kT[:, g, 0:128], start=True, stop=True)
            PE.matmul(ps[b0][:, 128:512], qT[:, h, 128:256], kT[:, g, 128:512], start=True, stop=True)
            PE.matmul(ps[b0 + 1][:, 0:384], qT[:, h, 256:384], kT[:, g, 128:512], start=True, stop=True)\
                .then_inc(sem("scores"), 1)

        def turn_probs(h):
            n = HEADS * a + h
            pe.wait_ge(sem("prob_norm"), n + 1)
            if h:
                pe.wait_ge(sem("probT_sb"), 2 * n)
            for c in range(7):
                last = PE.transpose(ps[4 + c // 4][:, (c % 4) * 128:(c % 4) * 128 + 128],
                                    prob[:, h % 2, c * 128:(c + 1) * 128], ident)
                if c in (3, 6):
                    last.then_inc(sem("probT_ps"), 1)

        def outputs(h):
            g = h // (HEADS // KV)
            n = HEADS * a + h
            pe.wait_ge(sem("probT_sb"), 2 * (n + 1))
            if h:
                pe.wait_ge(sem("oT_sb"), n)
            v = lambda t: qkv[:, t, (NQK + g) * HD:(NQK + g + 1) * HD]
            cv = ckv[:, 1, g * HD:(g + 1) * HD]
            b = ps[6]
            PE.matmul(b[:, 0:128], v(0), probT[:, h % 2, 0:128], start=True, stop=True)
            for t in (1, 2):
                for c, vals in enumerate((cv, v(1), v(2))):
                    at = 128 + (t - 1) * 384 + c * 128
                    last = PE.matmul(b[:, t * 128:(t + 1) * 128], vals, probT[:, h % 2, at:at + 128],
                                     start=c == 0, stop=c == 2)
            last.then_inc(sem("oT_ps"), 1)

        scores(0)
        scores(1)
        turn_probs(0)
        idx, s = (l + 1) * ADA_P, first_panel.get(("ada", l + 1))
        for h in range(HEADS):
            if h + 2 < HEADS:
                scores(h + 2)
            if in_heads(l):
                panel_landed(pe, s + 2 * h)
                pe_ada_product(pe, idx + 2 * h, panel[(s + 2 * h) % 2], 7)
            if h + 1 < HEADS:
                turn_probs(h + 1)
            if in_heads(l):
                pe_ada_columns(pe, idx + 2 * h, 7)
                panel_landed(pe, s + 2 * h + 1)
                pe_ada_product(pe, idx + 2 * h + 1, panel[(s + 2 * h + 1) % 2], 7)
            outputs(h)
            if in_heads(l):
                pe_ada_columns(pe, idx + 2 * h + 1, 7)
        for i in range(3, 5):
            s = first_panel["out", l] + i - 3
            panel_landed(pe, s)
            if i == 3:
                pe.wait_ge(sem("oT_sb"), HEADS * (a + 1))
            pe_project(pe, l, i, s, HEADS, lambda k, t: oT[:, k, t * 128:(t + 1) * 128], 0 if i == 3 else 3)

    def pe_pool(pe, l):
        f = first_panel["mix", l]
        pe.wait_ge(sem("gate_bc"), 4 * (2 * l + 1))
        pe_mod_bc(pe, l)
        pe.wait_ge(sem("mod_bc"), 8 * (l + 1))
        panel_landed(pe, f)
        for half in range(2):
            pe.wait_ge(sem("pool_u"), 2 * half + 2)
            for t in range(TILES):
                for g in range(2):
                    for c in range(2):
                        q = 2 * (2 * half + g) + c
                        last = PE.matmul(ps[3 * half + t][:, g * 256:(g + 1) * 256],
                                         uT[:, q, POFF[t]:POFF[t] + 128], panel[f % 2][:, q, 0:256],
                                         start=c == 0, stop=c == 1)
                last.then_inc(sem("proj_done"), 1)

    def pe_retention(pe, l):
        f = first_panel["mix", l]
        pe.wait_ge(sem("hT_dve"), KD // 2 * (2 * l + 1))
        pe.wait_ge(sem("hT_act"), KD // 2 * (2 * l + 1))
        pe.wait_ge(sem("gate_bc"), 4 * (2 * l + 1))
        pe_mod_bc(pe, l)
        pe.wait_ge(sem("mod_bc"), 8 * (l + 1))

        def ada_steps(h):
            idx = (l + 1) * ADA_P + 2 * h

            def product(j):
                pe.wait_ge(sem(f"ada_landed{2 + j}"), 48 * (ADA_P // 4 + 1) + 48 * h)
                pe_ada_product(pe, idx + j, ring4[2 + j])

            def first():
                atleast(pe, "ret_gate_sb", h + 1)
                product(0)

            def second():
                pe_ada_columns(pe, idx)
                product(1)

            return first, second, lambda: pe_ada_columns(pe, idx + 1)

        def project_qkv(h, between=None):
            panel_landed(pe, f, h, 2)
            atleast(pe, "ret_in_sb", 3 * h)
            for t in range(TILES):
                if between is not None:
                    between[t]()
                for k in range(KD):
                    last = PE.matmul(ps[t][:], hT[:, k, t * 128:(t + 1) * 128], panel[f % 2][:, k, :],
                                     start=k == 0, stop=k == KD - 1)
            last.then_inc(sem("ret_qkv"), 1)

        def project_gate(h, ada=None):
            panel_landed(pe, f + 1, h, 2)
            atleast(pe, "ret_gate_sb", h)
            if ada is not None:
                atleast(pe, "ada_mod", ada)
            for t in range(TILES):
                for k in range(KD):
                    last = PE.matmul(ps[3 + t // 2][:, (t % 2) * 256:(t % 2) * 256 + 256],
                                     hT[:, k, t * 128:(t + 1) * 128], panel[(f + 1) % 2][:, k, 0:256],
                                     start=k == 0, stop=k == KD - 1)
            last.then_inc(sem("ret_gate"), 1)

        def mix(h):
            atleast(pe, "ret_in_sb", 3 * h + 3)
            atleast(pe, "ret_yT_sb", 2 * h)
            for t in range(TILES):
                PE.transpose(ps[5][:, t * 128:(t + 1) * 128], rq[:, t, :], ident)
            for t in range(TILES):
                last = PE.transpose(ps[6][:, t * 128:(t + 1) * 128], rk[:, t, :], ident)
            last.then_inc(sem("ret_T_ps"), 1)
            pe.wait_ge(sem("ret_T_sb"), 4 * h + 4)
            for t in range(TILES):
                last = PE.matmul(ps[7][:, t * 128:(t + 1) * 128], rkT[:, t * 128:(t + 1) * 128],
                                 rqT[:, t * 128:(t + 1) * 128], start=True, stop=True)
            last.then_inc(sem("ret_S_ps"), 1)
            pe.wait_ge(sem("ret_kd"), h + 1)
            for n, t in enumerate((0, 0, 1, 2)):
                last = PE.matmul(ps[5 + n // 2][:, (n % 2) * 256:(n % 2) * 256 + 256], rkd[:, n, :], rv[:, t, :],
                                 start=True, stop=True)
            last.then_inc(sem("ret_U_ps"), 1)
            pe.wait_ge(sem("ret_S_sb"), h + 1)
            pe.wait_ge(sem("ret_mid"), h + 1)
            pe.wait_ge(sem("state_in"), 16 * h + 16)
            PE.matmul(ps[7][:, 0:256], rST[:, 0, :], rv[:, 0, :], start=True, stop=True)
            PE.matmul(ps[7][:, 256:512], rST[:, 1, :], rv[:, 1, :], start=True, stop=False)
            PE.matmul(ps[7][:, 256:512], rqf[:, 0, :], rs0[:, 0, :], start=False, stop=False)
            PE.matmul(ps[7][:, 256:512], rqb[:, 0, :], rs1[:, 1, :], start=False, stop=True)
            pe.wait_ge(sem("ret_state_out"), h + 1)
            PE.matmul(ps[5][:, 0:256], rST[:, 2, :], rv[:, 2, :], start=True, stop=False)
            PE.matmul(ps[5][:, 0:256], rqf[:, 1, :], rs1[:, 0, :], start=False, stop=False)
            PE.matmul(ps[5][:, 0:256], rqb[:, 1, :], rs0[:, 1, :], start=False, stop=True).then_inc(sem("ret_O_ps"), 1)

        def turn_y(h):
            pe.wait_ge(sem("ret_y"), h + 1)
            for c in range(2):
                for t in range(TILES):
                    last = PE.transpose(ps[6 - c][:, t * 128:(t + 1) * 128], rof[:, t, c * 128:(c + 1) * 128], ident)
                last.then_inc(sem("ret_yT_ps"), 1)

        project_qkv(0)
        project_gate(0)
        with pe.Fori(0, RH - 1) as h:
            mix(h)
            project_qkv(h + 1, ada_steps(h) if in_retention(l) else None)
            turn_y(h)
            project_gate(h + 1, (l + 1) * ADA_P + 2 * h + 2 if in_retention(l) else None)
        mix(RH - 1)
        if in_retention(l):
            for take in ada_steps(RH - 1):
                take()
        turn_y(RH - 1)
        atleast(pe, "ret_yT_sb", 2 * RH)
        if in_retention(l):
            atleast(pe, "ada_mod", (l + 2) * ADA_P)
        s = f + 2 * RH
        for half in range(2):
            for part in range(2):
                panel_landed(pe, s)
                for t in range(TILES):
                    for k in range(8):
                        src = (yTe, yTo)[k % 2]
                        last = PE.matmul(ps[3 * half + t][:], src[:, 4 * part + k // 2, t * 128:(t + 1) * 128],
                                         panel[s % 2][:, k, :], start=part == 0 and k == 0,
                                         stop=part == 1 and k == 7)
                    if part == 1:
                        last.then_inc(sem("proj_done"), 1)
                s += 1

    def pe_route(pe, l):
        n = 2 * l + 1
        pe.wait_ge(sem("hT_dve"), KD // 2 * (n + 1))
        pe.wait_ge(sem("hT_act"), KD // 2 * (n + 1))
        pe.wait_ge(sem("router_pad"), 1)
        pe.wait_ge(sem("router_landed"), 64 * DEPTH)
        for kk in range(2):
            for g in range(4):
                last = PE.matmul(ps[2][32 * g:32 * g + 32, 0:T], wr[:, l, 2 * g + kk, :], hT[:, 2 * g + kk, :],
                                 start=kk == 0, stop=kk == 1)
        last.then_inc(sem("logit_parts_ps"), 1)
        pe.wait_ge(sem("logit_parts"), l + 1)
        for t in range(TILES):
            last = PE.matmul(ps[3][:, t * 20:(t + 1) * 20], lpart[:, t * 128:(t + 1) * 128], quad[:, 0:20], start=True, stop=True)
        last.then_inc(sem("logits"), 1)
        pe_gate_bc(pe, n, 5)
        pe.wait_ge(sem("assigned"), l + 1)
        asg = rt[:, 96:96 + TILES * EXPERTS].rearrange("p (t e) -> p t e", t=TILES)
        for t in range(TILES):
            PE.matmul(ps[2][:, t * 16:(t + 1) * 16], tri, asg[:, t, :], start=True, stop=t == 0)
            for u in range(t):
                PE.matmul(ps[2][:, t * 16:(t + 1) * 16], ones[:], asg[:, u, :], start=False, stop=u == t - 1)
        for t in range(TILES):
            last = PE.matmul(ps[2][:, 64:65], wide[:, t, :], ones[:, 0:1], start=t == 0, stop=t == TILES - 1)
        last.then_inc(sem("ranks"), 1)
        pe.wait_ge(sem("unit_flags"), l + 1)
        PE.matmul(ps[3][:, 0:1], tri, uhot[:, UNITS:UNITS + 1], start=True, stop=True)
        PE.matmul(ps[3][:, 1:2], ones[:], uhot[:, UNITS:UNITS + 1], start=True, stop=True).then_inc(sem("unit_places"), 1)
        pe.wait_ge(sem("unit_hot"), l + 1)
        PE.matmul(ps[3][:, 32:32 + UNITS], expert_of.broadcast_to([128, 128]), uhot[:, 0:UNITS], start=True, stop=True)
        PE.matmul(ps[3][:, 64:64 + UNITS], past_less.broadcast_to([128, 128]), uhot[:, 0:UNITS], start=True, stop=True)\
            .then_inc(sem("unit_ids"), 1)
        pe.wait_ge(sem("gate_bc"), 4 * (n + 1))

    PAIRS_OF, GROUPS_OF, PER_OF = {"m": PAIRS, "o": MORE}, {"m": MAIN_GROUPS, "o": 1}, {"m": MAIN, "o": MORE}

    def pe_gather(pe, z, r, j):
        atleast(pe, z + "_P", r + 1)
        atleast(pe, z + "_hg_act", r)
        atleast(pe, z + "_hg_dve", r)
        for t in range(TILES):
            for n, part in enumerate((hhi, hlo)):
                for half in range(2):
                    last = PE.matmul(ps[half][:], Pm[:, j % 2, t, :], part[:, t, half * 512:half * 512 + 512],
                                     start=t == 0 and n == 0, stop=t == TILES - 1 and n == 1)
        last.then_inc(sem(z + "_gather"), 1)

    def pe_gathered_T(pe, z, r):
        pe.wait_ge(sem(z + "_hgt_act"), r + 1)
        pe.wait_ge(sem(z + "_hgt_dve"), r + 1)
        for k in range(KD):
            last = PE.transpose(ps[k // 4][:, (k % 4) * 128:(k % 4) * 128 + 128], hgt[:, k * 128:(k + 1) * 128], ident)
        last.then_inc(sem(z + "_hT"), 1)

    def pe_slots(pe, z, r, u, j):
        table = gates_r if z == "m" else gates_u
        atleast(pe, z + "_PT_sb", r)
        for t in range(TILES):
            PE.matmul(ps[5][:, T:T + 4], Pm[:, j % 2, t, :], table[:, t, ds(2 * u, 2), :].rearrange("p e c -> p (e c)"),
                      start=t == 0, stop=t == TILES - 1)
        for t in range(TILES):
            last = PE.transpose(ps[5][:, t * 128:(t + 1) * 128], Pm[:, j % 2, t, :].bitcast(F), ident)
        last.then_inc(sem(z + "_PT"), 1)

    def pe_experts(pe, z, P, g, u0, ada):
        per = PER_OF[z]
        it = P * GROUPS_OF[z] + g
        for j in range(per):
            e = g * per + j
            q, r = P * PAIRS_OF[z] + e, P * (PAIRS_OF[z] + 1) + e
            atleast(pe, z + "_hg_act", r + 1)
            atleast(pe, z + "_hg_dve", r + 1)
            atleast(pe, z + "_act", q)
            for k in range(KD):
                if k % (KD // 2) == 0:
                    if k:
                        last.then_inc(sem(z + "_gateup_half"), 1)
                    pe.wait_ge(sem(f"{z}_gu{2 * k // KD}_landed"), 64 * q + 64)
                for s in range(2):
                    last = PE.matmul(ps[2][CAP * s:CAP * s + CAP, :], hg[:, j % 2, k, CAP * s:CAP * s + CAP],
                                     gu_ring[s][:, k, :], start=k == 0, stop=k == KD - 1)
            last.then_inc(sem(z + "_gateup"), 1)
            pe_gather(pe, z, r + 1, j + 1)
            atleast(pe, z + "_act", q + 1)
            atleast(pe, z + "_actT_sb", q)
            for c in range(2):
                last = PE.transpose(ps[3][:, c * 128:c * 128 + 128], act[:, c * 128:(c + 1) * 128], ident)
            last.then_inc(sem(z + "_actT"), 1)
            if ada is not None:
                panel_landed(pe, ada[1], e, 2)
                pe_ada_product(pe, ada[0] + 2 * e, panel[ada[1] % 2])
            atleast(pe, z + "_actT_sb", q + 1)
            for s in range(2):
                pe.wait_ge(sem(f"{z}_dn_landed{s}"), 16 * q + 16)
            atleast(pe, z + "_y_hi", 2 * q)
            atleast(pe, z + "_y_lo", 2 * q)
            if j == 0:
                atleast(pe, z + "_term", 6 * it)
            for half in range(2):
                for c in range(2):
                    for s in range(2):
                        last = PE.matmul(ps[6 + half][CAP * s:CAP * s + CAP, :], actT[:, c, CAP * s:CAP * s + CAP],
                                         dn_ring[s][:, c, half * 512:half * 512 + 512], start=c == 0, stop=c == 1)
                last.then_inc(sem(z + "_down"), 1)
            if ada is not None:
                pe_ada_columns(pe, ada[0] + 2 * e)
            pe_gathered_T(pe, z, r + 1)
            if ada is not None:
                panel_landed(pe, ada[1] + 1, e, 2)
                pe_ada_product(pe, ada[0] + 2 * e + 1, panel[(ada[1] + 1) % 2])
            pe_slots(pe, z, r + 1, u0 + j + 1, j + 1)
            if ada is not None:
                pe_ada_columns(pe, ada[0] + 2 * e + 1)
        q = it * per + per
        atleast(pe, z + "_y_hi", 2 * q)
        atleast(pe, z + "_y_lo", 2 * q)
        for m in range(2 * TILES):
            t, half = m // 2, m % 2
            if m >= 2:
                atleast(pe, z + "_term", 6 * it + m - 1)
            for j in range(per):
                for n, part in enumerate((yhi, ylo)):
                    last = PE.matmul(ps[6 + half][:], PT[:, j, t * 128:(t + 1) * 128],
                                     part[:, j, half * 512:half * 512 + 512],
                                     start=j == 0 and n == 0, stop=j == per - 1 and n == 1)
            last.then_inc(sem(z + "_scatter"), 1)

    def pe_first(pe, z, P, u0):
        r = P * (PAIRS_OF[z] + 1)
        pe_gather(pe, z, r, 0)
        pe_gathered_T(pe, z, r)
        pe_slots(pe, z, r, u0, 0)

    def expert_passes(eng, first, group, passes, l, before=None):
        first("m", l, 0)
        with eng.Fori(0, MAIN_GROUPS) as g:
            group("m", l, g, g * MAIN)
        r = eng.value_load(extra[0:1, l:l + 1], min_val=0, max_val=MORE_GROUPS)
        done = sum(passes) if passes else 0
        with eng.If(r > 0):
            if before is not None:
                before()
            with eng.Fori(0, r) as p:
                first("o", done + p, p * MORE)
                group("o", done + p, 0, p * MORE)
        passes.append(r)

    @block.tensor
    def _(pe):
        pe.wait_ge(sem("vec_landed"), 32)
        pe.wait_ge(sem("const_landed"), 16)
        for a in range(3):
            last = PE.transpose(ps[0][:, a * 96:(a + 1) * 96], vecs[0:96, a, :], ident[0:96, 0:96])
        last.then_inc(sem("vT_ps"), 1)
        pe.wait_ge(sem("cond_ready"), 1)
        with pe.Fori(0, ADA_P // 4) as i:
            for j in range(4):
                pe.wait_ge(sem(f"panel_landed{j}" if j < 2 else f"ada_landed{j}"), 48 * i + 48)
                pe_ada_product(pe, 4 * i + j, ring4[j])
                pe_ada_columns(pe, 4 * i + j)
        passes = []
        for l in range(depth):
            pe.wait_ge(sem("mods_ready"), l + 1)
            pe_norm(pe, 2 * l)
            pe_gate_bc(pe, 2 * l, 2)
            (pe_attention, pe_pool, pe_retention)[l % 3](pe, l)
            pe_norm(pe, 2 * l + 1)
            pe_route(pe, l)
            pe.wait_ge(sem("h_lo"), TILES * (l + 1))
            pe.wait_ge(sem("routed"), l + 1)
            ada = ((l + 1) * ADA_P, first_panel["ada", l + 1]) if l + 1 < depth and not early(l) else None

            def first_pass_read():
                for name in ("m_hg_act", "m_hg_dve", "m_PT_sb"):
                    atleast(pe, name, (PAIRS + 1) * (l + 1))

            expert_passes(pe, lambda z, P, u0: pe_first(pe, z, P, u0),
                          lambda z, P, g, u0: pe_experts(pe, z, P, g, u0, ada if z == "m" else None), passes, l,
                          first_pass_read)
            pe.drain().then_inc(sem("experts_read"), 1)
        pe.wait_ge(sem("rstd"), TILES * (2 * depth + 1))
        for half in range(2):
            for q in range(4):
                last = PE.matmul(ps[4 + half][:, q * 128:(q + 1) * 128],
                                 vT[:, 72 + 4 * half + q:73 + 4 * half + q].broadcast_to([128, 128]), ident,
                                 start=True, stop=True)
        last.then_inc(sem("normf_ps"), 1)

    def mod_col(v, k, c):
        return mods[:, v * KD + k, c:c + 1]

    def hT_out(l, sub, k, c):
        if l % 3 == 1 and sub == 0:
            return hp[:, k, POFF[0]:POFF[0] + 128] if c == 0 else hp[:, k, POFF[1]:POFF[1] + DEC]
        return hT[:, k, 0:128] if c == 0 else hT[:, k, 128:T]

    @block.vector
    def _(dve):
        step = Order(dve, "dve_step")

        def finish_mods(l):
            for v in range(6):
                out, raw = mods[:, v * KD:(v + 1) * KD, :], mraw[:, v * KD:(v + 1) * KD, :]
                if v in (1, 4):
                    gain = vT[:, (0 if v == 1 else 32) + l * KD:(0 if v == 1 else 32) + (l + 1) * KD]
                    last = V.scalar_tensor_tensor(out, raw, 1.0, gain.unsqueeze(2).broadcast_to([128, KD, 2]), ALU.add, ALU.mult)
                elif v == 2 and l % 3 == 1:
                    last = V.tensor_tensor(out, raw, vT[:, 64:72].unsqueeze(2).broadcast_to([128, KD, 2]), ALU.mult)
                else:
                    last = V.tensor_copy(out, raw)
            last.then_inc(sem("mods_ready"), 1)
            dve.wait_ge(sem("mods_ready"), l + 1)

        def ada_mod(l, idx, p, bank=4):
            atleast(dve, "ada_col", idx + 1)
            V.tensor_tensor(mraw[:, ds(3 * p, 3), :], ps[bank][:, ADA_N:ADA_N + 6].rearrange("q (c o) -> q c o", c=3),
                            biasT[:, ds(l * 48 + 3 * p, 3)].unsqueeze(2).broadcast_to([128, 3, 2]), ALU.add)\
                .then_inc(sem("ada_mod"), 1)

        def mean_square(n):
            for t in range(TILES):
                dve.wait_ge(sem("ssq"), TILES * n + t + 1)
                V.tensor_scalar(msq[:, t:t + 1], ssq[:, t:t + 1], 1.0 / D, EPS, ALU.mult, ALU.add).then_inc(sem("msq"), 1)

        def norm(l, sub):
            n = 2 * l + sub
            mean_square(n)
            if sub == 1:
                token_major(l, 0)
            for k in range(0, KD, 2):
                dve.wait_ge(sem("hT_ps"), KD * n + k + 1)
                for c, src in enumerate((ps[k % 4][:, 0:128], ps[k % 4][:, 128:T])):
                    last = V.tensor_scalar(hT_out(l, sub, k, c), src, mod_col(1 + 3 * sub, k, c),
                                           mod_col(3 * sub, k, c), ALU.mult, ALU.add)
                last.then_inc(sem("hT_dve"), 1)

        def residual(l, order):
            b = prj_base[l] + (3 * TILES if l % 3 == 0 else 0)
            dve.wait_ge(sem("gate_bc"), 4 * (2 * l + 1))
            for m in range(2 * TILES):
                half, t = m // TILES, m % TILES
                dve.wait_ge(sem("proj_done"), b + m + 1)
                if 6 * l + m >= 2:
                    dve.wait_ge(sem("mix_added"), 6 * l + m - 1)
                if m == 0 and l:
                    dve.wait_ge(sem("layer_done"), l)
                V.tensor_tensor(tmp[:, m % 2, :], ps[3 * half + t][:], gate_bc[:, COND[t], half * 512:half * 512 + 512],
                                ALU.mult).then_inc(sem("mix_term"), 1)

        def attention(l):
            a = l // 3
            sums = stat[:, 0:30].rearrange("p (h t) -> p h t", t=TILES)
            means = stat[:, 32:62]
            rs = stat[:, 64:94].rearrange("p (h t) -> p h t", t=TILES)
            dve.wait_ge(sem("attn_landed"), 64 * (a + 1))
            for i, (h0, h1) in enumerate(((0, 4), (4, 8), (8, NQK))):
                o, nh = slice(h0 * HD, h1 * HD), h1 - h0
                for t in range(TILES):
                    dve.wait_ge(sem("qkv_sb"), 9 * a + 3 * i + t + 1)
                    step(V.tensor_tensor(sqv[:, o], qkv[:, t, o], qkv[:, t, o], ALU.mult))
                    step(V.tensor_reduce(sums[:, h0:h1, t], sqv[:, o].rearrange("p (h d) -> p h d", d=HD), AX.X, ALU.add))
                V.tensor_scalar(stat[:, 32 + 3 * h0:32 + 3 * h1], stat[:, 3 * h0:3 * h1], 1.0 / HD, EPS, ALU.mult, ALU.add)\
                    .then_inc(sem("qk_ms"), 1)
                dve.wait_ge(sem("qk_rstd"), 3 * a + i + 1)
                for t in range(TILES):
                    qk3 = qkv[:, t, o].rearrange("p (h d) -> p h d", d=HD)
                    step(V.tensor_tensor(qk3, qk3, rs[:, h0:h1, t:t + 1].broadcast_to([128, nh, HD]), ALU.mult))
                    last = V.tensor_tensor(qkv[:, t, o], qkv[:, t, o], gqk[:, o], ALU.mult)
                    if t == 0:
                        last.then_inc(sem("qk_ready"), 1)
                        continue
                    step(last)
                    x5 = qkv[:, t, o].rearrange("p (h a b f) -> p h a b f", h=nh, a=2, b=2)
                    r5 = ropet[:, o].rearrange("p (h a b f) -> p h a b f", h=nh, a=2, b=2)
                    tab = rope[:, t - 1, :].rearrange("p (s a b f) -> p s a b f", s=2, a=2, b=2)
                    for b in range(2):
                        for hh in range(2):
                            last = V.tensor_tensor(r5[:, :, hh, b, :], x5[:, :, hh, 1 - b, :],
                                                   tab[:, 1, hh, b, :].unsqueeze(1).broadcast_to([128, nh, 32]), ALU.mult)
                    step(last)
                    step(V.tensor_tensor(qk3, qk3, rope[:, t - 1, 0:128].unsqueeze(1).broadcast_to([128, nh, HD]), ALU.mult))
                    V.tensor_tensor(qkv[:, t, o], qkv[:, t, o], ropet[:, o], ALU.add).then_inc(sem("qk_ready"), 1)
                    dve.wait_ge(sem("qk_ready"), 9 * a + 3 * i + t + 1)
            mx = stat[:, 0:12].rearrange("p (b c) -> p b c", b=4)
            den = stat[:, 12:24].rearrange("p (b c) -> p b c", b=4)
            inv = stat[:, 24:30].rearrange("p (b c) -> p b c", b=2)
            def maxima(h):
                n, b0 = HEADS * a + h, 2 * (h % 2)
                units = (ps[b0][:, 0:128], ps[b0][:, 128:512], ps[b0 + 1][:, 0:384])
                dve.wait_ge(sem("scores"), n + 1)
                for u, src in enumerate(units):
                    last = V.tensor_reduce(mx[:, h % 2, u:u + 1], src, AX.X, ALU.max)
                step(last)
                V.tensor_scalar(mx[:, 2 + h % 2, :], mx[:, h % 2, :], -float(HD) ** -0.5, None, ALU.mult).then_inc(sem("neg_max"), 1)

            def normalise(h):
                dve.wait_ge(sem("prob"), 3 * (HEADS * a + h + 1))
                step(V.reciprocal(inv[:, h % 2, :], den[:, h % 2, :]))
                for u, (lo, hi) in enumerate(((0, 128), (128, 512), (512, 896))):
                    last = V.tensor_scalar(prob[:, h % 2, lo:hi], prob[:, h % 2, lo:hi], inv[:, h % 2, u:u + 1], None, ALU.mult)
                last.then_inc(sem("prob_norm"), 1)

            def beside(p):
                if in_heads(l) and p >= 0:
                    ada_mod(l + 1, (l + 1) * ADA_P + p, p, 7)

            maxima(0)
            maxima(1)
            normalise(0)
            for h in range(HEADS):
                if h + 1 < HEADS:
                    normalise(h + 1)
                beside(2 * h - 1)
                if h + 2 < HEADS:
                    maxima(h + 2)
                beside(2 * h)
            beside(2 * HEADS - 1)

        def pool(l):
            dve.wait_ge(sem("pool_pads"), 1)
            dve.wait_ge(sem("hT_dve"), KD // 2 * (2 * l + 1))
            dve.wait_ge(sem("hT_act"), KD // 2 * (2 * l + 1))
            dve.wait_ge(sem("count_landed"), 16)
            for g, win in enumerate(WINDOWS):
                src = hp[:, 2 * g:2 * g + 2, :]
                bufs, m, lo, hi = (win_a, win_b), 1, 0, PW
                while m < win:
                    a, b = (1, 0) if m == 1 else (m // 2, m // 2)
                    lo, hi = lo + a, hi - b
                    dst = bufs[0][:]
                    step(V.tensor_tensor(dst[:, :, lo:hi], src[:, :, lo - a:hi - a], src[:, :, lo + b:hi + b], ALU.add))
                    src, bufs, m = dst, bufs[::-1], 2 * m
                dst = bufs[0][:]
                step(V.tensor_tensor(dst[:, :, PAD:PW - PAD], src[:, :, PAD:PW - PAD],
                                     icnt[:, g:g + 1, PAD:PW - PAD].broadcast_to([128, 2, PW - 2 * PAD]), ALU.mult))
                V.tensor_tensor(uT[:, 2 * g:2 * g + 2, PAD:PW - PAD], dst[:, :, PAD:PW - PAD],
                                hp[:, 2 * g:2 * g + 2, PAD:PW - PAD], ALU.subtract).then_inc(sem("pool_u"), 1)
                dve.wait_ge(sem("pool_u"), g + 1)

        def decay_tables():
            dve.wait_ge(sem("ret_const"), 48)
            z = rsm[:, 0:16]
            neg, e1, w, w2, acc, lg = (rsm[:, 16 * i:16 * i + 16] for i in range(1, 7))
            step(V.tensor_scalar(neg, z, -1.0, None, ALU.mult))
            V.tensor_tensor(neg, z, neg, ALU.min).then_inc(sem("decay_in"), 1)
            dve.wait_ge(sem("decay_exp"), 1)
            step(V.tensor_scalar(w, e1, 2.0, None, ALU.add))
            step(V.reciprocal(w, w))
            step(V.tensor_tensor(w, w, e1, ALU.mult))
            step(V.tensor_tensor(w2, w, w, ALU.mult))
            step(V.tensor_scalar(acc, w2, 1.0 / 17, 1.0 / 15, ALU.mult, ALU.add))
            for d in (13, 11, 9, 7, 5, 3, 1):
                step(V.tensor_tensor(acc, acc, w2, ALU.mult))
                step(V.tensor_scalar(acc, acc, 1.0 / d, None, ALU.add))
            step(V.tensor_tensor(acc, acc, w, ALU.mult))
            step(V.tensor_scalar(lg, z, 0.0, None, ALU.min))
            V.scalar_tensor_tensor(lg, acc, -2.0, lg, ALU.mult, ALU.add).then_inc(sem("log_decay"), 1)
            for h in range(RH):
                dve.wait_ge(sem("mask_exp"), 2 * h + 2)
                step(V.tensor_tensor(rMT[:, h, :], rMT[:, h, :], kret[:, 128:256], ALU.mult))
                step(V.tensor_tensor(rof[:, h % 2, 0:128], rof[:, h % 2, 0:128], kret[:, 384:512], ALU.mult))
                V.tensor_tensor(rMT[:, h, :], rMT[:, h, :], rof[:, h % 2, 0:128], ALU.add).then_inc(sem("mask_done"), 1)

        def retention(l):
            decay_tables()
            dve.wait_ge(sem("mask_exp"), 2 * RH + 1)
            dve.wait_ge(sem("mask_done"), RH)
            with dve.Fori(0, RH) as h:
                step.enter(h, 5)
                dve.wait_ge(sem("ret_qkv"), h + 1)
                V.tensor_copy(rqkv[:, 1, :], ps[1][:]).then_inc(sem("ret_in_sb"), 1)
                atleast(dve, "ret_in_sb", 3 * h + 3)
                for n, (t, d) in enumerate(((0, 0), (0, 1), (1, 0), (2, 1))):
                    last = V.tensor_scalar(rkd[:, n, :], rk[:, t, :], rsm[:, ds(112 + 8 * d + h, 1)], float(RK) ** -0.5,
                                           ALU.mult, ALU.mult)
                last.then_inc(sem("ret_kd"), 1)
                dve.wait_ge(sem("ret_T_ps"), h + 1)
                V.tensor_copy(rqT[:], ps[5][:, 0:T]).then_inc(sem("ret_T_sb"), 1)
                V.tensor_tensor(rqf[:].rearrange("p t i -> p t i"), ps[5][:, 128:T].rearrange("p (t i) -> p t i", t=2),
                                rdf[:, ds(h, 1), :].broadcast_to([128, 2, 128]), ALU.mult).then_inc(sem("ret_T_sb"), 1)
                V.tensor_tensor(rqb[:], ps[5][:, 128:T].rearrange("p (t i) -> p t i", t=2),
                                rdb[:, ds(h, 1), :].broadcast_to([128, 2, 128]), ALU.mult).then_inc(sem("ret_T_sb"), 1)
                dve.wait_ge(sem("ret_S_ps"), h + 1)
                V.tensor_tensor(rST[:], ps[7][:, 0:T].rearrange("p (t i) -> p t i", t=TILES),
                                rMT[:, ds(h, 1), :].broadcast_to([128, TILES, 128]), ALU.mult).then_inc(sem("ret_S_sb"), 1)
                dve.wait_ge(sem("ret_U_ps"), h + 1)
                dve.wait_ge(sem("state_in"), 16 * h + 16)
                V.scalar_tensor_tensor(rs1[:, 0, :], rs0[:, 0, :], rsm[:, ds(128 + h, 1)], ps[6][:, 0:256], ALU.mult, ALU.add)
                V.scalar_tensor_tensor(rs1[:, 1, :], rs0[:, 1, :], rsm[:, ds(136 + h, 1)], ps[6][:, 256:512], ALU.mult, ALU.add)\
                    .then_inc(sem("ret_mid"), 1)
                atleast(dve, "ret_O_ps", h + 1)
                outs = (ps[7][:, 0:256], ps[7][:, 256:512], ps[5][:, 0:256])
                bst, agg = rsm[:, 144:162], rsm[:, 164:170]
                for t in range(TILES):
                    last = V.bn_stats(bst[:, 6 * t:6 * t + 6], outs[t])
                step(last)
                atleast(dve, "ret_gate_sb", h + 1)
                V.tensor_tensor(rg[:], rg[:], rnorm[:, ds(h, 1), :].broadcast_to([128, TILES, RV]), ALU.mult)
                for t in range(TILES):
                    last = V.bn_aggr(agg[:, 2 * t:2 * t + 2], bst[:, 6 * t:6 * t + 6])
                step(last)
                V.tensor_scalar(rsm[:, 172:175], agg.rearrange("p (t c) -> p t c", c=2)[:, :, 1], EPS, None, ALU.add)\
                    .then_inc(sem("ret_var"), 1)
                dve.wait_ge(sem("ret_rstd"), h + 1)
                for t in range(TILES):
                    step(V.tensor_scalar(rof[:, t, :], outs[t], agg[:, 2 * t:2 * t + 1], rsm[:, 176 + t:177 + t],
                                         ALU.subtract, ALU.mult))
                V.tensor_tensor(rof[:], rof[:], rg[:], ALU.mult).then_inc(sem("ret_y"), 1)
                if in_retention(l):
                    for j in range(2):
                        ada_mod(l + 1, (l + 1) * ADA_P + 2 * h + j, 2 * h + j)
            step.leave(RH)

        def pick(out, vals, mx, scratch):
            b = lambda a: a.unsqueeze(2).broadcast_to([128, TILES, 4])
            step(V.tensor_tensor(scratch, vals, b(mx), ALU.is_equal))
            step(V.tensor_tensor(scratch, scratch, tie.unsqueeze(1).broadcast_to([128, TILES, 4]), ALU.mult))
            step(V.tensor_reduce(scol, scratch, AX.X, ALU.max))
            step(V.tensor_tensor(out, scratch, b(scol), ALU.is_equal))

        scol = rt[:, 424:427]

        def route(l):
            g3 = lambda o, n: rt[:, o:o + 3 * n].rearrange("p (t e) -> p t e", t=TILES)
            lg, asg, gts, rk16 = g3(0, 20), g3(96, 16), g3(144, 16), g3(192, 16)
            gmax, ohg, scr, les = rt[:, 240:243], g3(243, 4), g3(255, 4), g3(267, 4)
            prod = rt[:, 280:328].rearrange("p (t g e) -> p t g e", t=TILES, g=4)
            m1, m2, oh1, oh2, les2 = rt[:, 328:331], rt[:, 331:334], g3(334, 4), g3(346, 4), g3(358, 4)
            ein, eout = g3(370, 5), g3(385, 5)
            den, w1, w2 = rt[:, 400:403], rt[:, 403:406], rt[:, 406:409]
            over, nx, place_of = rt[:, 410:410 + MORE_GROUPS], rt[:, 420:421], rt[:, 421:423]
            b4 = lambda a: a.unsqueeze(2).broadcast_to([128, TILES, 4])
            dve.wait_ge(sem("logits"), l + 1)
            dve.wait_ge(sem("router_landed"), 64 * DEPTH)
            step(V.tensor_tensor(lg, ps[3][:, 0:60].rearrange("p (t e) -> p t e", t=TILES),
                                 rb[:, l:l + 1, :].broadcast_to([128, TILES, 20]), ALU.add))
            step(V.tensor_reduce(gmax, lg[:, :, 0:4], AX.X, ALU.max))
            pick(ohg, lg[:, :, 0:4], gmax, scr)
            for t in range(TILES):
                last = V.tensor_tensor(prod[:, t], lg[:, t, 4:20].rearrange("p (g e) -> p g e", g=4),
                                       ohg[:, t, :].unsqueeze(2).broadcast_to([128, 4, 4]), ALU.mult)
            step(last)
            for t in range(TILES):
                last = V.tensor_reduce(les[:, t, :], prod[:, t].rearrange("p g e -> p e g"), AX.X, ALU.add)
            step(last)
            step(V.tensor_reduce(m1, les, AX.X, ALU.max))
            pick(oh1, les, m1, scr)
            step(V.scalar_tensor_tensor(les2, oh1, -1e30, les, ALU.mult, ALU.add))
            step(V.tensor_reduce(m2, les2, AX.X, ALU.max))
            pick(oh2, les2, m2, scr)
            step(V.tensor_tensor(asg[:, :, 0:4], oh1, oh2, ALU.add))
            step(V.tensor_copy(les2, asg[:, :, 0:4]))
            for t in range(TILES):
                last = V.tensor_tensor(asg[:, t, :].rearrange("p (g e) -> p g e", g=4),
                                       ohg[:, t, :].unsqueeze(2).broadcast_to([128, 4, 4]),
                                       les2[:, t, :].unsqueeze(1).broadcast_to([128, 4, 4]), ALU.mult)
            step(last)
            for t in range(TILES):
                last = V.tensor_copy(wide[:, t, :].rearrange("p (k e) -> p k e", e=EXPERTS),
                                     asg[:, t, :].unsqueeze(1).broadcast_to([128, 128 // EXPERTS, EXPERTS]))
            last.then_inc(sem("assigned"), 1)
            dve.wait_ge(sem("h_hi"), TILES * (l + 1))
            V.tensor_tensor(hlo[:, 2, :], htok[:, 2, :], hhi[:, 2, :].bitcast(F), ALU.subtract).then_inc(sem("h_lo"), 1)
            step(V.tensor_tensor(ein[:, :, 0:4], lg[:, :, 0:4], b4(gmax), ALU.subtract))
            V.tensor_tensor(ein[:, :, 4], m2, m1, ALU.subtract).then_inc(sem("route_exp_in"), 1)
            dve.wait_ge(sem("ranks"), l + 1)
            V.tensor_tensor(uhot[:, UNITS:UNITS + 1], ps[2][:, 64:65], past, ALU.is_gt).then_inc(sem("unit_flags"), 1)
            dve.wait_ge(sem("route_exp"), l + 1)
            step(V.tensor_reduce(den, eout[:, :, 0:4], AX.X, ALU.add))
            step(V.tensor_scalar(w2, eout[:, :, 4], 1.0, None, ALU.add))
            step(V.tensor_tensor(den, den, w2, ALU.mult))
            step(V.reciprocal(w1, den))
            step(V.tensor_tensor(w2, w1, eout[:, :, 4], ALU.mult))
            dve.wait_ge(sem("unit_places"), l + 1)
            step(V.tensor_copy(place_of, ps[3][:, 0:2]))
            V.tensor_scalar(uhot[:, 0:UNITS], iota[:, 0:UNITS], place_of[:, 0:1], uhot[:, UNITS:UNITS + 1],
                            ALU.is_equal, ALU.mult).then_inc(sem("unit_hot"), 1)
            step(V.tensor_tensor(over, place_of[:, 1:2].broadcast_to([128, MORE_GROUPS]), caps, ALU.is_gt))
            step(V.tensor_reduce(nx, over, AX.X, ALU.add))
            step(V.tensor_copy(extra[:, l:l + 1], nx))
            step(V.tensor_tensor(les, oh1, b4(w1), ALU.mult))
            step(V.tensor_tensor(les2, oh2, b4(w2), ALU.mult))
            step(V.tensor_tensor(les, les, les2, ALU.add))
            for t in range(TILES):
                last = V.tensor_tensor(gts[:, t, :].rearrange("p (g e) -> p g e", g=4),
                                       ohg[:, t, :].unsqueeze(2).broadcast_to([128, 4, 4]),
                                       les[:, t, :].unsqueeze(1).broadcast_to([128, 4, 4]), ALU.mult)
            step(last)
            step(V.tensor_copy(gates_r[:, :, 0:EXPERTS, 0], gts))
            step(V.tensor_tensor(gates_r[:, :, 0:EXPERTS, 1], gts, gates_r[:, :, 0:EXPERTS, 0].bitcast(F), ALU.subtract))
            dve.wait_ge(sem("ranks"), l + 1)
            step(V.tensor_scalar(rk16, ps[2][:, 0:48].rearrange("p (t e) -> p t e", t=TILES), 1.0, None, ALU.add))
            step(V.tensor_tensor(rk16, rk16, asg, ALU.mult))
            step(V.tensor_scalar(rankm[:, :, 0:EXPERTS], rk16, -1.0, None, ALU.add))
            dve.wait_ge(sem("unit_ids"), l + 1)
            step(V.tensor_copy(unit_ids[:, l, :], ps[3][:, 32:32 + UNITS]))
            step(V.tensor_copy(rt[:, 428:428 + UNITS], ps[3][:, 32:32 + UNITS]))
            V.tensor_scalar(uoff[:], ps[3][:, 64:64 + UNITS], 4096.0, None, ALU.add).then_inc(sem("routed"), 1)
            dve.wait_ge(sem("routed"), l + 1)

        def unit_tables(t, order):
            ids, picked = rt[:, 428:428 + UNITS], rt[:, 448:448 + UNITS]
            if t == 0:
                order(V.tensor_tensor(ue[:], iota[:, 0:EXPERTS].unsqueeze(1).broadcast_to([128, UNITS, EXPERTS]),
                                      ids.unsqueeze(2).broadcast_to([128, UNITS, EXPERTS]), ALU.is_equal))
            for out, src in ((rank_u[:, t, :], rankm[:, t, 0:EXPERTS]),
                             (gates_u[:, t, :, 0], gates_r[:, t, 0:EXPERTS, 0].bitcast(F)),
                             (gates_u[:, t, :, 1], gates_r[:, t, 0:EXPERTS, 1].bitcast(F))):
                order(V.tensor_tensor(uprod[:], ue[:], src.unsqueeze(1).broadcast_to([128, UNITS, EXPERTS]), ALU.mult))
                order(V.tensor_reduce(picked, uprod[:], AX.X, ALU.add))
                order(V.tensor_copy(out, picked))
            order(V.tensor_tensor(rank_u[:, t, :], rank_u[:, t, :], uoff[:], ALU.subtract))

        def token_major(l, t):
            if t == 0:
                if l % 3 == 0:
                    dve.wait_ge(sem("cache_stored"), 32 * (l // 3 + 1))
                elif l % 3 == 2:
                    atleast(dve, "state_stored", 16 * RH)
                dve.wait_ge(sem("mod_bc"), 8 * (l + 1))
            dve.wait_ge(sem("xn_ready"), TILES * (2 * l + 1) + t + 1)
            step(V.tensor_tensor(htok[:, t, :], xn[:, t, :], mod_bc[:, COND[t], :], ALU.mult))
            V.tensor_tensor(htok[:, t, :], htok[:, t, :], mod_bc[:, 2 + COND[t], :], ALU.add).then_inc(sem("h_tok"), 1)

        def place_tokens(z, r, u, j):
            table = rankm if z == "m" else rank_u
            atleast(dve, z + "_PT", r - 1)
            for t in range(TILES):
                last = V.tensor_tensor(Pm[:, j % 2, t, :].rearrange("p (s c) -> p s c", s=2),
                                       iota[:, 0:CAP].unsqueeze(1).broadcast_to([128, 2, CAP]),
                                       table[:, t, ds(2 * u, 2)].unsqueeze(2).broadcast_to([128, 2, CAP]), ALU.is_equal)
            last.then_inc(sem(z + "_P"), 1)

        def gathered_rows(z, r):
            dve.wait_ge(sem(z + "_gather"), r + 1)
            atleast(dve, z + "_hT", r)
            V.tensor_copy(hgt[:, 512:1024], ps[1][:]).then_inc(sem(z + "_hgt_dve"), 1)

        def gathered_cols(z, r, q, j):
            atleast(dve, z + "_hT", r + 1)
            atleast(dve, z + "_gateup", q - 1)
            V.tensor_copy(hg[:, j % 2, 4:8, :], ps[1][:].rearrange("p (k s) -> p k s", k=4)).then_inc(sem(z + "_hg_dve"), 1)

        def experts(z, P, g, u0, ada, order):
            per = PER_OF[z]
            it = P * GROUPS_OF[z] + g
            for j in range(per):
                e = g * per + j
                q, r = P * PAIRS_OF[z] + e, P * (PAIRS_OF[z] + 1) + e
                place_tokens(z, r + 1, u0 + j + 1, j + 1)
                atleast(dve, z + "_PT_sb", r + 1)
                for s in range(2):
                    last = V.tensor_reduce(gsum[CAP * s:CAP * s + CAP, 0:1], gslot[CAP * s:CAP * s + CAP, j % 2, s, :], AX.X, ALU.add)
                order(last)
                dve.wait_ge(sem(z + "_silu"), q + 1)
                atleast(dve, z + "_actT", q)
                V.scalar_tensor_tensor(act[:], ps[2][:, FE:2 * FE], gsum[:, 0:1], silu[:], ALU.mult, ALU.mult)\
                    .then_inc(sem(z + "_act"), 1)
                gathered_rows(z, r + 1)
                if ada is not None:
                    ada_mod(ada[0], ada[1] + 2 * e, 2 * e)
                atleast(dve, z + "_scatter", 6 * it)
                for half in range(2):
                    o = slice(half * 512, half * 512 + 512)
                    atleast(dve, z + "_y_hi", 2 * q + half + 1)
                    V.tensor_tensor(ylo[:, j, o], ps[6 + half][:], yhi[:, j, o].bitcast(F), ALU.subtract)\
                        .then_inc(sem(z + "_y_lo"), 1)
                gathered_cols(z, r + 1, q + 1, j + 1)
                if ada is not None:
                    ada_mod(ada[0], ada[1] + 2 * e + 1, 2 * e + 1)
                if z == "m" and j < TILES:
                    unit_tables(j, order)
            for m in range(2 * TILES):
                t, half = m // 2, m % 2
                atleast(dve, z + "_scatter", 6 * it + m + 1)
                atleast(dve, z + "_added", 6 * it + m - 1)
                V.tensor_tensor(tmp[:, m % 2, :], ps[6 + half][:], gate_bc[:, COND[t], half * 512:half * 512 + 512],
                                ALU.mult).then_inc(sem(z + "_term"), 1)

        dve.wait_ge(sem("vT_ps"), 1)
        V.memset(cond32[:], 0.0)
        V.memset(ones[:], 1.0)
        V.tensor_copy(vT[:], ps[0][:, 0:288]).then_inc(sem("vT_sb"), 1)
        dve.wait_ge(sem("vT_sb"), 1)
        with dve.Fori(0, ADA_P) as i:
            ada_mod(0, i, i)
        atleast(dve, "ada_mod", ADA_P)
        passes = []
        more_order = Order(dve, "dve_more_step")
        for l in range(depth):
            finish_mods(l)
            norm(l, 0)
            if l % 3 == 0:
                attention(l)
            elif l % 3 == 1:
                pool(l)
            else:
                retention(l)
            residual(l, step)
            norm(l, 1)
            token_major(l, 1)
            token_major(l, 2)
            route(l)
            dve.wait_ge(sem("gate_bc"), 4 * (2 * l + 2))
            dve.wait_ge(sem("mix_added"), 6 * (l + 1))
            dve.wait_ge(sem("h_lo"), TILES * (l + 1))
            nxt = (l + 1, (l + 1) * ADA_P) if l + 1 < depth and not early(l) else None

            def group(z, P, g, u0):
                if z == "m":
                    step.enter(g, MAIN + 1 + 10 * TILES)
                    experts(z, P, g, u0, nxt, step)
                    step.leave(MAIN_GROUPS)
                else:
                    more_order.base, more_order.n = P * MORE, 0
                    experts(z, P, g, u0, None, more_order)

            def first(z, P, u0):
                r = P * (PAIRS_OF[z] + 1)
                place_tokens(z, r, u0, 0)
                gathered_rows(z, r)
                gathered_cols(z, r, P * PAIRS_OF[z], 0)

            def main_pass_read():
                atleast(dve, "m_added", 6 * MAIN_GROUPS * (l + 1))
                atleast(dve, "m_PT", (PAIRS + 1) * (l + 1))

            expert_passes(dve, first, group, passes, l, main_pass_read)
            if l + 1 < depth:
                atleast(dve, "ada_mod", (l + 2) * ADA_P)
        n = 2 * depth
        mean_square(n)
        dve.wait_ge(sem("rstd"), TILES * (n + 1))
        dve.wait_ge(sem("normf_ps"), 1)
        for t in range(TILES):
            for half in range(2):
                o = slice(half * 512, half * 512 + 512)
                last = V.scalar_tensor_tensor(ofin[:, t, o], x[:, t, o], rstd[:, t:t + 1], ps[4 + half][:], ALU.mult, ALU.mult)
            last.then_inc(sem("final_ready"), 1)

    @block.scalar
    def _(act_e):
        e = act_e
        step = Order(e, "act_step")

        def sum_squares(n):
            if n == 0:
                e.wait_ge(sem("x_landed"), 32)
            elif n % 2 == 0:
                e.wait_ge(sem("layer_done"), n // 2)
            if n:
                e.wait_ge(sem("msq"), TILES * n)
            for t in range(TILES):
                if n % 2:
                    e.wait_ge(sem("mix_added"), 6 * (n // 2) + TILES + t + 1)
                squares = xn[:, t, :] if n % 2 == 0 else \
                    (kT.rearrange("p g s -> p (g s)"), hp[:, 0:4].rearrange("p k s -> p (k s)"),
                     rqkv[:, 0:2].rearrange("p t n -> p (t n)"))[n // 2 % 3][:, 0:D]
                if n % 2 and t:
                    e.wait_ge(sem("ssq"), TILES * n + t)
                S.activation(squares, x[:, t, :], ACT.Square, accum_out=ssq[:, t:t + 1]).then_inc(sem("ssq"), 1)

        def norm(l, sub):
            n = 2 * l + sub
            sum_squares(n)
            e.wait_ge(sem("ssq"), TILES * (n + 1))
            for t in range(TILES):
                e.wait_ge(sem("rstd"), TILES * n + t + 1)
                S.activation(xn[:, t, :], x[:, t, :], ACT.Copy, scale=rstd[:, t:t + 1]).then_inc(sem("xn_ready"), 1)
            e.wait_ge(sem("mods_ready"), l + 1)
            for k in range(1, KD, 2):
                e.wait_ge(sem("hT_ps"), KD * n + k + 1)
                for c, src in enumerate((ps[k % 4][:, 0:128], ps[k % 4][:, 128:T])):
                    last = S.activation(hT_out(l, sub, k, c), src, ACT.Identity, bias=mod_col(3 * sub, k, c),
                                        scale=mod_col(1 + 3 * sub, k, c))
                last.then_inc(sem("hT_act"), 1)

        def gate(n):
            for c in range(2):
                for half in range(2):
                    e.wait_ge(sem("gate_ps"), 4 * n + 2 * c + half + 1)
                    S.activation(gate_bc[:, c, half * 512:half * 512 + 512], ps[4 + 2 * c + half][:], ACT.Copy)\
                        .then_inc(sem("gate_bc"), 1)

        def mod_copies(l):
            for i in range(8):
                e.wait_ge(sem("mod_ps"), 8 * l + i + 1)
                S.activation(mod_bc[:, i // 2, (i % 2) * 512:(i % 2) * 512 + 512], ps[4 + i % 4][:], ACT.Copy)\
                    .then_inc(sem("mod_bc"), 1)

        def ada_copy(idx, bank=4):
            e.wait_ge(sem("ada_product"), idx + 1)
            atleast(e, "ada_col", idx)
            S.activation(mpan[:], ps[bank][:, 0:ADA_N], ACT.Copy).then_inc(sem("ada_evac"), 1)

        def attention(l):
            a = l // 3
            e.dma_start(ckv[:, 0, :], A["cache_k"][0, a].rearrange("s h d -> s (h d)")).then_inc(sem("cache_landed"), 16)
            e.dma_start(ckv[:, 1, :], A["cache_v"][0, a].rearrange("s h d -> s (h d)")).then_inc(sem("cache_landed"), 16)
            e.dma_start(gqk[:, 0:HEADS * HD].rearrange("p (h d) -> p h d", h=HEADS),
                        A["attn_q_norm"][a:a + 1, :].unsqueeze(1).broadcast_to([128, HEADS, HD])).then_inc(sem("attn_landed"), 16)
            e.dma_start(gqk[:, HEADS * HD:].rearrange("p (h d) -> p h d", h=KV),
                        A["attn_k_norm"][a:a + 1, :].unsqueeze(1).broadcast_to([128, KV, HD])).then_inc(sem("attn_landed"), 16)
            e.dma_start(rope[:], A["k_rope"]).then_inc(sem("attn_landed"), 32)
            def panel_rows(i):
                for t in range(TILES):
                    e.wait_ge(sem("proj_done"), prj_base[l] + 3 * i + t + 1)
                    S.activation(qkv[:, t, i * 512:(i + 1) * 512], ps[(0, 4, 0)[i] + t][:], ACT.Copy).then_inc(sem("qkv_sb"), 1)

            for i in range(3):
                panel_rows(i)
            mod_copies(l)
            for h in range(NQK):
                b = ps[4 + h % 4] if h < HEADS else ps[h % 2]
                e.wait_ge(sem("qkT_ps"), NQK * a + h + 1)
                if h < HEADS:
                    S.activation(qT[:, h, :], b[:, 0:T], ACT.Copy).then_inc(sem("qkT_sb"), 1)
                else:
                    S.activation(kT[:, h - HEADS, 0:128], b[:, 0:128], ACT.Copy)
                    S.activation(kT[:, h - HEADS, 128:256], b[:, 384:512], ACT.Copy)
                    S.activation(kT[:, h - HEADS, 256:512], b[:, 128:384], ACT.Copy).then_inc(sem("qkT_sb"), 1)
            e.dma_start(O["new_cache_k"][0, a].rearrange("s h d -> s (h d)"), qkv[:, 0, HEADS * HD:NQK * HD])\
                .then_inc(sem("cache_stored"), 16)
            e.dma_start(O["new_cache_v"][0, a].rearrange("s h d -> s (h d)"), qkv[:, 0, NQK * HD:])\
                .then_inc(sem("cache_stored"), 16)

            def soft(h):
                n, b0 = HEADS * a + h, 2 * (h % 2)
                units = ((ps[b0][:, 0:128], 0, 128), (ps[b0][:, 128:512], 128, 512), (ps[b0 + 1][:, 0:384], 512, 896))
                e.wait_ge(sem("neg_max"), n + 1)
                if h >= 2:
                    e.wait_ge(sem("probT_ps"), 2 * (n - 1))
                for u, (src, lo, hi) in enumerate(units):
                    S.activation(prob[:, h % 2, lo:hi], src, ACT.Exp, bias=stat[:, 6 + 3 * (h % 2) + u:7 + 3 * (h % 2) + u],
                                 scale=float(HD) ** -0.5, accum_out=stat[:, 12 + 3 * (h % 2) + u:13 + 3 * (h % 2) + u])\
                        .then_inc(sem("prob"), 1)

            def probs_T(h):
                n = HEADS * a + h
                if h >= 2:
                    e.wait_ge(sem("oT_ps"), n - 1)
                e.wait_ge(sem("probT_ps"), 2 * n + 1)
                S.activation(probT[:, h % 2, 0:512], ps[4][:], ACT.Copy).then_inc(sem("probT_sb"), 1)
                e.wait_ge(sem("probT_ps"), 2 * n + 2)
                S.activation(probT[:, h % 2, 512:896], ps[5][:, 0:384], ACT.Copy).then_inc(sem("probT_sb"), 1)

            soft(0)
            soft(1)
            probs_T(0)
            for h in range(HEADS):
                if h + 2 < HEADS:
                    soft(h + 2)
                if in_heads(l):
                    ada_copy((l + 1) * ADA_P + 2 * h, 7)
                if h + 1 < HEADS:
                    probs_T(h + 1)
                if in_heads(l):
                    ada_copy((l + 1) * ADA_P + 2 * h + 1, 7)
                e.wait_ge(sem("oT_ps"), HEADS * a + h + 1)
                S.activation(oT[:, h, :], ps[6][:, 0:T], ACT.Copy).then_inc(sem("oT_sb"), 1)

        def retention(l):
            kr = A["k_ret"]
            mod_copies(l)
            e.dma_start(kret[:], kr).then_inc(sem("ret_const"), 16)
            e.dma_start(rsm[:, 0:16], A["ret_decay_logit"].rearrange("l a h -> l (a h)").broadcast_to([128, 16])).then_inc(sem("ret_const"), 16)
            e.dma_start(rnorm[:].rearrange("p h v -> p (h v)"), A["ret_norm"].broadcast_to([128, RH * RV])).then_inc(sem("ret_const"), 16)
            e.wait_ge(sem("decay_in"), 1)
            S.activation(rsm[:, 32:48], rsm[:, 16:32], ACT.Exp).then_inc(sem("decay_exp"), 1)
            e.wait_ge(sem("log_decay"), 1)
            lgc = lambda d, h: rsm[:, 96 + 8 * d + h:97 + 8 * d + h]
            for h in range(RH):
                if h >= 2:
                    e.wait_ge(sem("mask_done"), h - 1)
                S.activation(rMT[:, h, :], kret[:, 0:128], ACT.Exp, scale=lgc(0, h)).then_inc(sem("mask_exp"), 1)
                S.activation(rof[:, h % 2, 0:128], kret[:, 256:384], ACT.Exp, scale=lgc(1, h)).then_inc(sem("mask_exp"), 1)
                S.activation(rdf[:, h, :], kret[:, 512:640], ACT.Exp, scale=lgc(0, h))
                S.activation(rdb[:, h, :], kret[:, 640:768], ACT.Exp, scale=lgc(1, h))
            S.activation(rsm[:, 112:120], rsm[:, 96:104], ACT.Exp, scale=kret[:, 768:769])
            S.activation(rsm[:, 120:128], rsm[:, 104:112], ACT.Exp, scale=kret[:, 769:770])
            S.activation(rsm[:, 128:144], rsm[:, 96:112], ACT.Exp, scale=128.0).then_inc(sem("mask_exp"), 1)
            st_in, st_out = A["state_ret"], O["new_state_ret"]
            e.wait_ge(sem("mask_done"), RH)
            with e.Fori(0, RH) as h:
                atleast(e, "ret_O_ps", h)
                e.dma_start(rs0[:], st_in[0, 0, :, ds(h, 1)].rearrange("a o k v -> k (a o) v")).then_inc(sem("state_in"), 16)
                e.wait_ge(sem("ret_qkv"), h + 1)
                for t in (0, 2):
                    S.activation(rqkv[:, t, :], ps[t][:], ACT.Copy).then_inc(sem("ret_in_sb"), 1)
                e.wait_ge(sem("ret_gate"), h + 1)
                S.activation(rg[:, 0:2, :], ps[3][:].rearrange("p (t v) -> p t v", t=2), ACT.Silu)
                S.activation(rg[:, 2, :], ps[4][:, 0:256], ACT.Silu).then_inc(sem("ret_gate_sb"), 1)
                e.wait_ge(sem("ret_T_ps"), h + 1)
                S.activation(rkT[:], ps[6][:, 0:T], ACT.Copy).then_inc(sem("ret_T_sb"), 1)
                e.wait_ge(sem("ret_U_ps"), h + 1)
                atleast(e, "state_stored", 16 * h)
                S.activation(rso[:], ps[5][:].rearrange("p (a v) -> p a v", a=2), ACT.Copy).then_inc(sem("ret_state_out"), 1)
                e.wait_ge(sem("ret_state_out"), h + 1)
                e.dma_start(st_out[0, 0, :, ds(h, 1)].rearrange("a o k v -> k (a o) v"), rso[:]).then_inc(sem("state_stored"), 16)
                if in_retention(l):
                    for j in range(2):
                        ada_copy((l + 1) * ADA_P + 2 * h + j)
                for c in range(2):
                    e.wait_ge(sem("ret_yT_ps"), 2 * h + c + 1)
                    S.activation((yTe, yTo)[c][:, ds(h, 1), :].rearrange("p o t -> p (o t)"), ps[6 - c][:, 0:T], ACT.Copy)\
                        .then_inc(sem("ret_yT_sb"), 1)

        def route(l):
            n = 2 * l + 1
            e.wait_ge(sem("logit_parts_ps"), l + 1)
            S.activation(lpart[:], ps[2][:, 0:T], ACT.Copy).then_inc(sem("logit_parts"), 1)
            for t in range(TILES):
                e.wait_ge(sem("h_tok"), TILES * l + t + 1)
                S.activation(hhi[:, t, :], htok[:, t, :], ACT.Copy).then_inc(sem("h_hi"), 1)
            gate(n)
            e.wait_ge(sem("route_exp_in"), l + 1)
            S.activation(rt[:, 385:400], rt[:, 370:385], ACT.Exp).then_inc(sem("route_exp"), 1)

        def gathered_rows(z, r):
            e.wait_ge(sem(z + "_gather"), r + 1)
            atleast(e, z + "_hT", r)
            S.activation(hgt[:, 0:512], ps[0][:], ACT.Copy).then_inc(sem(z + "_hgt_act"), 1)

        def gathered_cols(z, r, q, j):
            atleast(e, z + "_hT", r + 1)
            atleast(e, z + "_gateup", q - 1)
            S.activation(hg[:, j % 2, 0:4, :], ps[0][:].rearrange("p (k s) -> p k s", k=4), ACT.Copy)\
                .then_inc(sem(z + "_hg_act"), 1)

        def slots(z, r, q, j, scatters):
            atleast(e, z + "_PT", r + 1)
            if scatters is not None:
                atleast(e, z + "_scatter", scatters)
            S.activation(PT[:, j % PER_OF[z], :], ps[5][:, 0:T], ACT.Copy)
            atleast(e, z + "_act", q - 1)
            S.activation(gslot[:, j % 2].rearrange("p s c -> p (s c)"), ps[5][:, T:T + 4], ACT.Copy).then_inc(sem(z + "_PT_sb"), 1)

        def first(z, P, u0):
            r = P * (PAIRS_OF[z] + 1)
            gathered_rows(z, r)
            gathered_cols(z, r, P * PAIRS_OF[z], 0)
            slots(z, r, P * PAIRS_OF[z], 0, 6 * GROUPS_OF[z] * P)

        def experts(z, P, g, u0, ada):
            per = PER_OF[z]
            it = P * GROUPS_OF[z] + g
            for j in range(per):
                x_ = g * per + j
                q, r = P * PAIRS_OF[z] + x_, P * (PAIRS_OF[z] + 1) + x_
                atleast(e, z + "_gateup", q + 1)
                atleast(e, z + "_act", q)
                S.activation(silu[:], ps[2][:, 0:FE], ACT.Silu).then_inc(sem(z + "_silu"), 1)
                gathered_rows(z, r + 1)
                atleast(e, z + "_actT", q + 1)
                atleast(e, z + "_down", 2 * q)
                S.activation(actT[:], ps[3][:, 0:256].rearrange("p (c s) -> p c s", c=2), ACT.Copy)\
                    .then_inc(sem(z + "_actT_sb"), 1)
                if ada is not None:
                    ada_copy(ada + 2 * x_)
                for half in range(2):
                    atleast(e, z + "_down", 2 * q + half + 1)
                    S.activation(yhi[:, j, half * 512:half * 512 + 512], ps[6 + half][:], ACT.Copy)\
                        .then_inc(sem(z + "_y_hi"), 1)
                gathered_cols(z, r + 1, q + 1, j + 1)
                if ada is not None:
                    ada_copy(ada + 2 * x_ + 1)
                slots(z, r + 1, q + 1, j + 1, 6 * it + 6 if j == per - 1 else None)

        for l in range(DEPTH):
            e.dma_start(wr[:, l, :, 0:4], A["moe_w_router_g"][l].rearrange("(k p) g -> p k g", p=128)).then_inc(sem("router_landed"), 16)
            e.dma_start(wr[:, l, :, 4:20], A["moe_w_router_e"][l].rearrange("(k p) g -> p k g", p=128)).then_inc(sem("router_landed"), 16)
            e.dma_start(rb[:, l, 0:4], A["moe_b_router_g"][l:l + 1, :].broadcast_to([128, 4])).then_inc(sem("router_landed"), 16)
            e.dma_start(rb[:, l, 4:20], A["moe_b_router_e"][l:l + 1, :].broadcast_to([128, 16])).then_inc(sem("router_landed"), 16)
        e.wait_ge(sem("vT_sb"), 1)
        S.activation(cond32[:, :, 0], vT[:, 80:88], ACT.Silu)
        S.activation(cond32[:, :, 1], vT[:, 88:96], ACT.Silu).then_inc(sem("cond_ready"), 1)
        with e.Fori(0, ADA_P) as i:
            ada_copy(i)
        passes = []
        for l in range(depth):
            norm(l, 0)
            gate(2 * l)
            if l % 3 == 0:
                attention(l)
            elif l % 3 == 1:
                e.dma_start(icnt[:], A["k_cnt"].rearrange("(o g) w -> o g w", o=1).broadcast_to([128, 4, PW])).then_inc(sem("count_landed"), 16)
                mod_copies(l)
            else:
                retention(l)
            norm(l, 1)
            route(l)
            S.preload_act_table(ACT.Silu)
            e.wait_ge(sem("routed"), l + 1)
            nxt = (l + 1) * ADA_P if l + 1 < depth and not early(l) else None
            expert_passes(e, first, lambda z, P, g, u0: experts(z, P, g, u0, nxt if z == "m" else None), passes, l)
        sum_squares(2 * depth)

    @block.gpsimd
    def _(pool):
        for name, c in CREDIT.items():
            pool.sem_inc(sem(name), c)

        def inverse_root(n):
            for t in range(TILES):
                pool.wait_ge(sem("msq"), TILES * n + t + 1)
                G.tensor_tensor(rstd[:, t:t + 1], msq[:, t:t + 1], hpow[:, 0:1], ALU.pow).then_inc(sem("rstd"), 1)

        def experts(z, it):
            for m in range(2 * TILES):
                t, half = m // 2, m % 2
                o = slice(half * 512, half * 512 + 512)
                atleast(pool, z + "_term", 6 * it + m + 1)
                G.tensor_tensor(x[:, t, o], x[:, t, o], tmp[:, m % 2, :], ALU.add).then_inc(sem(z + "_added"), 1)

        passes = []
        G.memset(wr[:, :, :, 20:32], 0.0)
        G.memset(gates_r[:, :, EXPERTS:EXPERTS + 2, :].bitcast(F), 0.0)
        G.memset(rankm[:, :, EXPERTS:EXPERTS + 2], -1.0).then_inc(sem("router_pad"), 1)
        pool.wait_ge(sem("const_landed"), 16)
        for l in range(depth):
            a = l // 3
            inverse_root(2 * l)
            if l % 3 == 0:
                for i, (h0, h1) in enumerate(((0, 4), (4, 8), (8, NQK))):
                    pool.wait_ge(sem("qk_ms"), 3 * a + i + 1)
                    G.tensor_tensor(stat[:, 64 + 3 * h0:64 + 3 * h1], stat[:, 32 + 3 * h0:32 + 3 * h1],
                                    hpow[:, 0:3 * (h1 - h0)], ALU.pow).then_inc(sem("qk_rstd"), 1)
            elif l % 3 == 1:
                for lo, hi in ((0, POFF[0]), (POFF[0] + SEQ, POFF[1]), (POFF[1] + DEC, PW)):
                    last = G.memset(hp[:, :, lo:hi], 0.0)
                last.then_inc(sem("pool_pads"), 1)
            else:
                with pool.Fori(0, RH) as h:
                    pool.wait_ge(sem("ret_var"), h + 1)
                    G.tensor_tensor(rsm[:, 176:179], rsm[:, 172:175], hpow[:, 0:3], ALU.pow).then_inc(sem("ret_rstd"), 1)
            for m in range(2 * TILES):
                half, t = m // TILES, m % TILES
                o = slice(half * 512, half * 512 + 512)
                pool.wait_ge(sem("mix_term"), 6 * l + m + 1)
                G.tensor_tensor(x[:, t, o], x[:, t, o], tmp[:, m % 2, :], ALU.add).then_inc(sem("mix_added"), 1)
            inverse_root(2 * l + 1)
            for t in range(2):
                pool.wait_ge(sem("h_hi"), TILES * l + t + 1)
                G.tensor_tensor(hlo[:, t, :], htok[:, t, :], hhi[:, t, :].bitcast(F), ALU.subtract).then_inc(sem("h_lo"), 1)
            pool.wait_ge(sem("routed"), l + 1)
            expert_passes(pool, lambda z, P, u0: None, lambda z, P, g, u0: experts(z, P * GROUPS_OF[z] + g), passes, l)
            pool.drain().then_inc(sem("layer_done"), 1)
        inverse_root(2 * depth)

    ctx.close()


_INS = ["x_prompt", "x_sample", "cache_k", "cache_v", "state_ret", "w_ada", "b_ada", "attn_w_qkv", "attn_q_norm",
        "attn_k_norm", "attn_w_o", "pool_w", "ret_w_in", "ret_decay_logit", "ret_norm", "ret_w_out",
        "moe_w_router_g", "moe_b_router_g", "moe_w_router_e", "moe_b_router_e", "moe_w_gate", "moe_w_up", "moe_w_down"]
_OUTS = {"y_prompt": (1, SEQ, D), "y_sample": (1, DEC, D), "new_cache_k": (1, 2, SEQ, KV, HD),
         "new_cache_v": (1, 2, SEQ, KV, HD), "new_state_ret": (1, 1, 2, RH, RK, RV)}


def kernel(**inputs):
    import concourse.bacc as bacc
    from concourse import mybir
    from concourse.bass_utils import run_bass_kernel_spmd as run

    nc = bacc.Bacc("TRN2", target_bir_lowering=False, num_devices=1)
    arrays = {n: np.ascontiguousarray(inputs[n]) for n in _INS}
    arrays["vectors"] = np.concatenate([np.asarray(inputs[n]).reshape(-1, 128) for n in
                                        ("norm1", "norm2", "pool_scale", "norm_f", "c_ctx", "c")])
    arrays.update(shape_constants())
    feeds, A, O = {}, {}, {}
    for n, a in arrays.items():
        feeds["in_" + n] = a
        A[n] = nc.dram_tensor("in_" + n, a.shape, mybir.dt.from_np(a.dtype), kind="ExternalInput").ap()
    for n, shape in _OUTS.items():
        O[n] = nc.dram_tensor("out_" + n, shape, mybir.dt.float32, kind="ExternalOutput").ap()
    build_trunk(nc, A, O)
    r = run(nc, [feeds], core_ids=[0])
    return tuple(r.results[0]["out_" + n] for n in _OUTS)
```
